# Optimizing a Trainium2 kernel written in Bass

```python
import math
import jax, jax.numpy as jnp
from jax import lax
import numpy as np

D_MODEL = 1024
BATCH = 1
SEQ = 256
DEPTH = 2

GRID_W = 64
CTX_LEN = 256
EPS = 1e-6
CONV_CH = 512
CONV_WIDTH = 31
N_HEADS = 8
HEAD_DIM = 64
V_DIM = 2 * HEAD_DIM
QK_W = N_HEADS * 2 * HEAD_DIM
ATTN_W = N_HEADS * V_DIM
Q_BLOCK = 128
ROPE_BASE = 10000.0
POOL_CH = 512
POOL_WINDOWS = (2, 4, 8, 16)
POOL_GROUP = POOL_CH // len(POOL_WINDOWS)
N_BRANCH = 3
D_FF = -(-(8 * D_MODEL) // (3 * 256)) * 256
N_MOD = 6
COL_A = 0
COL_Q = COL_A + 2 * CONV_CH
COL_K = COL_Q + QK_W
COL_V = COL_K + QK_W
COL_P = COL_V + ATTN_W
COL_G = COL_P + POOL_CH
IN_W = COL_G + N_BRANCH * D_MODEL


def rms_norm(x, g):
    x32 = x.astype(jnp.float32)
    y = x32 * lax.rsqrt(jnp.mean(x32 * x32, axis=-1, keepdims=True) + EPS)
    return (y * g.astype(jnp.float32)).astype(x.dtype)

def layer_norm(x, g, b):
    x32 = x.astype(jnp.float32)
    mu = jnp.mean(x32, axis=-1, keepdims=True)
    var = jnp.mean(jnp.square(x32 - mu), axis=-1, keepdims=True)
    y = (x32 - mu) * lax.rsqrt(var + EPS) * g.astype(jnp.float32) + b.astype(jnp.float32)
    return y.astype(x.dtype)

def axial_rope_tables(n_tokens):
    rows = n_tokens // GRID_W
    row = jnp.repeat(jnp.arange(rows), GRID_W).astype(jnp.float32)
    col = jnp.tile(jnp.arange(GRID_W), rows).astype(jnp.float32)
    half = HEAD_DIM // 2
    inv = ROPE_BASE ** (-jnp.arange(0, half, 2, dtype=jnp.float32) / half)
    ang_r = row[:, None] * inv[None, :]
    ang_c = col[:, None] * inv[None, :]
    return (jnp.cos(ang_r), jnp.sin(ang_r), jnp.cos(ang_c), jnp.sin(ang_c))

def _rotate(x, cos, sin):
    n = x.shape[-1] // 2
    x1, x2 = x[..., :n], x[..., n:]
    cos = cos.astype(x.dtype)
    sin = sin.astype(x.dtype)
    return jnp.concatenate([x1 * cos - x2 * sin, x2 * cos + x1 * sin], axis=-1)

def apply_axial_rope(x, rope):
    cos_r, sin_r, cos_c, sin_c = rope
    half = HEAD_DIM // 2
    return jnp.concatenate([_rotate(x[..., :half], cos_r, sin_r),
                            _rotate(x[..., half:], cos_c, sin_c)], axis=-1)

def depthwise_conv(u, w, b):
    k, ch = w.shape
    out = lax.conv_general_dilated(u, w[:, None, :].astype(u.dtype), window_strides=(1,),
                                   padding=[(k // 2, k // 2)],
                                   dimension_numbers=('NWC', 'WIO', 'NWC'),
                                   feature_group_count=ch)
    return out + b.astype(u.dtype)

def conformer_conv(h, w_glu, conv_w, conv_b, ln_g, ln_b, w_proj):
    u = h @ w_glu
    u = u[..., :CONV_CH] * jax.nn.sigmoid(u[..., CONV_CH:])
    u = depthwise_conv(u, conv_w, conv_b)
    u = layer_norm(u, ln_g, ln_b)
    return jax.nn.silu(u) @ w_proj

def multiscale_pool(h, w_p, w_group, scale, w_proj):
    p = h @ w_p
    b_, l_ = p.shape[0], p.shape[1]
    cs = jnp.cumsum(p.astype(jnp.float32), axis=1)
    cs = jnp.pad(cs, ((0, 0), (1, 0), (0, 0)))
    t = jnp.arange(l_)
    outs = []
    for gi, w in enumerate(POOL_WINDOWS):
        lo = jnp.clip(t - w // 2, 0, l_)
        hi = jnp.clip(t + w // 2, 0, l_)
        csg = cs[..., gi * POOL_GROUP:(gi + 1) * POOL_GROUP]
        s = jnp.take(csg, hi, axis=1) - jnp.take(csg, lo, axis=1)
        outs.append(s / (hi - lo).astype(jnp.float32)[None, :, None])
    pooled = jnp.concatenate(outs, axis=-1).astype(p.dtype) - p
    pooled = pooled.reshape(b_, l_, len(POOL_WINDOWS), POOL_GROUP)
    mixed = jnp.einsum('blgc,gcd->blgd', pooled, w_group).reshape(b_, l_, POOL_CH)
    return (mixed * scale) @ w_proj

def diff_qkv(h, w_q, w_k, w_v):
    b_, l_ = h.shape[0], h.shape[1]
    q = (h @ w_q).reshape(b_, l_, N_HEADS, 2, HEAD_DIM).transpose(0, 2, 3, 1, 4)
    k = (h @ w_k).reshape(b_, l_, N_HEADS, 2, HEAD_DIM).transpose(0, 2, 3, 1, 4)
    v = (h @ w_v).reshape(b_, l_, N_HEADS, V_DIM).transpose(0, 2, 1, 3)
    return q, k, v

def diff_attend(q, k, v, lam):
    s = jnp.einsum('bhiqd,bhikd->bhiqk', q, k).astype(jnp.float32) * (HEAD_DIM ** -0.5)
    p = jax.nn.softmax(s, axis=-1)
    a = (p[:, :, 0] - lam * p[:, :, 1]).astype(v.dtype)
    return jnp.einsum('bhqk,bhkd->bhqd', a, v)

def diff_finish(o, subln_g, lam_init, w_proj):
    o = rms_norm(o, subln_g) * (1.0 - lam_init)
    b_, h_, l_, _ = o.shape
    return o.transpose(0, 2, 1, 3).reshape(b_, l_, ATTN_W) @ w_proj

def gated_merge(h, y_a, y_b, y_c, w_g, b_gate, w_out):
    g = jax.nn.sigmoid(h @ w_g + b_gate)
    m = (g[..., :D_MODEL] * y_a + g[..., D_MODEL:2 * D_MODEL] * y_b
         + g[..., 2 * D_MODEL:] * y_c)
    return m @ w_out

def token_mixer(h, hc, rope, need_ctx, lam_init, w_in, b_gate, conv_w, conv_b, ln_g, ln_b,
                w_conv_out, lam_q1, lam_k1, lam_q2, lam_k2, subln_g, w_attn_out,
                w_pool_group, pool_scale, w_pool_out, w_out):
    w_glu = w_in[:, COL_A:COL_Q]
    w_q = w_in[:, COL_Q:COL_K]
    w_k = w_in[:, COL_K:COL_V]
    w_v = w_in[:, COL_V:COL_P]
    w_p = w_in[:, COL_P:COL_G]
    w_g = w_in[:, COL_G:IN_W]
    lam = (jnp.exp(jnp.sum(lam_q1.astype(jnp.float32) * lam_k1.astype(jnp.float32)))
           - jnp.exp(jnp.sum(lam_q2.astype(jnp.float32) * lam_k2.astype(jnp.float32)))
           + lam_init)

    qc, kc, vc = diff_qkv(hc, w_q, w_k, w_v)
    q, k, v = diff_qkv(h, w_q, w_k, w_v)
    q = apply_axial_rope(q, rope)
    k = apply_axial_rope(k, rope)
    k_all = jnp.concatenate([kc, k], axis=3)
    v_all = jnp.concatenate([vc, v], axis=2)
    b_, h_, _, l_, _ = q.shape
    nb = l_ // Q_BLOCK
    qb = jnp.moveaxis(q.reshape(b_, h_, 2, nb, Q_BLOCK, HEAD_DIM), 3, 0)
    ob = lax.map(lambda qq: diff_attend(qq, k_all, v_all, lam), qb)
    o = jnp.moveaxis(ob, 0, 2).reshape(b_, h_, l_, V_DIM)

    y_a = conformer_conv(h, w_glu, conv_w, conv_b, ln_g, ln_b, w_conv_out)
    y_b = diff_finish(o, subln_g, lam_init, w_attn_out)
    y_c = multiscale_pool(h, w_p, w_pool_group, pool_scale, w_pool_out)
    y = gated_merge(h, y_a, y_b, y_c, w_g, b_gate, w_out)
    if not need_ctx:
        return y, None
    oc = diff_attend(qc, kc, vc, lam)
    yc_a = conformer_conv(hc, w_glu, conv_w, conv_b, ln_g, ln_b, w_conv_out)
    yc_b = diff_finish(oc, subln_g, lam_init, w_attn_out)
    yc_c = multiscale_pool(hc, w_p, w_pool_group, pool_scale, w_pool_out)
    yc = gated_merge(hc, yc_a, yc_b, yc_c, w_g, b_gate, w_out)
    return y, yc

def swiglu(h, w_ffn_in, w_ffn_out):
    u = h @ w_ffn_in
    return (jax.nn.silu(u[..., :D_FF]) * u[..., D_FF:]) @ w_ffn_out

def first_inputs(seed: int = 0) -> dict:
    key = jax.random.key(seed)
    ks = jax.random.split(key, 32)
    f32 = jnp.float32
    nrm = lambda k, shape, s: jax.random.normal(k, shape, f32) * s
    gain = lambda k, shape: 1.0 + 0.02 * jax.random.normal(k, shape, f32)
    L = DEPTH
    return {
        "x": nrm(ks[0], (BATCH, SEQ, D_MODEL), 1.0),
        "c": nrm(ks[1], (BATCH, D_MODEL), 1.0),
        "ctx": nrm(ks[2], (BATCH, CTX_LEN, D_MODEL), 1.0),
        "c_ctx": nrm(ks[3], (D_MODEL,), 1.0),
        "w_mod": nrm(ks[4], (L, D_MODEL, N_MOD * D_MODEL), 0.5 * D_MODEL ** -0.5),
        "b_mod": nrm(ks[5], (L, N_MOD * D_MODEL), 0.02),
        "g_pre_mix": gain(ks[6], (L, D_MODEL)),
        "g_post_mix": gain(ks[7], (L, D_MODEL)),
        "w_in": nrm(ks[8], (L, D_MODEL, IN_W), D_MODEL ** -0.5),
        "b_gate": nrm(ks[9], (L, N_BRANCH * D_MODEL), 0.02),
        "conv_w": nrm(ks[10], (L, CONV_WIDTH, CONV_CH), CONV_WIDTH ** -0.5),
        "conv_b": nrm(ks[11], (L, CONV_CH), 0.02),
        "conv_ln_g": gain(ks[12], (L, CONV_CH)),
        "conv_ln_b": nrm(ks[13], (L, CONV_CH), 0.02),
        "w_conv_out": nrm(ks[14], (L, CONV_CH, D_MODEL), CONV_CH ** -0.5),
        "lam_q1": nrm(ks[15], (L, HEAD_DIM), 0.1),
        "lam_k1": nrm(ks[16], (L, HEAD_DIM), 0.1),
        "lam_q2": nrm(ks[17], (L, HEAD_DIM), 0.1),
        "lam_k2": nrm(ks[18], (L, HEAD_DIM), 0.1),
        "subln_g": gain(ks[19], (L, V_DIM)),
        "w_attn_out": nrm(ks[20], (L, ATTN_W, D_MODEL), ATTN_W ** -0.5),
        "w_pool_group": nrm(ks[21], (L, len(POOL_WINDOWS), POOL_GROUP, POOL_GROUP), POOL_GROUP ** -0.5),
        "pool_scale": 1.0 + 0.1 * jax.random.normal(ks[22], (L, POOL_CH), f32),
        "w_pool_out": nrm(ks[23], (L, POOL_CH, D_MODEL), POOL_CH ** -0.5),
        "w_out": nrm(ks[24], (L, D_MODEL, D_MODEL), D_MODEL ** -0.5),
        "g_pre_ffn": gain(ks[25], (L, D_MODEL)),
        "g_post_ffn": gain(ks[26], (L, D_MODEL)),
        "w_ffn_in": nrm(ks[27], (L, D_MODEL, 2 * D_FF), D_MODEL ** -0.5),
        "w_ffn_out": nrm(ks[28], (L, D_FF, D_MODEL), D_FF ** -0.5),
    }

def first_block(x, c, ctx, c_ctx, w_mod, b_mod, g_pre_mix, g_post_mix, w_in, b_gate, conv_w,
              conv_b, conv_ln_g, conv_ln_b, w_conv_out, lam_q1, lam_k1, lam_q2, lam_k2,
              subln_g, w_attn_out, w_pool_group, pool_scale, w_pool_out, w_out, g_pre_ffn,
              g_post_ffn, w_ffn_in, w_ffn_out):
    rope = axial_rope_tables(x.shape[1])
    xl, xc = x, ctx
    for l in range(DEPTH):
        need_ctx = l < DEPTH - 1
        lam_init = 0.8 - 0.6 * math.exp(-0.3 * l)
        mod = jax.nn.silu(c) @ w_mod[l] + b_mod[l]
        modc = jax.nn.silu(c_ctx) @ w_mod[l] + b_mod[l]
        sh1, sc1, gt1, sh2, sc2, gt2 = jnp.split(mod[:, None, :], N_MOD, axis=-1)
        csh1, csc1, cgt1, csh2, csc2, cgt2 = jnp.split(modc, N_MOD, axis=-1)

        h = rms_norm(xl, g_pre_mix[l]) * (1.0 + sc1) + sh1
        hc = rms_norm(xc, g_pre_mix[l]) * (1.0 + csc1) + csh1
        y, yc = token_mixer(h, hc, rope, need_ctx, lam_init, w_in[l], b_gate[l], conv_w[l],
                            conv_b[l], conv_ln_g[l], conv_ln_b[l], w_conv_out[l], lam_q1[l],
                            lam_k1[l], lam_q2[l], lam_k2[l], subln_g[l], w_attn_out[l],
                            w_pool_group[l], pool_scale[l], w_pool_out[l], w_out[l])
        xl = xl + gt1 * rms_norm(y, g_post_mix[l])

        h = rms_norm(xl, g_pre_ffn[l]) * (1.0 + sc2) + sh2
        xl = xl + gt2 * rms_norm(swiglu(h, w_ffn_in[l], w_ffn_out[l]), g_post_ffn[l])

        if need_ctx:
            xc = xc + cgt1 * rms_norm(yc, g_post_mix[l])
            hc = rms_norm(xc, g_pre_ffn[l]) * (1.0 + csc2) + csh2
            xc = xc + cgt2 * rms_norm(swiglu(hc, w_ffn_in[l], w_ffn_out[l]), g_post_ffn[l])
    return xl


N_HEADS_A = 12
N_KV_A = 4
IDX_HEADS = 8
IDX_DIM = 64
IDX_ROPE_DIM = 32
TOPK_MAX = 256
DIL_PATTERNS = ((128, 1), (512, 4), (2048, 16))
HEADS_PER_DIL = 4
N_MEM_HEADS = 4
MEM_TOKENS = 256
D_FF_2 = ((8 * D_MODEL // 3 + 255) // 256) * 256
BLK = 128
ROPE_THETA = 10000.0
NEG = -1e30

A_SIZES = (N_HEADS_A * HEAD_DIM, N_KV_A * HEAD_DIM, N_KV_A * HEAD_DIM,
           IDX_HEADS * IDX_DIM, IDX_DIM, IDX_HEADS, N_MEM_HEADS * HEAD_DIM)
A_IN = sum(A_SIZES)
A_OUT = (N_HEADS_A + N_MEM_HEADS) * HEAD_DIM
B_SIZES = (HEADS_PER_DIL * HEAD_DIM,) * (3 * len(DIL_PATTERNS)) + (N_MEM_HEADS * HEAD_DIM,)
B_IN = sum(B_SIZES)
B_OUT = (HEADS_PER_DIL + N_MEM_HEADS) * HEAD_DIM


def _split(t, sizes):
    offs = np.cumsum(sizes)[:-1].tolist()
    return jnp.split(t, offs, axis=-1)

def rms_norm_2(x, g):
    xf = x.astype(jnp.float32)
    y = xf * lax.rsqrt(jnp.mean(xf * xf, axis=-1, keepdims=True) + EPS)
    return (y * g.astype(jnp.float32)).astype(x.dtype)

def rope(x, pos, rot_dim):
    half = rot_dim // 2
    freqs = ROPE_THETA ** (-jnp.arange(half, dtype=jnp.float32) / half)
    ang = pos.astype(jnp.float32)[:, :, None, None] * freqs
    cos, sin = jnp.cos(ang), jnp.sin(ang)
    xr = x[..., :rot_dim].astype(jnp.float32)
    x1, x2 = xr[..., :half], xr[..., half:]
    rot = jnp.concatenate([x1 * cos - x2 * sin, x2 * cos + x1 * sin], axis=-1).astype(x.dtype)
    return jnp.concatenate([rot, x[..., rot_dim:]], axis=-1)

def dsa_mixer(proj, pos):
    bsz, seq, _ = proj.shape
    q, k, v, qi, ki, wi, qm = _split(proj, A_SIZES)
    q = rope(q.reshape(bsz, seq, N_HEADS_A, HEAD_DIM), pos, HEAD_DIM)
    k = rope(k.reshape(bsz, seq, N_KV_A, HEAD_DIM), pos, HEAD_DIM)
    v = v.reshape(bsz, seq, N_KV_A, HEAD_DIM)
    qi = rope(qi.reshape(bsz, seq, IDX_HEADS, IDX_DIM), pos, IDX_ROPE_DIM)
    ki = rope(ki.reshape(bsz, seq, 1, IDX_DIM), pos, IDX_ROPE_DIM)[:, :, 0]
    wi = wi.astype(jnp.float32) * (IDX_HEADS ** -0.5 * IDX_DIM ** -0.5)
    n_sel = min(TOPK_MAX, seq // 4)
    grp = N_HEADS_A // N_KV_A
    scale = HEAD_DIM ** -0.5
    key_pos = jnp.arange(seq)
    b_idx = jnp.arange(bsz)[:, None, None]

    def block(i):
        start = i * BLK
        qb = lax.dynamic_slice_in_dim(q, start, BLK, axis=1)
        qib = lax.dynamic_slice_in_dim(qi, start, BLK, axis=1)
        wib = lax.dynamic_slice_in_dim(wi, start, BLK, axis=1)
        t_pos = start + jnp.arange(BLK)
        logits = jnp.einsum('bqhd,bsd->bqhs', qib, ki, preferred_element_type=jnp.float32)
        score = jnp.einsum('bqhs,bqh->bqs', jax.nn.relu(logits), wib)
        score = jnp.where(key_pos[None, None, :] <= t_pos[None, :, None], score, NEG)
        _, idx = lax.top_k(score, n_sel)
        k_sel = k[b_idx, idx]
        v_sel = v[b_idx, idx]
        qg = qb.reshape(bsz, BLK, N_KV_A, grp, HEAD_DIM)
        s = jnp.einsum('bqkgd,bqskd->bqkgs', qg, k_sel, preferred_element_type=jnp.float32) * scale
        valid = (idx <= t_pos[None, :, None])[:, :, None, None, :]
        p = jax.nn.softmax(jnp.where(valid, s, NEG), axis=-1)
        o = jnp.einsum('bqkgs,bqskd->bqkgd', p, v_sel.astype(jnp.float32))
        return o.reshape(bsz, BLK, N_HEADS_A * HEAD_DIM).astype(proj.dtype)

    out = lax.map(block, jnp.arange(seq // BLK))
    out = out.transpose(1, 0, 2, 3).reshape(bsz, seq, N_HEADS_A * HEAD_DIM)
    return out, qm

def dilated_group(q, k, v, window, dil):
    bsz, seq, nh, hd = q.shape
    steps = window // dil
    n = seq // dil
    nb = -(-n // BLK)
    n_pad = nb * BLK

    def to_sub(t, front):
        t = t.reshape(bsz, n, dil, nh, hd).transpose(0, 2, 3, 1, 4)
        return jnp.pad(t, ((0, 0), (0, 0), (0, 0), (front, n_pad - n), (0, 0)))

    qs = to_sub(q, 0).reshape(bsz, dil, nh, nb, BLK, hd)
    kb = to_sub(k, BLK).reshape(bsz, dil, nh, nb + 1, BLK, hd)
    vb = to_sub(v, BLK).reshape(bsz, dil, nh, nb + 1, BLK, hd)
    kw = jnp.concatenate([kb[:, :, :, :-1], kb[:, :, :, 1:]], axis=4)
    vw = jnp.concatenate([vb[:, :, :, :-1], vb[:, :, :, 1:]], axis=4)
    s = jnp.einsum('brhnqd,brhnkd->brhnqk', qs, kw, preferred_element_type=jnp.float32) * (hd ** -0.5)
    qi = jnp.arange(BLK)[None, :, None]
    kj = jnp.arange(2 * BLK)[None, None, :]
    blk = jnp.arange(nb)[:, None, None]
    dist = qi + BLK - kj
    valid = (dist >= 0) & (dist <= steps) & (blk * BLK + kj - BLK >= 0)
    s = jnp.where(valid, s, NEG)
    m = jnp.max(s, axis=-1, keepdims=True)
    p = jnp.exp(s - m)
    den = jnp.sum(p, axis=-1, keepdims=True)
    o = jnp.einsum('brhnqk,brhnkd->brhnqd', p, vw.astype(jnp.float32)) / den
    lse = m[..., 0] + jnp.log(den[..., 0])
    o = o.reshape(bsz, dil, nh, n_pad, hd)[:, :, :, :n].transpose(0, 3, 1, 2, 4).reshape(bsz, seq, nh, hd)
    lse = lse.reshape(bsz, dil, nh, n_pad)[..., :n].transpose(0, 3, 1, 2).reshape(bsz, seq, nh)
    return o, lse

def dilated_mixer(proj, pos):
    bsz, seq, _ = proj.shape
    parts = _split(proj, B_SIZES)
    outs, lses = [], []
    for g, (window, dil) in enumerate(DIL_PATTERNS):
        q, k, v = [parts[3 * g + j].reshape(bsz, seq, HEADS_PER_DIL, HEAD_DIM) for j in range(3)]
        o, lse = dilated_group(rope(q, pos, HEAD_DIM), rope(k, pos, HEAD_DIM), v, window, dil)
        outs.append(o)
        lses.append(lse)
    wts = jax.nn.softmax(jnp.stack(lses, axis=-1), axis=-1)
    o = jnp.sum(jnp.stack(outs, axis=-2) * wts[..., None], axis=-2)
    return o.reshape(bsz, seq, HEADS_PER_DIL * HEAD_DIM).astype(proj.dtype), parts[-1]

def memory_attention(qm, mem, g_mem, w_mem_kv):
    bsz, seq, _ = qm.shape
    kv = (rms_norm_2(mem, g_mem) @ w_mem_kv).reshape(bsz, mem.shape[1], 2, N_MEM_HEADS, HEAD_DIM)
    q = qm.reshape(bsz, seq, N_MEM_HEADS, HEAD_DIM)
    s = jnp.einsum('bshd,bmhd->bhsm', q, kv[:, :, 0], preferred_element_type=jnp.float32) * (HEAD_DIM ** -0.5)
    p = jax.nn.softmax(s, axis=-1)
    o = jnp.einsum('bhsm,bmhd->bshd', p, kv[:, :, 1].astype(jnp.float32))
    return o.reshape(bsz, seq, N_MEM_HEADS * HEAD_DIM).astype(qm.dtype)

def swiglu_ffn(h, w_gate_up, w_down):
    g, u = jnp.split(h @ w_gate_up, 2, axis=-1)
    return (jax.nn.silu(g) * u) @ w_down

def hybrid_layer(x, mem, pos, layer_idx, norm_mix, norm_mem, w_in, w_mem_kv, w_out,
                 norm_ffn, w_gate_up, w_down):
    proj = rms_norm_2(x, norm_mix) @ w_in
    if layer_idx % 2 == 0:
        mix, qm = dsa_mixer(proj, pos)
    else:
        mix, qm = dilated_mixer(proj, pos)
    mo = memory_attention(qm, mem, norm_mem, w_mem_kv)
    x = x + jnp.concatenate([mix, mo], axis=-1) @ w_out
    x = x + swiglu_ffn(rms_norm_2(x, norm_ffn), w_gate_up, w_down)
    return x

def second_inputs(seed: int = 0) -> dict:
    key = jax.random.key(seed)
    ks = jax.random.split(key, 24)
    f32 = jnp.float32

    def dense(k, fi, fo):
        return jax.random.normal(k, (fi, fo), f32) * fi ** -0.5

    def gain(k):
        return 1.0 + 0.02 * jax.random.normal(k, (D_MODEL,), f32)

    x = jax.random.normal(ks[0], (BATCH, SEQ, D_MODEL), f32)
    mem = jax.random.normal(ks[1], (BATCH, MEM_TOKENS, D_MODEL), f32)
    offs = jax.random.randint(ks[2], (BATCH, 1), 0, 1024, dtype=jnp.int32)
    positions = (jnp.arange(SEQ, dtype=jnp.int32)[None, :] + offs).astype(jnp.int32)
    return {
        'x': x, 'mem': mem, 'positions': positions,
        'l0_norm_mix': gain(ks[3]), 'l0_norm_mem': gain(ks[4]),
        'l0_w_in': dense(ks[5], D_MODEL, A_IN),
        'l0_w_mem_kv': dense(ks[6], D_MODEL, 2 * N_MEM_HEADS * HEAD_DIM),
        'l0_w_out': dense(ks[7], A_OUT, D_MODEL),
        'l0_norm_ffn': gain(ks[8]),
        'l0_w_gate_up': dense(ks[9], D_MODEL, 2 * D_FF_2),
        'l0_w_down': dense(ks[10], D_FF_2, D_MODEL),
        'l1_norm_mix': gain(ks[11]), 'l1_norm_mem': gain(ks[12]),
        'l1_w_in': dense(ks[13], D_MODEL, B_IN),
        'l1_w_mem_kv': dense(ks[14], D_MODEL, 2 * N_MEM_HEADS * HEAD_DIM),
        'l1_w_out': dense(ks[15], B_OUT, D_MODEL),
        'l1_norm_ffn': gain(ks[16]),
        'l1_w_gate_up': dense(ks[17], D_MODEL, 2 * D_FF_2),
        'l1_w_down': dense(ks[18], D_FF_2, D_MODEL),
        'final_norm': gain(ks[19]),
    }

def second_block(x, mem, positions,
              l0_norm_mix, l0_norm_mem, l0_w_in, l0_w_mem_kv, l0_w_out, l0_norm_ffn, l0_w_gate_up, l0_w_down,
              l1_norm_mix, l1_norm_mem, l1_w_in, l1_w_mem_kv, l1_w_out, l1_norm_ffn, l1_w_gate_up, l1_w_down,
              final_norm):
    layers = (
        (l0_norm_mix, l0_norm_mem, l0_w_in, l0_w_mem_kv, l0_w_out, l0_norm_ffn, l0_w_gate_up, l0_w_down),
        (l1_norm_mix, l1_norm_mem, l1_w_in, l1_w_mem_kv, l1_w_out, l1_norm_ffn, l1_w_gate_up, l1_w_down),
    )
    for i in range(DEPTH):
        x = hybrid_layer(x, mem, positions, i, *layers[i])
    return rms_norm_2(x, final_norm)


def setup_inputs(seed=0):
    out = dict(first_inputs(seed))
    for name, value in second_inputs(seed + 1).items():
        if name != "x":
            out[name + "_2"] = value
    return out


def reference(
    x, c, ctx, c_ctx, w_mod, b_mod, g_pre_mix, g_post_mix, w_in, b_gate, conv_w, conv_b,
    conv_ln_g, conv_ln_b, w_conv_out, lam_q1, lam_k1, lam_q2, lam_k2, subln_g, w_attn_out,
    w_pool_group, pool_scale, w_pool_out, w_out, g_pre_ffn, g_post_ffn, w_ffn_in, w_ffn_out,
    mem_2, positions_2, l0_norm_mix_2, l0_norm_mem_2, l0_w_in_2, l0_w_mem_kv_2, l0_w_out_2,
    l0_norm_ffn_2, l0_w_gate_up_2, l0_w_down_2, l1_norm_mix_2, l1_norm_mem_2, l1_w_in_2,
    l1_w_mem_kv_2, l1_w_out_2, l1_norm_ffn_2, l1_w_gate_up_2, l1_w_down_2, final_norm_2,
):
    x = first_block(
        x, c, ctx, c_ctx, w_mod, b_mod, g_pre_mix, g_post_mix, w_in, b_gate, conv_w, conv_b,
        conv_ln_g, conv_ln_b, w_conv_out, lam_q1, lam_k1, lam_q2, lam_k2, subln_g, w_attn_out,
        w_pool_group, pool_scale, w_pool_out, w_out, g_pre_ffn, g_post_ffn, w_ffn_in, w_ffn_out,
    )
    return second_block(
        x, mem_2, positions_2, l0_norm_mix_2, l0_norm_mem_2, l0_w_in_2, l0_w_mem_kv_2,
        l0_w_out_2, l0_norm_ffn_2, l0_w_gate_up_2, l0_w_down_2, l1_norm_mix_2, l1_norm_mem_2,
        l1_w_in_2, l1_w_mem_kv_2, l1_w_out_2, l1_norm_ffn_2, l1_w_gate_up_2, l1_w_down_2,
        final_norm_2,
    )


_drawn_inputs = setup_inputs


def setup_inputs(seed=0):
    import zlib

    import numpy as np

    out = dict(_drawn_inputs(seed))
    spreads = {}
    factors = {'g_pre_mix': 2.995,
     'g_post_mix': 3.21,
     'b_gate': 5.431,
     'conv_b': 3.289,
     'conv_ln_g': 4.597,
     'conv_ln_b': 4.642,
     'lam_q1': 2.929,
     'lam_k1': 3.112,
     'lam_q2': 2.881,
     'lam_k2': 2.679,
     'subln_g': 4.484,
     'g_pre_ffn': 2.764,
     'g_post_ffn': 3.268,
     'l0_norm_mem_2': 8.0,
     'l0_norm_ffn_2': 3.945,
     'l1_norm_mix_2': 8.0,
     'l1_norm_mem_2': 8.0,
     'l1_norm_ffn_2': 4.764}
    for name, (base, spread) in spreads.items():
        noise = np.random.default_rng([zlib.crc32(name.encode()), seed]).standard_normal(out[name].shape)
        drawn = base * np.exp(spread * noise) if base else spread * noise
        out[name] = __import__('jax').numpy.asarray(drawn.astype(out[name].dtype))
    for name, factor in factors.items():
        out[name] = (out[name] * factor).astype(out[name].dtype)
    return out
```

```python
from contextlib import ExitStack
import math

import numpy as np

import concourse.bass as bass
from concourse import mybir

F32 = mybir.dt.float32
I32 = mybir.dt.int32
ALU = mybir.AluOpType
ACT = mybir.ActivationFunctionType
AX_X = mybir.AxisListType.X

P = 128
D = 1024
KT = D // P
SEQ = 256
DEPTH = 2
GRID_W = 64
EPS = 1e-6
CONV_CH, CONV_W = 512, 31
HALF_W = CONV_W // 2
HEADS, HEAD_DIM, V_DIM = 8, 64, 128
POOL_CH = 512
POOL_PAD = 8
NCH = CONV_CH // P
D_FF = 2816
FT = D_FF // P
COL_Q = 2 * CONV_CH
COL_K = COL_Q + 1024
COL_V = COL_K + 1024
COL_P = COL_V + 1024
COL_G = COL_P + POOL_CH
NEG = -1e30
TAKEN = -3e38
N_SEL = 64
IDX_HEADS = 8
SCALE = HEAD_DIM ** -0.5
BANKS = 8
SLOTS = 4
SLOT = 2048

ROW_PRE, ROW_FFN, ROW_GATE = 0, 8, 16
ROW_CB, ROW_LG, ROW_LB, ROW_PS, ROW_SUB, ROW_C, ROW_CC = 40, 44, 48, 52, 56, 57, 65
N_ROWS = 73


def shape_constants():
    f = np.float32
    d = np.arange(P)
    t = np.arange(SEQ)
    inv = f(10000.0) ** (-np.arange(0, 32, 2, dtype=f) / f(32))
    pos = np.where((d % 64 < 32)[:, None], (t // GRID_W)[None, :], (t % GRID_W)[None, :]).astype(f)
    ang = pos * inv[d % 16][:, None]

    def swap(half, rot):
        m = np.zeros((P, P), f)
        for i in range(P):
            r = i % 64
            if r % rot < half and r < (64 if rot == 32 and half == 16 else rot):
                m[i + half, i] = -1
            elif r < (64 if rot == 32 and half == 16 else rot):
                m[i - half, i] = 1
        return m

    idx_swap = swap(16, 32)
    idx_swap[:, d % 64 >= 32] = 0
    counts = np.zeros((4, SEQ), f)
    for g, w in enumerate((2, 4, 8, 16)):
        counts[g] = 1 / (np.clip(t + w // 2, 0, SEQ) - np.clip(t - w // 2, 0, SEQ)).astype(f)
    q = np.arange(SEQ)
    causal = np.where(q[None, :] <= q[:, None], 0, NEG).astype(f)
    dil = np.stack([np.where((q[None, :] <= q[:, None]) & ((q[:, None] - q[None, :]) % r == 0)
                             & ((q[:, None] - q[None, :]) // r <= P), 0, NEG).astype(f)
                    for r in (1, 4, 16)], 1)
    freq = f(10000.0) ** (-np.arange(32, dtype=f) / f(32))
    ifreq = f(10000.0) ** (-np.arange(16, dtype=f) / f(16))
    freqs = np.stack([freq[d % 32], np.where(d % 64 < 32, ifreq[d % 16], 0).astype(f)], 1)
    sel = np.zeros((2, 2, P), f)
    sel[0, 0] = sel[1, 1] = 1
    return {
        "ident": np.eye(P, dtype=f), "swaps": np.stack([swap(16, 32), swap(32, 64), idx_swap], 1),
        "grid_rope": np.stack([np.cos(ang), np.sin(ang)], 1).astype(f),
        "inv_counts": np.ascontiguousarray(np.broadcast_to(counts, (P, 4, SEQ))),
        "causal": causal.reshape(2, P, SEQ), "dilated": dil.reshape(2, P, 3, SEQ),
        "freqs": freqs, "pick": sel,
    }


def build(nc, A, out, stop_after=9):
    ctx = ExitStack()
    sems = {}

    def S(name):
        if name not in sems:
            sems[name] = ctx.enter_context(nc.semaphore(name))
        return sems[name]

    def sb(stack, name, shape, dt=F32):
        return stack.enter_context(nc.sbuf_tensor(name, shape, dt))

    PS = ctx.enter_context(nc.psum_tensor("PS", [P, BANKS, 512], F32))
    pe_done, act_step, dve_step, pool_step = S("pe_done"), S("act_step"), S("dve_step"), S("pool_step")
    bank_read = [S(f"bank_read{b}") for b in range(BANKS)]
    slot_full = [S(f"slot_full{s}") for s in range(SLOTS)]
    uses, milestones, bank_no = {}, {}, [0, 0]
    chunks, chunk_free, loads = [], [], [0] * SLOTS
    count = {"act": 0, "dve": 0, "pool": 0}

    X = sb(ctx, "X", [P, 4, D])
    HT = sb(ctx, "HT", [P, KT, 2 * SEQ])
    W = sb(ctx, "W", [P, SLOTS, SLOT])
    Y = sb(ctx, "Y", [P, 4, D])
    ident = sb(ctx, "ident", [P, P])
    swaps = sb(ctx, "swaps", [P, 3, P])
    ones = sb(ctx, "ones", [P, P])
    half = sb(ctx, "half", [P, 8])
    ss = sb(ctx, "ss", [P, 64])
    ms = sb(ctx, "ms", [P, 64])
    rstd = sb(ctx, "rstd", [P, 64])
    XN = sb(ctx, "XN", [P, 2, D])
    R = sb(ctx, "R", [P, 12288])
    stat_col = {}


    def bank(key):
        return PS[:, uses[key] % BANKS, :]

    def wait_result(eng, key):
        eng.wait_ge(pe_done, milestones[key])

    def read_out(ins, key):
        ins.then_inc(bank_read[uses[key] % BANKS], 1)

    def wait_read(eng, key):
        eng.wait_ge(bank_read[uses[key] % BANKS], uses[key] // BANKS + 1)

    class Tensor:

        def __init__(self, pe):
            self.pe = pe

        def open(self, key):
            u = uses[key] = bank_no[0]
            bank_no[0] += 1
            if u >= BANKS:
                self.pe.wait_ge(bank_read[u % BANKS], u // BANKS)
            return PS[:, u % BANKS, :]

        def close(self, ins, key):
            bank_no[1] += 1
            milestones[key] = bank_no[1]
            ins.then_inc(pe_done, 1)

        def mark(self, ins):
            bank_no[1] += 1
            ins.then_inc(pe_done, 1)

        def load(self, src, shape):
            i = len(chunks)
            pieces = src if isinstance(src, list) else [src]
            chunks.append((pieces, shape))
            chunk_free.append(None)
            loads[i % SLOTS] += 16 * len(pieces)
            self.pe.wait_ge(slot_full[i % SLOTS], loads[i % SLOTS])
            return i, slot(i, shape)

        def used(self, i):
            chunk_free[i] = bank_no[1]

    def slot(i, shape):
        a, b = shape
        return W[:, i % SLOTS, 0:a * b].rearrange("p (a b) -> p a b", a=a)

    def rows(w, k0, nk, c0, nc_):
        return w[k0 * P:(k0 + nk) * P, c0:c0 + nc_].rearrange("(k p) c -> p k c", p=P)


    def product_t(T, pe, name, w, c0, tiles, kts, rhs, n, source=None, before=None):
        per = SLOT // kts // P
        for j in range(tiles):
            if j % per == 0:
                here = min(per, tiles - j)
                src = source(j // per) if source else rows(w, 0, kts, c0 + j * P, here * P)
                i, ws = T.load(src, (kts, here * P))
            if before:
                before(j)
            ps = T.open((name, j))
            for k in range(kts):
                ins = pe.matmul(ps[:, 0:n], ws[:, k, (j % per) * P:(j % per + 1) * P], rhs(k, j),
                                start=(k == 0), stop=(k == kts - 1))
            T.close(ins, (name, j))
            if j % per == here - 1:
                T.used(i)

    def product(T, pe, name, w, kts, cols, tiles, lhs, before=None):
        for n in range(cols // 512):
            ps = {}
            for k0 in range(0, kts, 4):
                kk = min(4, kts - k0)
                i, ws = T.load(rows(w, k0, kk, n * 512, 512), (kk, 512))
                if k0 == 0:
                    for t in tiles:
                        ps[t] = T.open((name, n, t))
                for k in range(k0, k0 + kk):
                    if before and n == 0:
                        before(k)
                    for t in tiles:
                        ins = pe.matmul(ps[t], lhs(k, t), ws[:, k - k0, :], start=(k == 0), stop=(k == kts - 1))
                        if k == kts - 1:
                            T.close(ins, (name, n, t))
                if k0 + kk < kts:
                    T.mark(ins)
                T.used(i)


    def norm_cols(name):
        if name not in stat_col:
            stat_col[name] = 4 * (len(stat_col) % 16)
        return stat_col[name]

    def norm_act(act, name, src, tiles, dst, scale, bias, ready):
        c = norm_cols(name)
        for n, t in enumerate(tiles):
            ready(act, t)
            if n >= 2:
                wait_result(act, (name, tiles[n - 2], 1))
            act.activation(XN[:, n % 2, :], src(t), ACT.Square,
                           accum_out=ss[:, c + n:c + n + 1]).then_inc(S(name + "_squares"), 1)
            if n >= 1:
                columns(act, name, tiles[n - 1], 0, dst, scale, bias)
        columns(act, name, tiles[-1], 0, dst, scale, bias)

    def columns(eng, name, t, g, dst, scale, bias):
        key = (name, t, g)
        wait_result(eng, key)
        for k in range(4 * g, 4 * g + 4):
            src = bank(key)[:, (k % 4) * P:(k % 4 + 1) * P]
            if eng is nc.scalar:
                ins = eng.activation(dst(k, t), src, ACT.Identity, scale=scale(k, t), bias=bias(k, t) if bias else 0.0)
            elif bias:
                ins = eng.tensor_scalar(dst(k, t), src, scale(k, t), bias(k, t), ALU.mult, ALU.add)
            else:
                ins = eng.tensor_scalar(dst(k, t), src, scale(k, t), None, ALU.mult)
        read_out(ins, key)

    def rstd_pool(pool, name, tiles, width, sem):
        c = norm_cols(name)
        for n, t in enumerate(tiles):
            pool.wait_ge(S(name + "_squares"), n + 1)
            pool.tensor_scalar(ms[:, c + n:c + n + 1], ss[:, c + n:c + n + 1], 1.0 / width, EPS, ALU.mult,
                               ALU.add).then_inc(pool_step, 1)
            count["pool"] += 1
            pool.wait_ge(pool_step, count["pool"])
            pool.tensor_tensor(rstd[:, c + n:c + n + 1], ms[:, c + n:c + n + 1], half[:, 0:1],
                               ALU.pow).then_inc(S(name + sem), 1)

    def norm_dve(dve, name, src, tiles, dst, scale, bias, ready):
        c = norm_cols(name)
        for n, t in enumerate(tiles):
            ready(dve, t)
            dve.wait_ge(S(name + "_rstd"), n + 1)
            dve.tensor_scalar(XN[:, n % 2, :], src(t), rstd[:, c + n:c + n + 1], None,
                              ALU.mult).then_inc(S(name + "_xn"), 1)
            if n >= 1:
                columns(dve, name, tiles[n - 1], 1, dst, scale, bias)
        columns(dve, name, tiles[-1], 1, dst, scale, bias)

    def norm_pe(T, pe, name, tiles):
        for n, t in enumerate(tiles):
            pe.wait_ge(S(name + "_xn"), n + 1)
            transposes(T, pe, name, t, XN[:, n % 2, :])

    def transposes(T, pe, name, t, src):
        for g in range(2):
            ps = T.open((name, t, g))
            for k in range(4):
                c = (4 * g + k) * P
                ins = pe.transpose(ps[:, k * P:(k + 1) * P], src[:, c:c + P], ident[:, :])
            T.close(ins, (name, t, g))

    def norm_wait(eng, name, tiles):
        for t in tiles:
            for g in range(2):
                wait_read(eng, (name, t, g))

    def dve_link(dve, ins):
        count["dve"] += 1
        ins.then_inc(dve_step, 1)
        dve.wait_ge(dve_step, count["dve"])

    def act_link(act, ins):
        count["act"] += 1
        ins.then_inc(act_step, 1)
        act.wait_ge(act_step, count["act"])


    def rope_pe(T, pe, name, j, x, swap):
        wait_read(pe, (name, j))
        ps = T.open((name + "_rot", j))
        T.close(pe.matmul(ps[:, 0:SEQ], swap, x, start=True, stop=True), (name + "_rot", j))

    def rope_dve(dve, name, j, x, cos, sin, tmp):
        key = (name + "_rot", j)
        wait_result(dve, key)
        read_out(dve.tensor_tensor(tmp, bank(key)[:, 0:SEQ], sin, ALU.mult), key)
        wait_read(dve, key)
        dve_link(dve, dve.tensor_tensor(x, x, cos, ALU.mult))
        dve.tensor_tensor(x, x, tmp, ALU.add).then_inc(S(name + "_roped"), 1)

    st = ExitStack()
    QT = R[:, 0:4096].rearrange("p (j t) -> p j t", j=8)
    KTT = R[:, 4096:8192].rearrange("p (j t) -> p j t", j=8)
    V = R[:, 8192:12288].rearrange("p (j t) -> p j t", j=4)
    MT, OT = QT, KTT
    UT = R[:, 0:FT * 512].rearrange("p (j t) -> p j t", j=FT)
    UP = sb(st, "UP", [P, NCH, 2, SEQ + 2 * HALF_W])
    CV = sb(st, "CV", [P, NCH, 2, SEQ])
    PP = sb(st, "PP", [P, 4, 2, SEQ + 2 * POOL_PAD])
    G = sb(st, "G", [P, 2, D])
    TMP = sb(st, "TMP", [P, 4096])
    E2 = TMP[:, 0:2048].rearrange("p (b i k) -> p b i k", b=2, i=2)
    AA = TMP[:, 2048:3072].rearrange("p (b k) -> p b k", b=2)
    AT = TMP[:, 3072:4096].rearrange("p (b k) -> p b k", b=2)
    PT = XN[:, :, 0:2 * (SEQ + 2 * POOL_PAD)].rearrange("p b (s t) -> p b s t", s=2)
    GP = TMP[:, 1024:2048]
    MR = TMP[0:2, 2048:3072].rearrange("p (b k) -> p b k", b=2)
    BM = TMP[0:2, 3072:4096].rearrange("p (b k) -> p b k", b=2)
    stage = TMP[:, 0:512].rearrange("p (l m k) -> p l m k", l=2, m=2)
    lamv = TMP[:, 512:1024].rearrange("p (l m k) -> p l m k", l=2, m=4)
    SG = TMP[:, 0:1024].rearrange("p (b k) -> p b k", b=2)
    GY = TMP[:, 1024:2048].rearrange("p (b k) -> p b k", b=2)
    rope_tmp = TMP[:, 2048:2560].rearrange("p (b k) -> p b k", b=2)
    grid = sb(st, "grid", [P, 2, SEQ])
    counts = sb(st, "counts", [P, 4, SEQ])
    pick = sb(st, "pick", [2, 2, P])
    cols = sb(st, "cols", [P, 2, 2, P])
    silu_c = sb(st, "silu_c", [P, KT, 2])
    mod = sb(st, "mod", [P, 4, KT, 2])
    gain = sb(st, "gain", [P, 2, KT, 2])
    sub_g = sb(st, "sub_g", [P, 2])
    lams = sb(st, "lams", [P, 2, 8])
    mx = sb(st, "mx", [P, 2, 8])
    subs = sb(st, "subs", [P, 3, 4, 8])

    def first_rows(l):
        v = lambda n: A[n][l].rearrange("(r p) -> r p", p=P)
        lst = [(ROW_PRE, v("g_pre_mix")), (ROW_FFN, v("g_pre_ffn")), (ROW_GATE, v("b_gate")), (ROW_CB, v("conv_b")),
               (ROW_LG, v("conv_ln_g")), (ROW_LB, v("conv_ln_b")), (ROW_PS, v("pool_scale")), (ROW_SUB, v("subln_g")),
               (ROW_C, A["c"][0].rearrange("(r p) -> r p", p=P)), (ROW_CC, A["c_ctx"].rearrange("(r p) -> r p", p=P))]
        return lst

    def section(l, s):
        return "L%d_mod%d" % (l, s)

    SECTIONS = ((0, "col", 0), (1, "col", 1), (2, "row", 0), (3, "col", 2), (4, "col", 3), (5, "row", 1))

    def layer_tokens(l):
        ns = 2 if l < DEPTH - 1 else 1
        return ns, ns * SEQ, list(range(2 * ns))

    units_of = {l: [(t, h) for t in layer_tokens(l)[2] for h in range(HEADS)] for l in range(DEPTH)}

    def ffn_pe(T, pe, L, w_up, w_down, tiles, n, U=None):
        U = UT if U is None else U
        norm_pe(T, pe, L + "n2", tiles)
        norm_wait(pe, L + "n2", tiles)
        for c in range(FT // 2):
            ia, wa = T.load(rows(w_up, 0, KT, c * 256, 256), (KT, 256))
            ib, wb = T.load(rows(w_up, 0, KT, D_FF + c * 256, 256), (KT, 256))
            for jj in range(2):
                for nm, ws in (("ffn_gate", wa), ("ffn_up", wb)):
                    ps = T.open((L + nm, 2 * c + jj))
                    for k in range(KT):
                        ins = pe.matmul(ps[:, 0:n], ws[:, k, jj * P:(jj + 1) * P], HT[:, k, 0:n], start=(k == 0), stop=(k == KT - 1))
                    T.close(ins, (L + nm, 2 * c + jj))
            T.used(ia)
            T.used(ib)
        product(T, pe, L + "ffn", w_down, FT, D, tiles, lambda k, t: U[:, k, t * P:(t + 1) * P],
                before=lambda k: wait_read(pe, (L + "ffn_up", k)))

    def ffn_act(act, L, n, U=None):
        U = UT if U is None else U
        for j in range(FT):
            key = (L + "ffn_gate", j)
            wait_result(act, key)
            read_out(act.activation(U[:, j, 0:n], bank(key)[:, 0:n], ACT.Silu), key)

    def ffn_dve(dve, L, n, U=None):
        U = UT if U is None else U
        for j in range(FT):
            key = (L + "ffn_up", j)
            wait_read(dve, (L + "ffn_gate", j))
            wait_result(dve, key)
            read_out(dve.tensor_tensor(U[:, j, 0:n], U[:, j, 0:n], bank(key)[:, 0:n], ALU.mult), key)

    def post_act(act, L, name, tiles):
        c = norm_cols(L + name)
        for nn in range(2):
            for n, t in enumerate(tiles):
                key = (L + name, nn, t)
                wait_result(act, key)
                read_out(act.activation(Y[:, t, nn * 512:(nn + 1) * 512], bank(key), ACT.Copy), key)
                if nn == 1:
                    wait_read(act, key)
                    act.activation(XN[:, n % 2, :], Y[:, t, :], ACT.Square,
                                   accum_out=ss[:, c + n:c + n + 1]).then_inc(S(L + name + "_squares"), 1)

    def post_dve(dve, L, name, tiles, which):
        c = norm_cols(L + name)
        for s in range(2):
            for nn in range(2):
                if s * 2 in tiles:
                    wait_read(dve, ("L%s_mod_turn" % L[1], 2 + 3 * which, nn, s))
        for n, t in enumerate(tiles):
            dve.wait_ge(S(L + name + "_rstd"), n + 1)
            dve_link(dve, dve.scalar_tensor_tensor(Y[:, t, :], Y[:, t, :], rstd[:, c + n:c + n + 1], G[:, t // 2, :], ALU.mult, ALU.mult))
            dve.tensor_tensor(X[:, t, :], X[:, t, :], Y[:, t, :], ALU.add).then_inc(S(L + name + "_added"), 1)

    def h_dst(k, t):
        return HT[:, k, t * P:(t + 1) * P]

    def x_ready(l, which):
        def wait(eng, t):
            if which == 0 and l == 0:
                eng.wait_ge(S("x_loaded"), 16 * 2)
            else:
                eng.wait_ge(S(("L%d_ffn_added" % (l - 1)) if which == 0 else "L%d_y_added" % l), t + 1)
        return wait

    block1 = st.enter_context(nc.Block())

    @block1.tensor
    def _(pe):
        T = Tensor(pe)

        def modulation(l, part):
            name = "L%d_mod" % l
            lst = SECTIONS[3 * part:3 * part + 3]
            todo = []

            def turn(s, kind, n):
                wait_read(pe, (name, s, n))
                row = MR[:, n % 2, :]
                if kind == "col":
                    ps = T.open((name + "_turn", s, n))
                    for k in range(4):
                        ins = pe.transpose(ps[:, 2 * k:2 * k + 2], row[:, k * P:(k + 1) * P], ident[0:2, 0:2])
                    T.close(ins, (name + "_turn", s, n))
                else:
                    for m in range(2):
                        ps = T.open((name + "_turn", s, n, m))
                        T.close(pe.matmul(ps, pick[:, m, :], row, start=True, stop=True), (name + "_turn", s, n, m))

            for s, kind, _ in lst:
                for n in range(2):
                    for k0 in (0, 4):
                        i, ws = T.load(rows(A["w_mod"][l], k0, 4, s * D + n * 512, 512), (4, 512))
                        if k0 == 0:
                            ps = T.open((name, s, n))
                        for k in range(4):
                            ins = pe.matmul(ps[0:2, :], silu_c[:, k0 + k, :], ws[:, k, :], start=(k0 + k == 0), stop=(k0 + k == 7))
                        if k0 == 0:
                            T.mark(ins)
                        else:
                            T.close(ins, (name, s, n))
                        T.used(i)
                    todo.append((s, kind, n))
                    if len(todo) > 1:
                        turn(*todo.pop(0))
            turn(*todo.pop(0))

        pe.wait_ge(S("consts"), 16 * 5)
        for l in range(DEPTH):
            for m in range(2):
                if m == 0:
                    pe.wait_ge(S("params%d" % l), 16 * 11)
                ps = T.open(("cols", l, m))
                T.close(pe.transpose(ps[:, 0:P], stage[:, l, m, :], ident[:, :]), ("cols", l, m))
        pe.wait_ge(S("silu_c"), 1)
        modulation(0, 0)
        for l in range(DEPTH):
            ns, n, tiles = layer_tokens(l)
            L = "L%d_" % l
            if l:
                modulation(l, 0)
            norm_pe(T, pe, L + "n1", [0, 1, 2, 3])
            norm_wait(pe, L + "n1", [0, 1, 2, 3])
            w_in = A["w_in"][l]
            own = lambda k, j: HT[:, k, 0:n]
            every = lambda k, j: HT[:, k, :]
            order = [0, 4, 1, 5, 2, 6, 3, 7]
            for c in range(2):
                ia, wa = T.load(rows(w_in, 0, KT, c * 256, 256), (KT, 256))
                ib, wb = T.load(rows(w_in, 0, KT, CONV_CH + c * 256, 256), (KT, 256))
                for jj in range(2):
                    for nm, ws in (("glu_gate", wb), ("glu", wa)):
                        ps = T.open((L + nm, 2 * c + jj))
                        for k in range(KT):
                            ins = pe.matmul(ps[:, 0:n], ws[:, k, jj * P:(jj + 1) * P], own(k, 0), start=(k == 0), stop=(k == KT - 1))
                        T.close(ins, (L + nm, 2 * c + jj))
                T.used(ia)
                T.used(ib)
            product_t(T, pe, L + "pool", w_in, COL_P, 4, KT, own, n)

            def turn_q(j):
                if j >= 1:
                    rope_pe(T, pe, L + "q", j - 1, QT[:, j - 1, 0:SEQ], swaps[:, 0, :])

            def turn_k(j):
                if j == 0:
                    rope_pe(T, pe, L + "q", 7, QT[:, 7, 0:SEQ], swaps[:, 0, :])
                else:
                    rope_pe(T, pe, L + "k", j - 1, KTT[:, j - 1, 0:SEQ], swaps[:, 0, :])

            product_t(T, pe, L + "q", w_in, COL_Q, 8, KT, own, n, before=turn_q)
            product_t(T, pe, L + "k", w_in, COL_K, 8, KT, every, 2 * SEQ, before=turn_k)
            rope_pe(T, pe, L + "k", 7, KTT[:, 7, 0:SEQ], swaps[:, 0, :])
            product(T, pe, L + "v", w_in[:, COL_V:COL_P], KT, D, [0, 1, 2, 3], lambda k, t: HT[:, k, t * P:(t + 1) * P])
            pe.wait_ge(S(L + "conv"), NCH)
            ps = T.open((L + "mean",))
            for j in range(NCH):
                ins = pe.matmul(ps[:, 0:n], ones[:, :], CV[:, j, 0:ns, :], start=(j == 0), stop=(j == NCH - 1))
            T.close(ins, (L + "mean",))
            us = units_of[l]
            pe.wait_ge(S(L + "q_roped"), 8)
            pe.wait_ge(S(L + "k_roped"), 8)
            for j in range(4, 8):
                wait_read(pe, (L + "k", j))
            for t in range(4):
                wait_read(pe, (L + "v", 1, t))
                wait_read(pe, (L + "v", 0, t))

            def blocks(t):
                return [0, 1, 2, 3] if t < 2 else [2, 3]

            for i in range(len(us) + 2):
                if i < len(us):
                    t, h = us[i]
                    k0, k1 = (0, 2 * SEQ) if t < 2 else (SEQ, 2 * SEQ)
                    for m in range(2):
                        ps = T.open((L + "s", i, m))
                        T.close(pe.matmul(ps[:, 0:k1 - k0], QT[64 * m:64 * m + 64, h, t * P:(t + 1) * P],
                                          KTT[64 * m:64 * m + 64, h, k0:k1], start=True, stop=True), (L + "s", i, m))
                if i == 1:
                    pe.wait_ge(S(L + "conv_sq"), NCH)
                    ps = T.open((L + "var",))
                    for j in range(NCH):
                        ins = pe.matmul(ps[:, 0:n], ones[:, :], UP[:, j, 0:ns, HALF_W:HALF_W + SEQ], start=(j == 0), stop=(j == NCH - 1))
                    T.close(ins, (L + "var",))
                if 1 <= i <= len(us):
                    t, h = us[i - 1]
                    pe.wait_ge(S(L + "probs"), i)
                    ps = T.open((L + "pt", i - 1))
                    for b in range(len(blocks(t))):
                        ins = pe.transpose(ps[:, b * P:(b + 1) * P], AA[:, (i - 1) % 2, b * P:(b + 1) * P], ident[:, :])
                    T.close(ins, (L + "pt", i - 1))
                if i >= 2:
                    t, h = us[i - 2]
                    wait_read(pe, (L + "pt", i - 2))
                    ps = T.open((L + "o", i - 2))
                    for b, kb in enumerate(blocks(t)):
                        ins = pe.matmul(ps[:, 0:V_DIM], AT[:, i % 2, b * P:(b + 1) * P], V[:, kb, h * V_DIM:(h + 1) * V_DIM],
                                        start=(b == 0), stop=(b == len(blocks(t)) - 1))
                    T.close(ins, (L + "o", i - 2))
            pe.wait_ge(S(L + "pooled"), 4)
            i, ws = T.load(A["w_pool_group"][l].rearrange("g c d -> c g d"), (4, P))
            for g in range(4):
                ps = T.open((L + "mixed", g))
                ins = pe.matmul(ps[:, 0:n], ws[:, g, :], PP[:, g, 0:ns, POOL_PAD:POOL_PAD + SEQ], start=True, stop=True)
                T.close(ins, (L + "mixed", g))
            T.used(i)

            def branch(name, gate_col, w, kts, rhs, ready):
                per = SLOT // kts // P
                for j in range(KT):
                    if j % 2 == 0:
                        ig, wg = T.load(rows(w_in, 0, KT, COL_G + gate_col * D + j * P, 256), (KT, 256))
                    ps = T.open((name + "_gate", j))
                    for k in range(KT):
                        ins = pe.matmul(ps[:, 0:n], wg[:, k, (j % 2) * P:(j % 2 + 1) * P], own(k, 0), start=(k == 0), stop=(k == KT - 1))
                    T.close(ins, (name + "_gate", j))
                    if j % 2 == 1:
                        T.used(ig)
                    if j == 0:
                        ready()
                    if j % per == 0:
                        iy, wy = T.load(rows(w, 0, kts, j * P, per * P), (kts, per * P))
                    ps = T.open((name, j))
                    for k in range(kts):
                        ins = pe.matmul(ps[:, 0:n], wy[:, k, (j % per) * P:(j % per + 1) * P], rhs(k), start=(k == 0), stop=(k == kts - 1))
                    T.close(ins, (name, j))
                    if j % per == per - 1:
                        T.used(iy)

            def mixed_ready():
                for g in range(4):
                    wait_read(pe, (L + "mixed", g))

            branch(L + "yc", 2, A["w_pool_out"][l], 4, lambda k: PP[:, k, 0:ns, POOL_PAD:POOL_PAD + SEQ], mixed_ready)
            branch(L + "ya", 0, A["w_conv_out"][l], 4, lambda k: CV[:, k, 0:ns, :],
                   lambda: pe.wait_ge(S(L + "conv_act"), NCH))
            for t in tiles:
                pe.wait_ge(S(L + "o_normed"), t + 1)
                transposes(T, pe, L + "ot", t, Y[:, t, :])
            branch(L + "yb", 1, A["w_attn_out"][l], 8, lambda k: OT[:, k, 0:n], lambda: norm_wait(pe, L + "ot", tiles))
            pe.wait_ge(S(L + "merged"), 2 * KT)
            product(T, pe, L + "y", A["w_out"][l], KT, D, tiles, lambda k, t: MT[:, k, t * P:(t + 1) * P])
            modulation(l, 1)
            ffn_pe(T, pe, L, A["w_ffn_in"][l], A["w_ffn_out"][l], tiles, n)

    @block1.scalar
    def _(act):
        act.wait_ge(S("zeroed"), 1)
        for l in range(DEPTH):
            for r, src in first_rows(l):
                act.dma_start(stage[r:r + src.shape[0], l, 0, :], src).then_inc(S("params%d" % l), 16)
            act.dma_start(stage[0:CONV_W * NCH, l, 1, :], A["conv_w"][l].rearrange("t (j p) -> (t j) p", p=P)).then_inc(S("params%d" % l), 16)

        def modulation(l, part):
            name = "L%d_mod" % l
            for s, kind, at in SECTIONS[3 * part:3 * part + 3]:
                for n in range(2):
                    key = (name + "_turn", s, n)
                    if kind == "col":
                        wait_result(act, key)
                        src = bank(key)[:, 0:8].rearrange("p (k m) -> p k m", m=2)
                        read_out(act.activation(mod[:, at, 4 * n:4 * n + 4, :], src, ACT.Copy), key)

        for l in range(DEPTH):
            for m in range(2):
                wait_result(act, ("cols", l, m))
                read_out(act.activation(cols[:, l, m, :], bank(("cols", l, m))[:, 0:P], ACT.Copy), ("cols", l, m))
        wait_read(act, ("cols", 0, 0))
        act.activation(silu_c[:, :, :].rearrange("p k m -> p m k"), cols[:, 0, 0, ROW_C:ROW_C + 16].rearrange("p (m k) -> p m k", m=2),
                       ACT.Silu).then_inc(S("silu_c"), 1)
        for l in range(DEPTH):
            act.wait_ge(S("lam_sums"), l + 1)
            act.activation(lams[:, l, 2:4], lams[:, l, 0:2], ACT.Exp).then_inc(S("lam_exps"), 1)
        modulation(0, 0)
        for l in range(DEPTH):
            ns, n, tiles = layer_tokens(l)
            L = "L%d_" % l
            if l:
                modulation(l, 0)
            act.wait_ge(S(L + "gains"), 1)
            norm_act(act, L + "n1", lambda t: X[:, t, :], [0, 1, 2, 3], h_dst, lambda k, t: gain[:, 0, k, t // 2:t // 2 + 1],
                     lambda k, t: mod[:, 0, k, t // 2:t // 2 + 1], x_ready(l, 0))
            for j in range(NCH):
                key = (L + "glu_gate", j)
                wait_result(act, key)
                if j >= 2:
                    wait_read(act, (L + "glu", j - 2))
                read_out(act.activation(SG[:, j % 2, 0:n], bank(key)[:, 0:n], ACT.Sigmoid), key)
            for j in range(4):
                key = (L + "pool", j)
                wait_result(act, key)
                read_out(act.activation(PP[:, j, 0:ns, POOL_PAD:POOL_PAD + SEQ], bank(key)[:, 0:n].rearrange("p (s t) -> p s t", s=ns), ACT.Copy), key)
            for nm, dst, w in (("q", QT, n), ("k", KTT, 2 * SEQ)):
                for j in range(8):
                    key = (L + nm, j)
                    wait_result(act, key)
                    read_out(act.activation(dst[:, j, 0:w], bank(key)[:, 0:w], ACT.Copy), key)
            for nn in range(2):
                for t in range(4):
                    key = (L + "v", nn, t)
                    wait_result(act, key)
                    read_out(act.activation(V[:, t, nn * 512:(nn + 1) * 512], bank(key), ACT.Copy), key)
            us = units_of[l]
            for i in range(len(us) + 1):
                if i < len(us):
                    t, h = us[i]
                    w = 2 * SEQ if t < 2 else SEQ
                    act.wait_ge(S(L + "maxes"), i + 1)
                    if i >= 2:
                        act.wait_ge(S(L + "probs"), i - 1)
                    for m in range(2):
                        key = (L + "s", i, m)
                        read_out(act.activation(E2[:, i % 2, m, 0:w], bank(key)[:, 0:w], ACT.Exp, bias=mx[:, i % 2, 2 + m:3 + m],
                                                scale=SCALE, accum_out=mx[:, i % 2, 4 + m:5 + m]), key)
                if i >= 1:
                    w = 2 * SEQ if us[i - 1][0] < 2 else SEQ
                    key = (L + "pt", i - 1)
                    wait_result(act, key)
                    if i >= 3:
                        wait_result(act, (L + "o", i - 3))
                    read_out(act.activation(AT[:, (i - 1) % 2, 0:w], bank(key)[:, 0:w], ACT.Copy), key)
            wait_read(act, (L + "var",))
            act.activation(XN[:, 0, 0:n], XN[:, 0, 0:n], ACT.Sqrt).then_inc(S(L + "std"), 1)
            for j in range(NCH):
                act.wait_ge(S(L + "conv_normed"), j + 1)
                act.activation(CV[:, j, 0:ns, :], CV[:, j, 0:ns, :], ACT.Silu, scale=cols[:, l, 0, ROW_LG + j:ROW_LG + j + 1],
                               bias=cols[:, l, 0, ROW_LB + j:ROW_LB + j + 1]).then_inc(S(L + "conv_act"), 1)
            for g in range(4):
                key = (L + "mixed", g)
                wait_result(act, key)
                read_out(act.activation(PP[:, g, 0:ns, POOL_PAD:POOL_PAD + SEQ], bank(key)[:, 0:n].rearrange("p (s t) -> p s t", s=ns), ACT.Copy,
                                        scale=cols[:, l, 0, ROW_PS + g:ROW_PS + g + 1]), key)
            done = 0
            for nm, gc in (("yc", 2), ("ya", 0), ("yb", 1)):
                if nm == "yb":
                    for t in tiles:
                        for g in range(2):
                            key = (L + "ot", t, g)
                            wait_result(act, key)
                            read_out(act.activation(OT[:, 4 * g:4 * g + 4, t * P:(t + 1) * P], bank(key).rearrange("p (k t) -> p k t", k=4),
                                                    ACT.Copy, scale=sub_g[:, l:l + 1]), key)
                for j in range(KT):
                    key = (L + nm + "_gate", j)
                    wait_result(act, key)
                    if done >= 2:
                        wait_read(act, (L + ("yc", "ya", "yb")[(done - 2) // KT], (done - 2) % KT))
                    c = ROW_GATE + 8 * gc + j
                    read_out(act.activation(SG[:, done % 2, 0:n], bank(key)[:, 0:n], ACT.Sigmoid, bias=cols[:, l, 0, c:c + 1]), key)
                    done += 1
            post_act(act, L, "y", tiles)
            modulation(l, 1)
            act.wait_ge(S(L + "gains"), 2)
            norm_act(act, L + "n2", lambda t: X[:, t, :], tiles, h_dst, lambda k, t: gain[:, 1, k, t // 2:t // 2 + 1],
                     lambda k, t: mod[:, 2, k, t // 2:t // 2 + 1], x_ready(l, 1))
            ffn_act(act, L, n)
            post_act(act, L, "ffn", tiles)

    @block1.gpsimd
    def _(pool):
        pool.memset(TMP[:, 0:512], 0.0).then_inc(S("zeroed"), 1)
        pool.memset(ones[:], 1.0).then_inc(S("filled"), 1)
        pool.memset(half[:], -0.5).then_inc(S("filled"), 1)
        pool.memset(UP[:], 0.0).then_inc(S("filled"), 1)
        pool.memset(PP[:], 0.0).then_inc(S("filled"), 1)
        pool.wait_ge(S("filled"), 4)

        def bias_rows(l, part):
            for s, _, _ in SECTIONS[3 * part:3 * part + 3]:
                for n in range(2):
                    i = 12 * l + 2 * s + n
                    if i >= 2:
                        l2, s2 = (i - 2) // 12, ((i - 2) % 12) // 2
                        wait_read(pool, ("L%d_mod" % l2, s2, n))
                    src = A["b_mod"][l:l + 1, s * D + n * 512:s * D + (n + 1) * 512].broadcast_to([2, 512])
                    pool.dma_start(BM[:, n, :], src).then_inc(S("bias_row%d" % n), 16)

        def gain_row(l, part):
            if l or part:
                l2, s2 = (l, 2) if part else (l - 1, 5)
                for n in range(2):
                    for m in range(2):
                        wait_read(pool, ("L%d_mod_turn" % l2, s2, n, m))
            src = A["g_post_ffn" if part else "g_post_mix"][l:l + 1, :].broadcast_to([P, D])
            pool.dma_start(GP[:, :], src).then_inc(S("gain_row"), 16)

        gain_row(0, 0)
        bias_rows(0, 0)
        for l in range(DEPTH):
            ns, n, tiles = layer_tokens(l)
            L = "L%d_" % l
            if l:
                gain_row(l, 0)
                bias_rows(l, 0)
            rstd_pool(pool, L + "n1", [0, 1, 2, 3], D, "_rstd")
            for g in range(4):
                wait_read(pool, (L + "pool", g))
                if g:
                    pool.wait_ge(S(L + "pooled"), g)
                src = PP[:, g, 0:ns, :]
                lo, hi, off = 0, SEQ + 2 * POOL_PAD, 1
                for step in range(g + 1):
                    dst = PT[:, step % 2, 0:ns, :]
                    a, b = (1, 0) if step == 0 else (2 ** (step - 1), 2 ** (step - 1))
                    lo, hi = lo + a, hi - b
                    pool.tensor_tensor(dst[:, :, lo:hi], src[:, :, lo - a:hi - a], src[:, :, lo + b:hi + b], ALU.add).then_inc(pool_step, 1)
                    count["pool"] += 1
                    pool.wait_ge(pool_step, count["pool"])
                    src = dst
                mid = PT[:, g % 2, 0:ns, POOL_PAD:POOL_PAD + SEQ]
                inside = PP[:, g, 0:ns, POOL_PAD:POOL_PAD + SEQ]
                for s in range(ns):
                    pool.tensor_tensor(mid[:, s, :], mid[:, s, :], counts[:, g, :], ALU.mult).then_inc(pool_step, 1)
                    count["pool"] += 1
                pool.wait_ge(pool_step, count["pool"])
                pool.tensor_tensor(inside, mid, inside, ALU.subtract).then_inc(S(L + "pooled"), 1)
            for t in tiles:
                pool.wait_ge(S(L + "o_squares"), t + 1)
                pool.tensor_tensor(subs[:, 2, t, :], subs[:, 1, t, :], half[:, 0:8], ALU.pow).then_inc(S(L + "o_rstd"), 1)
            rstd_pool(pool, L + "y", tiles, D, "_rstd")
            pool.wait_ge(S(L + "merged"), 2 * KT)
            gain_row(l, 1)
            bias_rows(l, 1)
            rstd_pool(pool, L + "n2", tiles, D, "_rstd")
            rstd_pool(pool, L + "ffn", tiles, D, "_rstd")

    @block1.vector
    def _(dve):
        def modulation(l, part):
            name = "L%d_mod" % l
            lst = SECTIONS[3 * part:3 * part + 3]
            todo = []

            def gates(s, n):
                for m in range(2):
                    key = (name + "_turn", s, n, m)
                    wait_result(dve, key)
                    ins = dve.tensor_tensor(G[:, m, n * 512:(n + 1) * 512], bank(key), GP[:, n * 512:(n + 1) * 512], ALU.mult)
                    read_out(ins, key)

            for s, kind, at in lst:
                for n in range(2):
                    i = 12 * l + 2 * s + n
                    key = (name, s, n)
                    wait_result(dve, key)
                    dve.wait_ge(S("bias_row%d" % n), 16 * (i // 2 + 1))
                    if i >= 2:
                        l2, s2, n2 = (i - 2) // 12, ((i - 2) % 12) // 2, i % 2
                        kind2 = SECTIONS[s2][1]
                        wait_result(dve, ("L%d_mod_turn" % l2, s2, n2) + ((1,) if kind2 == "row" else ()))
                    ins = dve.tensor_tensor(MR[:, n, :], bank(key)[0:2, :], BM[:, n, :], ALU.add)
                    read_out(ins, key)
                    if kind == "row" and n == 1:
                        dve.wait_ge(S("gain_row"), 16 * (2 * l + part + 1))
                        gates(s, 0)
            gates(lst[-1][0], 1)
            for n in range(2):
                wait_read(dve, (name + "_turn", 1 + 3 * part, n))
            for m in range(2):
                ins = dve.scalar_tensor_tensor(gain[:, part, :, m], mod[:, 1 + 2 * part, :, m], 1.0,
                                               cols[:, l, 0, (ROW_FFN if part else ROW_PRE):(ROW_FFN if part else ROW_PRE) + KT], ALU.add, ALU.mult)
                if m == 0:
                    dve_link(dve, ins)
            ins.then_inc(S("L%d_gains" % l), 1)

        dve.wait_ge(S("filled"), 4)
        dve.wait_ge(S("consts"), 16 * 5)
        dve.wait_ge(S("lam_loaded"), 16 * 8)
        for l in range(DEPTH):
            for m in range(2):
                dve_link(dve, dve.tensor_tensor(lamv[:, l, 2 * m, :], lamv[:, l, 2 * m, :], lamv[:, l, 2 * m + 1, :], ALU.mult))
            dve.tensor_reduce(lams[:, l, 0:2], lamv[:, l, 0:4:2, :], AX_X, ALU.add).then_inc(S("lam_sums"), 1)
        for l in range(DEPTH):
            lam_init = 0.8 - 0.6 * math.exp(-0.3 * l)
            dve.wait_ge(S("lam_exps"), l + 1)
            dve_link(dve, dve.tensor_tensor(lams[:, l, 4:5], lams[:, l, 3:4], lams[:, l, 2:3], ALU.subtract))
            dve_link(dve, dve.tensor_scalar(lams[:, l, 5:6], lams[:, l, 4:5], -lam_init, None, ALU.add))
            wait_read(dve, ("cols", l, 0))
            dve_link(dve, dve.tensor_scalar(sub_g[:, l:l + 1], cols[:, l, 0, ROW_SUB:ROW_SUB + 1], 1.0 - lam_init, None, ALU.mult))
            wait_read(dve, ("cols", l, 1))
        modulation(0, 0)
        for l in range(DEPTH):
            ns, n, tiles = layer_tokens(l)
            L = "L%d_" % l
            if l:
                modulation(l, 0)
            norm_dve(dve, L + "n1", lambda t: X[:, t, :], [0, 1, 2, 3], h_dst, lambda k, t: gain[:, 0, k, t // 2:t // 2 + 1],
                     lambda k, t: mod[:, 0, k, t // 2:t // 2 + 1], x_ready(l, 0))
            for j in range(NCH):
                key = (L + "glu", j)
                wait_read(dve, (L + "glu_gate", j))
                wait_result(dve, key)
                read_out(dve.tensor_tensor(UP[:, j, 0:ns, HALF_W:HALF_W + SEQ], bank(key)[:, 0:n].rearrange("p (s t) -> p s t", s=ns),
                                           SG[:, j % 2, 0:n].rearrange("p (s t) -> p s t", s=ns), ALU.mult), key)
            for j in range(NCH):
                wait_read(dve, (L + "glu", j))
            ropes = [("q", j) for j in range(8)] + [("k", j) for j in range(8)]
            last = [0] * NCH
            for tap in range(CONV_W):
                for j in range(NCH):
                    wt = cols[:, l, 1, tap * NCH + j:tap * NCH + j + 1]
                    src = UP[:, j, 0:ns, tap:tap + SEQ]
                    if tap == 0:
                        ins = dve.tensor_scalar(CV[:, j, 0:ns, :], src, wt, cols[:, l, 0, ROW_CB + j:ROW_CB + j + 1], ALU.mult, ALU.add)
                    else:
                        dve.wait_ge(dve_step, last[j])
                        ins = dve.scalar_tensor_tensor(CV[:, j, 0:ns, :], src, wt, CV[:, j, 0:ns, :], ALU.mult, ALU.add)
                    if tap < CONV_W - 1:
                        count["dve"] += 1
                        last[j] = count["dve"]
                        ins.then_inc(dve_step, 1)
                    else:
                        ins.then_inc(S(L + "conv"), 1)
                if tap % 2 == 1 and ropes:
                    nm, j = ropes.pop(0)
                    x = (QT if nm == "q" else KTT)[:, j, 0:SEQ]
                    rope_dve(dve, L + nm, j, x, grid[:, 0, :], grid[:, 1, :], rope_tmp[:, j % 2, :])
            for nm, j in ropes:
                x = (QT if nm == "q" else KTT)[:, j, 0:SEQ]
                rope_dve(dve, L + nm, j, x, grid[:, 0, :], grid[:, 1, :], rope_tmp[:, j % 2, :])
            key = (L + "mean",)
            wait_result(dve, key)
            dve.wait_ge(S(L + "pooled"), 4)
            dve_link(dve, dve.tensor_scalar(XN[:, 0, 0:n], bank(key)[:, 0:n], -1.0 / CONV_CH, None, ALU.mult))
            for j in range(NCH):
                ins = dve.tensor_tensor(CV[:, j, 0:ns, :], CV[:, j, 0:ns, :], XN[:, 0, 0:n].rearrange("p (s t) -> p s t", s=ns), ALU.add)
                if j == NCH - 1:
                    read_out(ins, key)
                    wait_read(dve, key)
                else:
                    dve_link(dve, ins)
            for j in range(NCH):
                dve.tensor_tensor(UP[:, j, 0:ns, HALF_W:HALF_W + SEQ], CV[:, j, 0:ns, :], CV[:, j, 0:ns, :], ALU.mult).then_inc(S(L + "conv_sq"), 1)
            us = units_of[l]

            def maxes(i):
                t, h = us[i]
                w = 2 * SEQ if t < 2 else SEQ
                for m in range(2):
                    wait_result(dve, (L + "s", i, m))
                    ins = dve.tensor_reduce(mx[:, i % 2, m:m + 1], bank((L + "s", i, m))[:, 0:w], AX_X, ALU.max)
                dve_link(dve, ins)
                dve.tensor_scalar(mx[:, i % 2, 2:4], mx[:, i % 2, 0:2], -SCALE, None, ALU.mult).then_inc(S(L + "maxes"), 1)

            def probs(i):
                w = 2 * SEQ if us[i][0] < 2 else SEQ
                for m in range(2):
                    wait_read(dve, (L + "s", i, m))
                dve_link(dve, dve.reciprocal(mx[:, i % 2, 6:8], mx[:, i % 2, 4:6]))
                dve_link(dve, dve.tensor_scalar(mx[:, i % 2, 7:8], mx[:, i % 2, 7:8], lams[:, l, 5:6], None, ALU.mult))
                if i >= 2:
                    wait_result(dve, (L + "pt", i - 2))
                dve_link(dve, dve.tensor_scalar(AA[:, i % 2, 0:w], E2[:, i % 2, 0, 0:w], mx[:, i % 2, 6:7], None, ALU.mult))
                dve.scalar_tensor_tensor(AA[:, i % 2, 0:w], E2[:, i % 2, 1, 0:w], mx[:, i % 2, 7:8], AA[:, i % 2, 0:w],
                                         ALU.mult, ALU.add).then_inc(S(L + "probs"), 1)

            def take_o(i):
                t, h = us[i]
                key = (L + "o", i)
                wait_result(dve, key)
                read_out(dve.tensor_copy(Y[:, t, h * V_DIM:(h + 1) * V_DIM], bank(key)[:, 0:V_DIM]), key)

            for i in range(len(us) + 3):
                if i < len(us):
                    maxes(i)
                if i == 2:
                    key = (L + "var",)
                    wait_result(dve, key)
                    read_out(dve.tensor_scalar(XN[:, 0, 0:n], bank(key)[:, 0:n], 1.0 / CONV_CH, EPS, ALU.mult, ALU.add), key)
                if 1 <= i <= len(us):
                    probs(i - 1)
                if i >= 3:
                    take_o(i - 3)
            dve.wait_ge(S(L + "std"), 1)
            dve_link(dve, dve.reciprocal(XN[:, 1, 0:n], XN[:, 0, 0:n]))
            for j in range(NCH):
                dve.tensor_tensor(CV[:, j, 0:ns, :], CV[:, j, 0:ns, :], XN[:, 1, 0:n].rearrange("p (s t) -> p s t", s=ns),
                                  ALU.mult).then_inc(S(L + "conv_normed"), 1)
            sq = TMP[:, 2048:3072]
            for t in tiles:
                for h in range(HEADS):
                    i = t * HEADS + h
                    wait_read(dve, (L + "o", i))
                dve_link(dve, dve.tensor_tensor(sq, Y[:, t, :], Y[:, t, :], ALU.mult))
                dve_link(dve, dve.tensor_reduce(subs[:, 0, t, :], sq.rearrange("p (h d) -> p h d", h=HEADS), AX_X, ALU.add))
                dve.tensor_scalar(subs[:, 1, t, :], subs[:, 0, t, :], 1.0 / V_DIM, EPS, ALU.mult, ALU.add).then_inc(S(L + "o_squares"), 1)
                dve.wait_ge(S(L + "o_rstd"), t + 1)
                yv = Y[:, t, :].rearrange("p (h d) -> p h d", h=HEADS)
                dve.tensor_tensor(yv, yv, subs[:, 2, t, :].rearrange("p (h o) -> p h o", o=1).broadcast_to([P, HEADS, V_DIM]),
                                  ALU.mult).then_inc(S(L + "o_normed"), 1)
            done = 0
            for nm in ("yc", "ya", "yb"):
                for j in range(KT):
                    key = (L + nm, j)
                    wait_result(dve, key)
                    wait_read(dve, (L + nm + "_gate", j))
                    if nm == "yc":
                        ins = dve.tensor_tensor(MT[:, j, 0:n], bank(key)[:, 0:n], SG[:, done % 2, 0:n], ALU.mult)
                        read_out(ins, key)
                    else:
                        read_out(dve.tensor_tensor(GY[:, done % 2, 0:n], bank(key)[:, 0:n], SG[:, done % 2, 0:n], ALU.mult), key)
                        wait_read(dve, key)
                        wait_read(dve, (L + "yc", j))
                        if nm == "yb":
                            dve.wait_ge(S(L + "merged"), j + 1)
                        dve.tensor_tensor(MT[:, j, 0:n], MT[:, j, 0:n], GY[:, done % 2, 0:n], ALU.add).then_inc(S(L + "merged"), 1)
                    done += 1
            post_dve(dve, L, "y", tiles, 0)
            modulation(l, 1)
            norm_dve(dve, L + "n2", lambda t: X[:, t, :], tiles, h_dst, lambda k, t: gain[:, 1, k, t // 2:t // 2 + 1],
                     lambda k, t: mod[:, 2, k, t // 2:t // 2 + 1], x_ready(l, 1))
            ffn_dve(dve, L, n)
            post_dve(dve, L, "ffn", tiles, 1)

    done1 = len(chunks)

    def load_chunks(sp, lo, hi):
        for i in range(lo, hi):
            if i >= SLOTS:
                sp.wait_ge(pe_done, chunk_free[i - SLOTS])
            pieces, shape = chunks[i]
            dst = slot(i, shape)
            w = shape[1] // len(pieces)
            for m, piece in enumerate(pieces):
                sp.dma_start(dst[:, :, m * w:(m + 1) * w], piece).then_inc(slot_full[i % SLOTS], 16)

    @block1.sync
    def _(sp):
        sp.dma_start(ident[:, :], A["ident"]).then_inc(S("consts"), 16)
        sp.dma_start(swaps[:], A["swaps"]).then_inc(S("consts"), 16)
        sp.dma_start(grid[:], A["grid_rope"]).then_inc(S("consts"), 16)
        sp.dma_start(pick[:], A["pick"]).then_inc(S("consts"), 16)
        sp.dma_start(counts[:], A["inv_counts"]).then_inc(S("consts"), 16)
        for l in range(DEPTH):
            for m, v in enumerate(("lam_q1", "lam_k1", "lam_q2", "lam_k2")):
                sp.dma_start(lamv[:, l, m, :], A[v][l:l + 1, :].broadcast_to([P, 64])).then_inc(S("lam_loaded"), 16)
        sp.dma_start(X[:, 0:2, :], A["x"][0].rearrange("(t p) d -> p t d", p=P)).then_inc(S("x_loaded"), 16)
        sp.dma_start(X[:, 2:4, :], A["ctx"][0].rearrange("(t p) d -> p t d", p=P)).then_inc(S("x_loaded"), 16)
        load_chunks(sp, 0, done1)

    st.close()
    if stop_after == 1:
        with nc.Block() as b:
            @b.sync
            def _(sp):
                sp.dma_start(out[0].rearrange("(t p) d -> p t d", p=P), X[:, 0:2, :]).then_inc(S("stored"), 16)
                sp.wait_ge(S("stored"), 16)
        ctx.close()
        return

    st = ExitStack()
    NM, MD = 4, 4 * HEAD_DIM
    Q2 = R[:, 0:3072].rearrange("p (j t) -> p j t", j=12)
    K2 = R[:, 3072:5120].rearrange("p (j t) -> p j t", j=8)
    V2 = R[:, 5120:7168].rearrange("p (j t) -> p j t", j=8)
    O2 = R[:, 7168:9216].rearrange("p (j t) -> p j t", j=8)
    U2 = sb(st, "U2", [P, FT, SEQ])
    stage2 = sb(st, "stage2", [P, P])
    cols2 = sb(st, "cols2", [P, P])
    FN = sb(st, "FN", [P, D])
    causal = sb(st, "causal", [P, 2, SEQ])
    dilated = sb(st, "dilated", [P, 2, 3, SEQ])
    freqs = sb(st, "freqs", [P, 2])
    pos_i = sb(st, "pos_i", [P, SEQ], I32)
    pos = sb(st, "pos", [P, SEQ])
    turns, angle = U2[:, 0:4, :], U2[:, 4:8, :]
    table = sb(st, "table", [P, 4, SEQ])
    RT = sb(st, "RT", [P, 2, SEQ])
    RL = sb(st, "RL", [P, 2, SEQ])
    WI = sb(st, "WI", [P, 2, IDX_HEADS])
    SC = sb(st, "SC", [P, 2, SEQ])
    TOP = sb(st, "TOP", [P, 2, 8])
    MASK = sb(st, "MASK", [P, 2, SEQ])
    SM = sb(st, "SM", [P, 2, 3 * SEQ])
    ET = sb(st, "ET", [P, 2, 3 * SEQ])
    mz = sb(st, "mz", [P, 2, 4])
    KI = K2[:, 2, :]

    def q_slot(h):
        g = h // 3
        return 64 * (g % 2), (h % 3) + 3 * (g // 2), g

    def attention_units(e):
        us = []
        mem_q, mem_k = (10, 4) if e == 0 else (6, 6)
        for t in range(2):
            for h in range(NM):
                b = 64 * (h % 2)
                part = (Q2[b:b + 64, mem_q + h // 2, t * P:(t + 1) * P], K2[b:b + 64, mem_k + h // 2, :], SEQ)
                c = (768 if e == 0 else 256) + h * 64
                us.append((c, t, [part], [None], [V2[:, 6 + kb, h * 64:(h + 1) * 64] for kb in range(2)]))
        for t in range(2):
            w = (t + 1) * P
            if e == 0:
                for h in range(12):
                    b, j, g = q_slot(h)
                    part = (Q2[b:b + 64, j, t * P:(t + 1) * P], K2[b:b + 64, g // 2, 0:w], w)
                    us.append((h * 64, t, [part], [MASK[:, t, 0:w]], [V2[:, kb, g * 64:(g + 1) * 64] for kb in range(t + 1)]))
            else:
                for h in range(4):
                    b = 64 * (h % 2)
                    parts = [(Q2[b:b + 64, 2 * g + h // 2, t * P:(t + 1) * P], K2[b:b + 64, 2 * g + h // 2, 0:w], w) for g in range(3)]
                    us.append((h * 64, t, parts, [dilated[:, t, g, 0:w] for g in range(3)],
                               [V2[:, 2 * g + kb, h * 64:(h + 1) * 64] for g in range(3) for kb in range(t + 1)]))
        return us

    PROJ = [
        [("qi", 1280, 4, Q2, 6, 2), ("q", 0, 6, Q2, 0, 0), ("k", 768, 2, K2, 0, 0), ("qm", 1864, 2, Q2, 10, None)],
        [("q0", 0, 2, Q2, 0, 0), ("k0", 256, 2, K2, 0, 0), ("q1", 768, 2, Q2, 2, 0), ("k1", 1024, 2, K2, 2, 0),
         ("q2", 1536, 2, Q2, 4, 0), ("k2", 1792, 2, K2, 4, 0), ("qm", 2304, 2, Q2, 6, None)],
    ]
    VALUES = [[("v", 1024, 0)], [("v0", 512, 0), ("v1", 1280, 2), ("v2", 2048, 4)]]
    MEM_K = (4, 6)
    OUT_TILES = (8, 4)

    def pname(e, n):
        return A["l%d_%s_2" % (e, n)]

    def rotations(e):
        r = []
        for nm, _, n, dst, at, tab in PROJ[e]:
            if tab is not None:
                r += [(nm, j, dst[:, at + j, :], tab) for j in range(n)]
            if nm == "qi":
                r.append(("ki", 0, KI, tab))
        return r

    block2 = st.enter_context(nc.Block())

    @block2.tensor
    def _(pe):
        T = Tensor(pe)
        pe.wait_ge(S("norms_loaded"), 16 * 6)
        ps = T.open(("cols2",))
        T.close(pe.transpose(ps[:, 0:P], stage2[:, :], ident[:, :]), ("cols2",))
        own = lambda k, j: HT[:, k, 0:SEQ]
        mem = lambda k, j: HT[:, k, SEQ:2 * SEQ]
        for e in range(DEPTH):
            L = "E%d_" % e
            w_in = pname(e, "w_in")
            norm_pe(T, pe, L + "n1", [0, 1, 2, 3])
            norm_wait(pe, L + "n1", [0, 1, 2, 3])

            def values(name, src, tok, nt):
                i, ws = T.load(src, (KT, MD))
                for t in range(nt):
                    ps = T.open((name, t))
                    for k in range(KT):
                        ins = pe.matmul(ps[:, 0:MD], HT[:, k, tok + t * P:tok + (t + 1) * P], ws[:, k, :], start=(k == 0), stop=(k == KT - 1))
                    T.close(ins, (name, t))
                T.used(i)

            def turn(nm, n, tab, x):
                for j in range(n):
                    rope_pe(T, pe, L + nm, j, x(j), swaps[:, 1 + (tab == 2), :])

            pending = []
            for nm, c0, n, dst, at, tab in PROJ[e]:
                src = None
                if nm == "q":
                    def src(c):
                        heads = []
                        for j in (2 * c, 2 * c + 1):
                            a = (j % 3) + 6 * (j // 3)
                            heads += [a, a + 3]
                        return [rows(w_in, 0, KT, h * 64, 64) for h in heads]
                product_t(T, pe, L + nm, w_in, c0, n, KT, own, SEQ, source=src)
                if nm == "qi":
                    i, ws = T.load(rows(w_in, 0, KT, 1792, 64 + IDX_HEADS), (KT, 64 + IDX_HEADS))
                    ps = T.open((L + "ki", 0))
                    for b in range(2):
                        for k in range(KT):
                            ins = pe.matmul(ps[64 * b:64 * b + 64, 0:SEQ], ws[:, k, 0:64], own(k, 0), start=(k == 0), stop=(k == KT - 1))
                    T.close(ins, (L + "ki", 0))
                    for t in range(2):
                        ps = T.open((L + "wi", t))
                        for k in range(KT):
                            ins = pe.matmul(ps[:, 0:IDX_HEADS], HT[:, k, t * P:(t + 1) * P], ws[:, k, 64:], start=(k == 0), stop=(k == KT - 1))
                        T.close(ins, (L + "wi", t))
                    T.used(i)
                for p in pending:
                    turn(*p)
                pending = []
                if tab is not None:
                    pending.append((nm, n, tab, lambda j, dst=dst, at=at: dst[:, at + j, :]))
                    if nm == "qi":
                        pending.append(("ki", 1, tab, lambda j: KI))
            for nm, c0, _ in VALUES[e]:
                values(L + nm, rows(w_in, 0, KT, c0, MD), 0, 2)
            product_t(T, pe, L + "km", pname(e, "w_mem_kv"), 0, 2, KT, mem, SEQ)
            values(L + "vm", rows(pname(e, "w_mem_kv"), 0, KT, MD, MD), SEQ, 2)
            if e == 0:
                pe.wait_ge(S(L + "qi_roped"), 4)
                pe.wait_ge(S(L + "ki_roped"), 1)
                for t in range(2):
                    for h in range(IDX_HEADS):
                        b = 64 * (h % 2)
                        ps = T.open((L + "is", t, h))
                        T.close(pe.matmul(ps[:, 0:(t + 1) * P], Q2[b:b + 64, 6 + h // 2, t * P:(t + 1) * P], KI[b:b + 64, 0:(t + 1) * P],
                                          start=True, stop=True), (L + "is", t, h))
            us = attention_units(e)
            for nm, _, n, _, _, tab in PROJ[e]:
                if tab is None:
                    for j in range(n):
                        wait_read(pe, (L + nm, j))
                else:
                    pe.wait_ge(S(L + nm + "_roped"), n)
            for j in range(2):
                wait_read(pe, (L + "km", j))
                wait_read(pe, (L + "vm", j))
                for nm, _, _ in VALUES[e]:
                    wait_read(pe, (L + nm, j))
            for i in range(len(us) + 2):
                if i < len(us):
                    _, _, parts, _, _ = us[i]
                    for m, (q, k, w) in enumerate(parts):
                        if m * w % 512 == 0:
                            ps = T.open((L + "s", i, m * w // 512))
                        c = m * w % 512
                        ins = pe.matmul(ps[:, c:c + w], q, k, start=True, stop=True)
                        if m == len(parts) - 1 or (m + 1) * w % 512 == 0:
                            T.close(ins, (L + "s", i, m * w // 512))
                if 1 <= i <= len(us):
                    nb = len(us[i - 1][4])
                    pe.wait_ge(S(L + "exps"), i)
                    for b in range(nb):
                        if b % 4 == 0:
                            ps = T.open((L + "pt", i - 1, b // 4))
                        ins = pe.transpose(ps[:, b % 4 * P:(b % 4 + 1) * P], SM[:, (i - 1) % 2, b * P:(b + 1) * P], ident[:, :])
                        if b == nb - 1 or b % 4 == 3:
                            T.close(ins, (L + "pt", i - 1, b // 4))
                if i >= 2:
                    vs = us[i - 2][4]
                    for b in range(0, len(vs), 4):
                        wait_read(pe, (L + "pt", i - 2, b // 4))
                    ps = T.open((L + "o", i - 2))
                    for b, v in enumerate(vs):
                        ins = pe.matmul(ps[:, 0:64], ET[:, i % 2, b * P:(b + 1) * P], v, start=(b == 0), stop=(b == len(vs) - 1))
                    T.close(ins, (L + "o", i - 2))
            for t in range(2):
                for i, u in enumerate(us):
                    if u[1] == t:
                        wait_read(pe, (L + "o", i))
                for g in range(OUT_TILES[e] // 4):
                    ps = T.open((L + "ot", t, g))
                    for k in range(4):
                        ins = pe.transpose(ps[:, k * P:(k + 1) * P], Y[:, t, (4 * g + k) * P:(4 * g + k + 1) * P], ident[:, :])
                    T.close(ins, (L + "ot", t, g))
            for t in range(2):
                for g in range(OUT_TILES[e] // 4):
                    wait_read(pe, (L + "ot", t, g))
            product(T, pe, L + "y", pname(e, "w_out"), OUT_TILES[e], D, [0, 1], lambda k, t: O2[:, k, t * P:(t + 1) * P])
            ffn_pe(T, pe, L, pname(e, "w_gate_up"), pname(e, "w_down"), [0, 1], SEQ, U2)

    def x2_ready(e, which):
        def wait(eng, t):
            if which == 0 and e == 0:
                eng.wait_ge(S("mem_loaded"), 16)
            elif which == 0 and t >= 2:
                pass
            else:
                name = "E%d_y" % e if which else "E%d_ffn" % (e - 1)
                for nn in range(2):
                    wait_read(eng, (name, nn, t))
        return wait

    def gain2(e, which, mem_which=None):
        def col(k, t):
            c = 24 * e + 8 * (mem_which if mem_which is not None and t >= 2 else which) + k
            return cols2[:, c:c + 1]
        return col

    @block2.scalar
    def _(act):
        act.wait_ge(S("zeroed"), 2)
        for e in range(DEPTH):
            for r, nm in enumerate(("norm_mix", "norm_mem", "norm_ffn")):
                r0 = 24 * e + 8 * r
                act.dma_start(stage2[r0:r0 + 8, :], pname(e, nm).rearrange("(r p) -> r p", p=P)).then_inc(S("norms_loaded"), 16)
        wait_result(act, ("cols2",))
        read_out(act.activation(cols2[:, :], bank(("cols2",))[:, 0:P], ACT.Copy), ("cols2",))
        wait_read(act, ("cols2",))
        act.wait_ge(S("angles"), 4)
        act.activation(table[:], angle[:], ACT.Sin).then_inc(S("tables"), 1)
        for e in range(DEPTH):
            L = "E%d_" % e
            norm_act(act, L + "n1", lambda t: X[:, t, :], [0, 1, 2, 3], h_dst, gain2(e, 0, 1), None, x2_ready(e, 0))

            def copy(key, dst, width, scale=1.0):
                wait_result(act, key)
                read_out(act.activation(dst, bank(key)[:, 0:width], ACT.Copy, scale=scale), key)

            for nm, _, n, dst, at, _ in PROJ[e]:
                for j in range(n):
                    copy((L + nm, j), dst[:, at + j, :], SEQ)
                if nm == "qi":
                    copy((L + "ki", 0), KI, SEQ)
                    for t in range(2):
                        copy((L + "wi", t), WI[:, t, :], IDX_HEADS, IDX_HEADS ** -0.5 * HEAD_DIM ** -0.5)
            for nm, _, at in VALUES[e]:
                for t in range(2):
                    copy((L + nm, t), V2[:, at + t, :], MD)
            for j in range(2):
                copy((L + "km", j), K2[:, MEM_K[e] + j, :], SEQ)
            for t in range(2):
                copy((L + "vm", t), V2[:, 6 + t, :], MD)
            if e == 0:
                for t in range(2):
                    for h in range(IDX_HEADS):
                        key = (L + "is", t, h)
                        i = IDX_HEADS * t + h
                        wait_result(act, key)
                        if i >= 2:
                            act.wait_ge(S("scored"), i - 1)
                        read_out(act.activation(RL[:, i % 2, 0:(t + 1) * P], bank(key)[:, 0:(t + 1) * P], ACT.Relu), key)
            us = attention_units(e)
            for i in range(len(us) + 1):
                if i < len(us):
                    w = P * len(us[i][4])
                    act.wait_ge(S(L + "maxes"), i + 1)
                    if i >= 2:
                        wait_read(act, (L + "o", i - 2))
                    act.activation(SM[:, i % 2, 0:w], SM[:, i % 2, 0:w], ACT.Exp, bias=mz[:, i % 2, 1:2],
                                   accum_out=mz[:, i % 2, 2:3]).then_inc(S(L + "exps"), 1)
                if i >= 1:
                    nb = len(us[i - 1][4])
                    if i >= 3:
                        wait_result(act, (L + "o", i - 3))
                    for b in range(0, nb, 4):
                        key = (L + "pt", i - 1, b // 4)
                        w = P * min(4, nb - b)
                        wait_result(act, key)
                        read_out(act.activation(ET[:, (i - 1) % 2, b * P:b * P + w], bank(key)[:, 0:w], ACT.Copy), key)
            for t in range(2):
                for g in range(OUT_TILES[e] // 4):
                    key = (L + "ot", t, g)
                    wait_result(act, key)
                    read_out(act.activation(O2[:, 4 * g:4 * g + 4, t * P:(t + 1) * P], bank(key).rearrange("p (k t) -> p k t", k=4), ACT.Copy), key)
            norm_act(act, L + "n2", lambda t: X[:, t, :], [0, 1], h_dst, gain2(e, 2), None, x2_ready(e, 1))
            ffn_act(act, L, SEQ, U2)
        c = norm_cols("final")
        for t in range(2):
            x2_ready(2, 0)(act, t)
            act.activation(XN[:, t, :], X[:, t, :], ACT.Square, accum_out=ss[:, c + t:c + t + 1]).then_inc(S("final_squares"), 1)

    @block2.gpsimd
    def _(pool):
        pool.memset(stage2[:], 0.0).then_inc(S("zeroed"), 1)
        pool.dma_start(FN[:, :], A["final_norm_2"].rearrange("(o d) -> o d", o=1).broadcast_to([P, D])).then_inc(S("final_gain"), 16)
        for e in range(DEPTH):
            L = "E%d_" % e
            rstd_pool(pool, L + "n1", [0, 1, 2, 3], D, "_rstd")
            rstd_pool(pool, L + "n2", [0, 1], D, "_rstd")
        rstd_pool(pool, "final", [0, 1], D, "_rstd")

    def add_rows(dve, name):
        for nn in range(2):
            for t in range(2):
                key = (name, nn, t)
                wait_result(dve, key)
                x = X[:, t, nn * 512:(nn + 1) * 512]
                read_out(dve.tensor_tensor(x, x, bank(key), ALU.add), key)

    @block2.vector
    def _(dve):
        TWO_PI_A, TWO_PI_B = 6.28125, 0.0019350051879882812
        TWO_PI_C = 2 * math.pi - TWO_PI_A - TWO_PI_B
        WHOLE = 12582912.0
        dve.wait_ge(S("tables_loaded"), 16 * 5)
        dve_link(dve, dve.tensor_copy(pos[:, :], pos_i[:, :]))
        for r in range(4):
            ahead = 0.25 if r % 2 == 0 else 0.0
            f = freqs[:, r // 2:r // 2 + 1]
            a, k = angle[:, r, :], turns[:, r, :]
            dve_link(dve, dve.tensor_scalar(a, pos[:, :], f, None, ALU.mult))
            dve_link(dve, dve.tensor_scalar(k, a, 0.5 / math.pi, ahead, ALU.mult, ALU.add))
            dve_link(dve, dve.tensor_scalar(k, k, WHOLE, None, ALU.add))
            dve_link(dve, dve.tensor_scalar(k, k, -WHOLE, None, ALU.add))
            for part in (TWO_PI_A, TWO_PI_B, TWO_PI_C):
                dve_link(dve, dve.scalar_tensor_tensor(a, k, -part, a, ALU.mult, ALU.add))
            if r % 2 == 0:
                dve_link(dve, dve.tensor_scalar(a, a, 0.5 * math.pi, None, ALU.add))
            dve.tensor_scalar(a, a, 3.1415925, -3.1415925, ALU.min, ALU.max).then_inc(S("angles"), 1)
        wait_read(dve, ("cols2",))
        for e in range(DEPTH):
            L = "E%d_" % e
            norm_dve(dve, L + "n1", lambda t: X[:, t, :], [0, 1, 2, 3], h_dst, gain2(e, 0, 1), None, x2_ready(e, 0))
            if e == 0:
                dve.wait_ge(S("tables"), 1)
            for n, (nm, j, x, tab) in enumerate(rotations(e)):
                rope_dve(dve, L + nm, j, x, table[:, tab, :], table[:, tab + 1, :], RT[:, n % 2, :])
            if e == 0:
                for t in range(2):
                    w = (t + 1) * P
                    wait_read(dve, (L + "wi", t))
                    for h in range(IDX_HEADS):
                        i = IDX_HEADS * t + h
                        wait_read(dve, (L + "is", t, h))
                        if h == 0:
                            ins = dve.scalar_tensor_tensor(SC[:, t, 0:w], RL[:, i % 2, 0:w], WI[:, t, h:h + 1], causal[:, t, 0:w], ALU.mult, ALU.add)
                        else:
                            dve.wait_ge(S("scored"), i)
                            ins = dve.scalar_tensor_tensor(SC[:, t, 0:w], RL[:, i % 2, 0:w], WI[:, t, h:h + 1], SC[:, t, 0:w], ALU.mult, ALU.add)
                        ins.then_inc(S("scored"), 1)
                    dve.wait_ge(S("scored"), IDX_HEADS * (t + 1))
                for r in range(N_SEL // 8):
                    for t in range(2):
                        w = (t + 1) * P
                        dve_link(dve, dve.max(TOP[:, t, :], SC[:, t, 0:w]))
                    for t in range(2):
                        w = (t + 1) * P
                        dve_link(dve, dve.match_replace(SC[:, t, 0:w], TOP[:, t, :], SC[:, t, 0:w], TAKEN))
                for t in range(2):
                    w = (t + 1) * P
                    dve_link(dve, dve.tensor_scalar(MASK[:, t, 0:w], SC[:, t, 0:w], 0.5 * TAKEN, NEG, ALU.is_gt, ALU.mult))
                    dve_link(dve, dve.tensor_tensor(MASK[:, t, 0:w], MASK[:, t, 0:w], causal[:, t, 0:w], ALU.add))
            us = attention_units(e)

            def maxes(i):
                _, _, parts, masks, _ = us[i]
                if i >= 2:
                    for b in range(0, len(us[i - 2][4]), 4):
                        wait_result(dve, (L + "pt", i - 2, b // 4))
                for m, (_, _, w) in enumerate(parts):
                    key = (L + "s", i, m * w // 512)
                    c = m * w % 512
                    if c == 0:
                        wait_result(dve, key)
                    src, dst = bank(key)[:, c:c + w], SM[:, i % 2, m * w:(m + 1) * w]
                    if masks[m] is None:
                        ins = dve.tensor_scalar(dst, src, SCALE, None, ALU.mult)
                    else:
                        ins = dve.scalar_tensor_tensor(dst, src, SCALE, masks[m], ALU.mult, ALU.add)
                    if m == len(parts) - 1 or (m + 1) * w % 512 == 0:
                        read_out(ins, key)
                        wait_read(dve, key)
                    else:
                        dve_link(dve, ins)
                dve_link(dve, dve.tensor_reduce(mz[:, i % 2, 0:1], SM[:, i % 2, 0:sum(p[2] for p in parts)], AX_X, ALU.max))
                dve.tensor_scalar(mz[:, i % 2, 1:2], mz[:, i % 2, 0:1], -1.0, None, ALU.mult).then_inc(S(L + "maxes"), 1)

            def take_o(i):
                c, t, _, _, _ = us[i]
                key = (L + "o", i)
                wait_result(dve, key)
                dve.wait_ge(S(L + "exps"), i + 1)
                dve_link(dve, dve.reciprocal(mz[:, i % 2, 3:4], mz[:, i % 2, 2:3]))
                read_out(dve.tensor_scalar(Y[:, t, c:c + 64], bank(key)[:, 0:64], mz[:, i % 2, 3:4], None, ALU.mult), key)

            for i in range(len(us) + 2):
                if i >= 2:
                    take_o(i - 2)
                if i < len(us):
                    maxes(i)
            add_rows(dve, L + "y")
            norm_dve(dve, L + "n2", lambda t: X[:, t, :], [0, 1], h_dst, gain2(e, 2), None, x2_ready(e, 1))
            ffn_dve(dve, L, SEQ, U2)
            add_rows(dve, L + "ffn")
        c = norm_cols("final")
        dve.wait_ge(S("final_gain"), 16)
        for t in range(2):
            dve.wait_ge(S("final_rstd"), t + 1)
            dve.scalar_tensor_tensor(Y[:, t, :], X[:, t, :], rstd[:, c + t:c + t + 1], FN[:, :], ALU.mult, ALU.mult).then_inc(S("final"), 1)

    @block2.sync
    def _(sp):
        sp.dma_start(X[:, 2:4, :], A["mem_2"][0].rearrange("(t p) d -> p t d", p=P)).then_inc(S("mem_loaded"), 16)
        sp.dma_start(causal[:], A["causal"].rearrange("t p k -> p t k")).then_inc(S("tables_loaded"), 16)
        for t in range(2):
            sp.dma_start(dilated[:, t, :, :], A["dilated"][t]).then_inc(S("tables_loaded"), 16)
        sp.dma_start(freqs[:], A["freqs"]).then_inc(S("tables_loaded"), 16)
        sp.dma_start(pos_i[:], A["positions_2"][0:1, :].broadcast_to([P, SEQ])).then_inc(S("tables_loaded"), 16)
        load_chunks(sp, done1, len(chunks))
        for t in range(2):
            sp.wait_ge(S("final"), t + 1)
            sp.dma_start(out[0, t * P:(t + 1) * P, :], Y[:, t, :]).then_inc(S("stored"), 16)
        sp.wait_ge(S("stored"), 32)

    st.close()
    ctx.close()


def kernel(**inputs):
    import numpy as _np
    import concourse.bacc as _bacc
    from concourse import mybir as _mybir
    from concourse.bass_utils import run_bass_kernel_spmd as _run

    nc = _bacc.Bacc("TRN2", target_bir_lowering=False, num_devices=1)
    arrays, args = {}, {}
    for name, a in list(inputs.items()) + list(shape_constants().items()):
        a = _np.ascontiguousarray(a)
        arrays[f"in_{name}_dram"] = a
        args[name] = nc.dram_tensor(f"in_{name}_dram", a.shape, _mybir.dt.from_np(a.dtype), kind="ExternalInput").ap()
    out = nc.dram_tensor("out_0_dram", (1, SEQ, D), F32, kind="ExternalOutput").ap()
    build(nc, args, out, STOP)
    r = _run(nc, [arrays], core_ids=[0])
    return r.results[0]["out_0_dram"]


STOP = 9
```

```python
from contextlib import ExitStack
import math

import numpy as np

import concourse.bass as bass
from concourse import mybir

F32 = mybir.dt.float32
F32R = mybir.dt.float32r
I32 = mybir.dt.int32
ALU = mybir.AluOpType
ACT = mybir.ActivationFunctionType
AX_X = mybir.AxisListType.X

P = 128
D = 1024
KT = D // P
SEQ = 256
DEPTH = 2
GRID_W = 64
EPS = 1e-6
CONV_CH, CONV_W = 512, 31
HALF_W = CONV_W // 2
HEADS, HEAD_DIM, V_DIM = 8, 64, 128
POOL_CH = 512
POOL_PAD = 8
NCH = CONV_CH // P
D_FF = 2816
FT = D_FF // P
COL_Q = 2 * CONV_CH
COL_K = COL_Q + 1024
COL_V = COL_K + 1024
COL_P = COL_V + 1024
COL_G = COL_P + POOL_CH
NEG = -1e30
TAKEN = -3e38
N_SEL = 64
IDX_HEADS = 8
SCALE = HEAD_DIM ** -0.5
BANKS = 8
SLOT = 1024
RAW = (3, 5)
SPLIT = (3, 4)
AHEAD = 2

ROW_PRE, ROW_FFN, ROW_GATE = 0, 8, 16
ROW_CB, ROW_LG, ROW_LB, ROW_PS, ROW_SUB, ROW_C, ROW_CC = 40, 44, 48, 52, 56, 57, 65
N_ROWS = 73


def shape_constants():
    f = np.float32
    d = np.arange(P)
    t = np.arange(SEQ)
    inv = f(10000.0) ** (-np.arange(0, 32, 2, dtype=f) / f(32))
    pos = np.where((d % 64 < 32)[:, None], (t // GRID_W)[None, :], (t % GRID_W)[None, :]).astype(f)
    ang = pos * inv[d % 16][:, None]

    def swap(half, rot):
        m = np.zeros((P, P), f)
        for i in range(P):
            r = i % 64
            if r % rot < half and r < (64 if rot == 32 and half == 16 else rot):
                m[i + half, i] = -1
            elif r < (64 if rot == 32 and half == 16 else rot):
                m[i - half, i] = 1
        return m

    idx_swap = swap(16, 32)
    idx_swap[:, d % 64 >= 32] = 0
    counts = np.zeros((4, SEQ), f)
    for g, w in enumerate((2, 4, 8, 16)):
        counts[g] = 1 / (np.clip(t + w // 2, 0, SEQ) - np.clip(t - w // 2, 0, SEQ)).astype(f)
    q = np.arange(SEQ)
    causal = np.where(q[None, :] <= q[:, None], 0, NEG).astype(f)
    dil = np.stack([np.where((q[None, :] <= q[:, None]) & ((q[:, None] - q[None, :]) % r == 0)
                             & ((q[:, None] - q[None, :]) // r <= P), 0, NEG).astype(f)
                    for r in (1, 4, 16)], 1)
    freq = f(10000.0) ** (-np.arange(32, dtype=f) / f(32))
    ifreq = f(10000.0) ** (-np.arange(16, dtype=f) / f(16))
    freqs = np.stack([freq[d % 32], np.where(d % 64 < 32, ifreq[d % 16], 0).astype(f)], 1)
    sel = np.zeros((4, 2, P), f)
    sel[0, 0] = sel[1, 1] = sel[2, 0] = sel[3, 1] = 1
    return {
        "ident": np.eye(P, dtype=f), "swaps": np.stack([swap(16, 32), swap(32, 64), idx_swap], 1),
        "grid_rope": np.stack([np.cos(ang), np.sin(ang)], 1).astype(f),
        "inv_counts": np.ascontiguousarray(np.broadcast_to(counts, (P, 4, SEQ))),
        "causal": causal.reshape(2, P, SEQ), "dilated": dil.reshape(2, P, 3, SEQ),
        "freqs": freqs, "pick": sel,
    }


def build(nc, A, out, stop_after=9):
    ctx = ExitStack()
    sems = {}

    def S(name):
        if name not in sems:
            sems[name] = ctx.enter_context(nc.semaphore(name))
        return sems[name]

    place = [(nc.sbuf_base + 31) // 32 * 32]

    def sb(name, shape, dt=F32):
        t = nc.alloc_sbuf_tensor_at(name, shape, dt, offset=place[0])
        place[0] += (4 * math.prod(shape[1:]) + 31) // 32 * 32
        assert place[0] <= nc.sbuf_usable_end, (name, place[0])
        return t

    def over(offset, name, shape, dt=F32):
        assert offset + 4 * math.prod(shape[1:]) <= nc.sbuf_usable_end, name
        return nc.alloc_sbuf_tensor_at(name, shape, dt, offset=offset)

    PS = ctx.enter_context(nc.psum_tensor("PS", [P, BANKS, 512], F32))
    pe_done, act_step, dve_step, pool_step = S("pe_done"), S("act_step"), S("dve_step"), S("pool_step")
    high_done, low_done = S("high_done"), S("low_done")
    bank_read = [S(f"bank_read{b}") for b in range(BANKS)]
    slot_full = [S(f"slot_full{s}") for s in range(max(RAW))]
    uses, milestones, bank_no = {}, {}, [0, 0]
    chunks, loads = [], [0] * max(RAW)
    splits, chunk_of = [], {}
    now = {"block": 0, "chunk0": 0, "split0": 0, "act": 0, "dve": 0}
    count = {"act": 0, "dve": 0, "pool": 0}

    X = sb("X", [P, 4, D])
    XN = sb("XN", [P, 2, D])
    at_h = place[0]
    HH = sb("HH", [P, KT, 2 * SEQ], F32R)
    HL = sb("HL", [P, KT, 2 * SEQ], F32R)
    YY = over(at_h, "YY", [P, 4, D])
    ident = sb("ident", [P, P])
    swaps = sb("swaps", [P, 3, P])
    ones = sb("ones", [P, P])
    half = sb("half", [P, 8])
    ss = sb("ss", [P, 64])
    ms = sb("ms", [P, 64])
    rstd = sb("rstd", [P, 64])
    common_end = place[0]

    def weight_rings(b):
        return ([sb("raw%d_%d" % (b, i), [P, SLOT]) for i in range(RAW[b])],
                [sb("split%d_%d" % (b, i), [P, 2, SLOT], F32R) for i in range(SPLIT[b])])

    rings = [weight_rings(0)]
    stat_col = {}


    def bank(key):
        return PS[:, uses[key] % BANKS, :]

    def wait_result(eng, key):
        keep_splitting(eng, key)
        eng.wait_ge(pe_done, milestones[key])

    def read_out(ins, key):
        ins.then_inc(bank_read[uses[key] % BANKS], 1)

    def wait_read(eng, key):
        keep_splitting(eng, key)
        eng.wait_ge(bank_read[uses[key] % BANKS], uses[key] // BANKS + 1)

    class Tensor:

        def __init__(self, pe):
            self.pe = pe

        def open(self, key):
            u = uses[key] = bank_no[0]
            bank_no[0] += 1
            if u >= BANKS:
                self.pe.wait_ge(bank_read[u % BANKS], u // BANKS)
            return PS[:, u % BANKS, :]

        def close(self, ins, key):
            bank_no[1] += 1
            milestones[key] = bank_no[1]
            chunk_of[key] = len(chunks) - 1
            ins.then_inc(pe_done, 1)

        def mark(self, ins):
            bank_no[1] += 1
            ins.then_inc(pe_done, 1)

        def load(self, src, shape, split=True):
            i = len(chunks)
            b = now["block"]
            s = (i - now["chunk0"]) % RAW[b]
            pieces = src if isinstance(src, list) else [src]
            loads[s] += 16 * len(pieces)
            c = {"pieces": pieces, "shape": shape, "slot": s, "raw": view(rings[b][0][s][:, :], shape), "full": loads[s],
                 "free": None, "split": None}
            chunks.append(c)
            if not split:
                self.pe.wait_ge(slot_full[s], loads[s])
                return c, c["raw"]
            k = c["split"] = len(splits)
            two = rings[b][1][(k - now["split0"]) % SPLIT[b]]
            c["high"], c["low"] = view(two[:, 0, :], shape), view(two[:, 1, :], shape)
            splits.append(c)
            self.pe.wait_ge(low_done, k + 1)
            return c, (c["high"], c["low"])

        def used(self, c):
            c["free"] = bank_no[1]

    def view(t, shape):
        a, b = shape
        return t[:, 0:a * b].rearrange("p (a b) -> p a b", a=a)

    def rows(w, k0, nk, c0, nc_):
        return w[k0 * P:(k0 + nk) * P, c0:c0 + nc_].rearrange("(k p) c -> p k c", p=P)

    def keep_splitting(eng, key):
        if eng is nc.scalar or eng is nc.vector:
            split_until(eng, chunk_of[key] + AHEAD)

    def split_until(eng, last):
        who = "act" if eng is nc.scalar else "dve"
        b = now["block"]
        while now[who] < len(splits) and chunks.index(splits[now[who]]) <= last:
            k = now[who]
            c = splits[k]
            now[who] = k + 1
            if who == "act":
                eng.wait_ge(slot_full[c["slot"]], c["full"])
                if k - SPLIT[b] >= now["split0"]:
                    eng.wait_ge(pe_done, splits[k - SPLIT[b]]["free"])
                eng.activation(c["high"], c["raw"], ACT.Copy).then_inc(high_done, 1)
            else:
                eng.wait_ge(high_done, k + 1)
                eng.tensor_tensor(c["low"], c["raw"], c["high"].bitcast(F32), ALU.subtract).then_inc(low_done, 1)

    def split_value(dve, high, low, value):
        dve_link(dve, dve.tensor_copy(high, value))
        return dve.tensor_tensor(low, value, high.bitcast(F32), ALU.subtract)


    def multiply(pe, out, a, b, first, last):
        pe.matmul(out, a[0], b[0], start=first, stop=False)
        pe.matmul(out, a[0], b[1], start=False, stop=False)
        return pe.matmul(out, a[1], b[0], start=False, stop=last)

    def cut2(pair, *index):
        return pair[0][index], pair[1][index]

    def tile_t(T, pe, key, ws, kts, c, rhs, n):
        ps = T.open(key)
        for k in range(kts):
            ins = multiply(pe, ps[:, 0:n], cut2(ws, slice(None), k, slice(c * P, (c + 1) * P)), rhs(k), k == 0, k == kts - 1)
        T.close(ins, key)

    def product_t(T, pe, name, w, c0, tiles, kts, rhs, n, source=None, before=None):
        per = SLOT // kts // P
        for j in range(tiles):
            if j % per == 0:
                src = source(j) if source else rows(w, 0, kts, c0 + j * P, per * P)
                i, ws = T.load(src, (kts, per * P))
            if before:
                before(j)
            tile_t(T, pe, (name, j), ws, kts, j % per, rhs, n)
            if j % per == per - 1:
                T.used(i)

    def product(T, pe, name, w, kts, cols, tiles, lhs, before=None):
        width = min(512, cols)
        step = SLOT // width
        for n in range(cols // width):
            ps = {}
            for k0 in range(0, kts, step):
                i, ws = T.load(rows(w, k0, step, n * width, width), (step, width))
                if k0 == 0:
                    for t in tiles:
                        ps[t] = T.open((name, n, t))
                for k in range(k0, k0 + step):
                    if before and n == 0:
                        before(k)
                    for t in tiles:
                        ins = multiply(pe, ps[t][:, 0:width], lhs(k, t), cut2(ws, slice(None), k - k0), k == 0, k == kts - 1)
                        if k == kts - 1:
                            T.close(ins, (name, n, t))
                if k0 + step < kts:
                    T.mark(ins)
                T.used(i)


    def norm_cols(name):
        if name not in stat_col:
            stat_col[name] = 4 * (len(stat_col) % 16)
        return stat_col[name]

    def norm_act(act, name, src, tiles, hf, scale, bias, ready):
        c = norm_cols(name)
        for n, t in enumerate(tiles):
            ready(act, t)
            if n >= 2:
                wait_result(act, (name, tiles[n - 2], 1))
            act.activation(XN[:, n % 2, :], src(t), ACT.Square,
                           accum_out=ss[:, c + n:c + n + 1]).then_inc(S(name + "_squares"), 1)
            if n >= 1:
                if n >= 2:
                    act.wait_ge(S(name + "_parts"), 2 * (n - 2) + 1)
                columns(act, name, tiles[n - 1], 0, hf, scale, bias)
        if len(tiles) >= 2:
            act.wait_ge(S(name + "_parts"), 2 * (len(tiles) - 2) + 1)
        columns(act, name, tiles[-1], 0, hf, scale, bias)

    def columns(eng, name, t, g, hf, scale, bias):
        key = (name, t, g)
        wait_result(eng, key)
        for k in range(4 * g, 4 * g + 4):
            src = bank(key)[:, (k % 4) * P:(k % 4 + 1) * P]
            dst = hf[:, g, (k % 4) * P:(k % 4 + 1) * P]
            if eng is nc.scalar:
                ins = eng.activation(dst, src, ACT.Identity, scale=scale(k, t), bias=bias(k, t) if bias else 0.0)
            elif bias:
                ins = eng.tensor_scalar(dst, src, scale(k, t), bias(k, t), ALU.mult, ALU.add)
            else:
                ins = eng.tensor_scalar(dst, src, scale(k, t), None, ALU.mult)
        read_out(ins, key)

    def rstd_pool(pool, name, tiles, width, sem):
        c = norm_cols(name)
        for n, t in enumerate(tiles):
            pool.wait_ge(S(name + "_squares"), n + 1)
            pool.tensor_scalar(ms[:, c + n:c + n + 1], ss[:, c + n:c + n + 1], 1.0 / width, EPS, ALU.mult,
                               ALU.add).then_inc(pool_step, 1)
            count["pool"] += 1
            pool.wait_ge(pool_step, count["pool"])
            pool.tensor_tensor(rstd[:, c + n:c + n + 1], ms[:, c + n:c + n + 1], half[:, 0:1],
                               ALU.pow).then_inc(S(name + sem), 1)

    def norm_dve(dve, name, src, tiles, hf, scale, bias, ready):
        c = norm_cols(name)

        def parts(n, t):
            if n:
                dve.wait_ge(S(name + "_parts"), 2 * n)
            columns(dve, name, t, 1, hf, scale, bias)
            for g in range(2):
                wait_read(dve, (name, t, g))
                to = (slice(None), slice(4 * g, 4 * g + 4), slice(t * P, (t + 1) * P))
                split_value(dve, HH[to], HL[to], hf[:, g, :].rearrange("p (k c) -> p k c", k=4)).then_inc(S(name + "_parts"), 1)

        for n, t in enumerate(tiles):
            ready(dve, t)
            dve.wait_ge(S(name + "_rstd"), n + 1)
            dve.tensor_scalar(XN[:, n % 2, :], src(t), rstd[:, c + n:c + n + 1], None,
                              ALU.mult).then_inc(S(name + "_xn"), 1)
            if n >= 1:
                parts(n - 1, tiles[n - 1])
        parts(len(tiles) - 1, tiles[-1])

    def norm_pe(T, pe, name, tiles):
        for n, t in enumerate(tiles):
            pe.wait_ge(S(name + "_xn"), n + 1)
            transposes(T, pe, name, t, XN[:, n % 2, :])

    def transposes(T, pe, name, t, src):
        for g in range(2):
            ps = T.open((name, t, g))
            for k in range(4):
                c = (4 * g + k) * P
                ins = pe.transpose(ps[:, k * P:(k + 1) * P], src[:, c:c + P], ident[:, :])
            T.close(ins, (name, t, g))

    def norm_wait(eng, name, tiles):
        eng.wait_ge(S(name + "_parts"), 2 * len(tiles))

    def dve_link(dve, ins):
        count["dve"] += 1
        ins.then_inc(dve_step, 1)
        dve.wait_ge(dve_step, count["dve"])

    def act_link(act, ins):
        count["act"] += 1
        ins.then_inc(act_step, 1)
        act.wait_ge(act_step, count["act"])


    def rope_pe(T, pe, name, j, x, swap):
        wait_read(pe, (name, j))
        ps = T.open((name + "_rot", j))
        T.close(pe.matmul(ps[:, 0:SEQ], swap, x, start=True, stop=True), (name + "_rot", j))

    def rope_dve(dve, name, j, x, cos, sin, tmp):
        key = (name + "_rot", j)
        wait_result(dve, key)
        read_out(dve.tensor_tensor(tmp, bank(key)[:, 0:SEQ], sin, ALU.mult), key)
        wait_read(dve, key)
        dve_link(dve, dve.tensor_tensor(x, x, cos, ALU.mult))
        dve.tensor_tensor(x, x, tmp, ALU.add).then_inc(S(name + "_roped"), 1)

    grid_cols = sb("cols", [P, 2, 2, P])
    cols = grid_cols
    G = sb("G", [P, 2, D])
    pick = sb("pick", [4, 2, P])
    silu_f = sb("silu_f", [P, KT, 2])
    silu_c = sb("silu_c", [P, KT, 4], F32R)
    mod = sb("mod", [P, 4, KT, 2])
    gain = sb("gain", [P, 2, KT, 2])
    sub_g = sb("sub_g", [P, 2])
    lams = sb("lams", [P, 2, 8])
    mx = sb("mx", [P, 2, 8])
    subs = sb("subs", [P, 3, 4, 8])
    hidden_at = place[0]
    at_q = place[0]
    QT = sb("QT", [P, 8, 2 * SEQ])
    at_k = place[0]
    KTT = sb("KTT", [P, 8, 2 * SEQ])
    at_v = place[0]
    V = sb("V", [P, 4, D])
    at_o = place[0]
    O = over(at_o, "O", [P, 4, D])
    place[0] += 2 * D * 4
    UP = sb("UP", [P, NCH, 2, SEQ + 2 * HALF_W])
    CV = sb("CV", [P, NCH, 2, SEQ])
    PP = sb("PP", [P, 4, 2, SEQ + 2 * POOL_PAD])
    at_tmp = place[0]
    TMP = sb("TMP", [P, 4096])
    MT = over(at_q, "MT", [P, KT, 2 * SEQ])
    MTL = over(at_q, "MTL", [P, KT, 2 * SEQ], F32R)
    MTH = over(at_o, "MTH", [P, KT, 2 * SEQ], F32R)
    OTH = over(at_k, "OTH", [P, KT, 2 * SEQ], F32R)
    OTL = over(at_v, "OTL", [P, KT, 2 * SEQ], F32R)
    MIX = [over(at_k + 8192 * i, "MIX%d" % i, [P, 4, 2 * SEQ], F32R) for i in range(2)]
    CS = [over(at_v + 8192 * i, "CS%d" % i, [P, NCH, 2 * SEQ], F32R) for i in range(2)]
    UH = over(hidden_at, "UH", [P, FT, 2 * SEQ], F32R)
    UL = over(hidden_at + FT * 2 * SEQ * 4, "UL", [P, FT, 2 * SEQ], F32R)
    UT = over(hidden_at + 2 * FT * 2 * SEQ * 4, "UT", [P, 2, 2, 2 * SEQ])
    PT = XN[:, :, 0:2 * (SEQ + 2 * POOL_PAD)].rearrange("p b (s t) -> p b s t", s=2)
    GP = TMP[:, 1024:2048]
    MR = TMP[0:4, 2048:3072].rearrange("p (b k) -> p b k", b=2)
    BM = TMP[0:2, 3072:4096].rearrange("p (b k) -> p b k", b=2)
    stage = TMP[:, 0:512].rearrange("p (l m k) -> p l m k", l=2, m=2)
    lamv = TMP[:, 512:1024].rearrange("p (l m k) -> p l m k", l=2, m=4)
    HF = TMP[:, 0:1024].rearrange("p (b k) -> p b k", b=2)
    SG = TMP[:, 0:1024].rearrange("p (b k) -> p b k", b=2)
    E2 = TMP[:, 0:2048].rearrange("p (b i k) -> p b i k", b=2, i=2)
    GY = TMP[:, 1024:2048].rearrange("p (b k) -> p b k", b=2)
    rope_tmp = TMP[:, 2048:2560].rearrange("p (b k) -> p b k", b=2)
    grid = TMP[:, 2560:3072].rearrange("p (b k) -> p b k", b=2)
    AA = TMP[:, 2048:3072].rearrange("p (b k) -> p b k", b=2)
    OF = TMP[:, 3072:4096].rearrange("p (b k) -> p b k", b=2)
    AT = TMP[:, 3072:4096].rearrange("p (b k) -> p b k", b=2)
    counts = TMP[:, 3072:4096].rearrange("p (g k) -> p g k", g=4)

    def both(pair, n):
        return lambda k: (pair[0][:, k, 0:n], pair[1][:, k, 0:n])

    def lefts(pair):
        return lambda k, t: (pair[0][:, k, t * P:(t + 1) * P], pair[1][:, k, t * P:(t + 1) * P])

    def first_rows(l):
        v = lambda n: A[n][l].rearrange("(r p) -> r p", p=P)
        lst = [(ROW_PRE, v("g_pre_mix")), (ROW_FFN, v("g_pre_ffn")), (ROW_GATE, v("b_gate")), (ROW_CB, v("conv_b")),
               (ROW_LG, v("conv_ln_g")), (ROW_LB, v("conv_ln_b")), (ROW_PS, v("pool_scale")), (ROW_SUB, v("subln_g")),
               (ROW_C, A["c"][0].rearrange("(r p) -> r p", p=P)), (ROW_CC, A["c_ctx"].rearrange("(r p) -> r p", p=P))]
        return lst

    def section(l, s):
        return "L%d_mod%d" % (l, s)

    SECTIONS = ((0, "col", 0), (1, "col", 1), (2, "row", 0), (3, "col", 2), (4, "col", 3), (5, "row", 1))

    def layer_tokens(l):
        ns = 2 if l < DEPTH - 1 else 1
        return ns, ns * SEQ, list(range(2 * ns))

    units_of = {l: [(t, h) for t in layer_tokens(l)[2] for h in range(HEADS)] for l in range(DEPTH)}

    def ffn_pe(T, pe, L, w_up, w_down, tiles, n, U):
        norm_pe(T, pe, L + "n2", tiles)
        norm_wait(pe, L + "n2", tiles)
        for j in range(FT):
            for nm, c0 in (("ffn_gate", 0), ("ffn_up", D_FF)):
                i, ws = T.load(rows(w_up, 0, KT, c0 + j * P, P), (KT, P))
                tile_t(T, pe, (L + nm, j), ws, KT, 0, both((HH, HL), n), n)
                T.used(i)
        product(T, pe, L + "ffn", w_down, FT, D, tiles, lefts(U), before=lambda k: pe.wait_ge(S(L + "hidden"), k + 1))

    def ffn_act(act, L, n, tmp):
        for j in range(FT):
            key = (L + "ffn_gate", j)
            wait_result(act, key)
            if j >= 2:
                wait_read(act, (L + "ffn_up", j - 2))
            read_out(act.activation(tmp[:, 0, j % 2, 0:n], bank(key)[:, 0:n], ACT.Silu), key)

    def ffn_dve(dve, L, n, tmp, U):
        for j in range(FT):
            key = (L + "ffn_up", j)
            wait_read(dve, (L + "ffn_gate", j))
            wait_result(dve, key)
            value = tmp[:, 1, j % 2, 0:n]
            if j >= 2:
                dve.wait_ge(S(L + "hidden"), j - 1)
            read_out(dve.tensor_tensor(value, tmp[:, 0, j % 2, 0:n], bank(key)[:, 0:n], ALU.mult), key)
            wait_read(dve, key)
            split_value(dve, U[0][:, j, 0:n], U[1][:, j, 0:n], value).then_inc(S(L + "hidden"), 1)

    def post_act(act, L, name, tiles):
        c = norm_cols(L + name)
        for nn in range(2):
            for n, t in enumerate(tiles):
                key = (L + name, nn, t)
                wait_result(act, key)
                read_out(act.activation(YY[:, t, nn * 512:(nn + 1) * 512], bank(key), ACT.Copy), key)
                if nn == 1:
                    wait_read(act, key)
                    act.activation(XN[:, n % 2, :], YY[:, t, :], ACT.Square,
                                   accum_out=ss[:, c + n:c + n + 1]).then_inc(S(L + name + "_squares"), 1)

    def post_dve(dve, L, name, tiles, which):
        c = norm_cols(L + name)
        for s in range(2):
            for nn in range(2):
                if s * 2 in tiles:
                    wait_read(dve, ("L%s_mod_turn" % L[1], 2 + 3 * which, nn, s))
        for n, t in enumerate(tiles):
            wait_result(dve, (L + name, 1, t))
            dve.wait_ge(S(L + name + "_rstd"), n + 1)
            dve_link(dve, dve.scalar_tensor_tensor(YY[:, t, :], YY[:, t, :], rstd[:, c + n:c + n + 1], G[:, t // 2, :], ALU.mult, ALU.mult))
            dve.tensor_tensor(X[:, t, :], X[:, t, :], YY[:, t, :], ALU.add).then_inc(S(L + name + "_added"), 1)

    def x_ready(l, which):
        def wait(eng, t):
            if which == 0 and l == 0:
                eng.wait_ge(S("x_loaded"), 16 * 2)
            else:
                eng.wait_ge(S(("L%d_ffn_added" % (l - 1)) if which == 0 else "L%d_y_added" % l), t + 1)
        return wait

    st = ExitStack()
    block1 = st.enter_context(nc.Block())

    @block1.tensor
    def _(pe):
        T = Tensor(pe)

        def modulation(l, part):
            name = "L%d_mod" % l
            lst = SECTIONS[3 * part:3 * part + 3]
            todo = []

            def turn(s, kind, n):
                wait_read(pe, (name, s, n))
                row = MR[:, n % 2, :]
                if kind == "col":
                    ps = T.open((name + "_turn", s, n))
                    for k in range(4):
                        ins = pe.matmul(ps[:, 2 * k:2 * k + 2], row[:, k * P:(k + 1) * P], pick[:, 0:2, 0], start=True, stop=True)
                    T.close(ins, (name + "_turn", s, n))
                else:
                    for m in range(2):
                        ps = T.open((name + "_turn", s, n, m))
                        T.close(pe.matmul(ps, pick[:, m, :], row, start=True, stop=True), (name + "_turn", s, n, m))

            for s, kind, _ in lst:
                for n in range(2):
                    for k0 in range(0, KT, 2):
                        i, ws = T.load(rows(A["w_mod"][l], k0, 2, s * D + n * 512, 512), (2, 512))
                        if k0 == 0:
                            ps = T.open((name, s, n))
                        for k in range(2):
                            for part in range(2):
                                ins = pe.matmul(ps[0:4, :], silu_c[:, k0 + k, :], ws[part][:, k, :],
                                                start=(k0 + k + part == 0), stop=(k0 + k + part == KT))
                        if k0 < KT - 2:
                            T.mark(ins)
                        else:
                            T.close(ins, (name, s, n))
                        T.used(i)
                    todo.append((s, kind, n))
                    if len(todo) > 1:
                        turn(*todo.pop(0))
            turn(*todo.pop(0))

        pe.wait_ge(S("consts"), 16 * 3)
        for l in range(DEPTH):
            for m in range(2):
                if m == 0:
                    pe.wait_ge(S("params%d" % l), 16 * 11)
                ps = T.open(("cols", l, m))
                T.close(pe.transpose(ps[:, 0:P], stage[:, l, m, :], ident[:, :]), ("cols", l, m))
        pe.wait_ge(S("silu_c"), 1)
        modulation(0, 0)
        for l in range(DEPTH):
            ns, n, tiles = layer_tokens(l)
            L = "L%d_" % l
            if l:
                modulation(l, 0)
            norm_pe(T, pe, L + "n1", [0, 1, 2, 3])
            norm_wait(pe, L + "n1", [0, 1, 2, 3])
            w_in = A["w_in"][l]
            own = both((HH, HL), n)
            for j in range(NCH):
                for nm, c0 in (("glu_gate", CONV_CH), ("glu", 0)):
                    i, ws = T.load(rows(w_in, 0, KT, c0 + j * P, P), (KT, P))
                    tile_t(T, pe, (L + nm, j), ws, KT, 0, own, n)
                    T.used(i)
            product_t(T, pe, L + "pool", w_in, COL_P, 4, KT, own, n)

            def turn_q(j):
                if j >= 1:
                    rope_pe(T, pe, L + "q", j - 1, QT[:, j - 1, 0:SEQ], swaps[:, 0, :])

            def turn_k(j):
                if j == 0:
                    rope_pe(T, pe, L + "q", 7, QT[:, 7, 0:SEQ], swaps[:, 0, :])
                else:
                    rope_pe(T, pe, L + "k", j - 1, KTT[:, j - 1, 0:SEQ], swaps[:, 0, :])

            product_t(T, pe, L + "q", w_in, COL_Q, 8, KT, own, n, before=turn_q)
            product_t(T, pe, L + "k", w_in, COL_K, 8, KT, both((HH, HL), 2 * SEQ), 2 * SEQ, before=turn_k)
            rope_pe(T, pe, L + "k", 7, KTT[:, 7, 0:SEQ], swaps[:, 0, :])
            product(T, pe, L + "v", w_in[:, COL_V:COL_P], KT, D, [0, 1, 2, 3], lefts((HH, HL)))
            pe.wait_ge(S(L + "conv"), NCH)
            ps = T.open((L + "mean",))
            for j in range(NCH):
                ins = pe.matmul(ps[:, 0:n], ones[:, :], CV[:, j, 0:ns, :], start=(j == 0), stop=(j == NCH - 1))
            T.close(ins, (L + "mean",))
            us = units_of[l]
            pe.wait_ge(S(L + "q_roped"), 8)
            pe.wait_ge(S(L + "k_roped"), 8)
            for j in range(4, 8):
                wait_read(pe, (L + "k", j))
            for t in range(4):
                wait_read(pe, (L + "v", 1, t))
                wait_read(pe, (L + "v", 0, t))

            def blocks(t):
                return [0, 1, 2, 3] if t < 2 else [2, 3]

            for i in range(len(us) + 3):
                if i < len(us):
                    t, h = us[i]
                    k0, k1 = (0, 2 * SEQ) if t < 2 else (SEQ, 2 * SEQ)
                    for m in range(2):
                        ps = T.open((L + "s", i, m))
                        T.close(pe.matmul(ps[:, 0:k1 - k0], QT[64 * m:64 * m + 64, h, t * P:(t + 1) * P],
                                          KTT[64 * m:64 * m + 64, h, k0:k1], start=True, stop=True), (L + "s", i, m))
                if i == 1:
                    pe.wait_ge(S(L + "conv_sq"), NCH)
                    ps = T.open((L + "var",))
                    for j in range(NCH):
                        ins = pe.matmul(ps[:, 0:n], ones[:, :], UP[:, j, 0:ns, HALF_W:HALF_W + SEQ], start=(j == 0), stop=(j == NCH - 1))
                    T.close(ins, (L + "var",))
                if 2 <= i < len(us) + 2:
                    t, h = us[i - 2]
                    pe.wait_ge(S(L + "probs"), i - 1)
                    ps = T.open((L + "pt", i - 2))
                    for b in range(len(blocks(t))):
                        ins = pe.transpose(ps[:, b * P:(b + 1) * P], AA[:, i % 2, b * P:(b + 1) * P], ident[:, :])
                    T.close(ins, (L + "pt", i - 2))
                if i >= 3:
                    t, h = us[i - 3]
                    wait_read(pe, (L + "pt", i - 3))
                    ps = T.open((L + "o", i - 3))
                    for b, kb in enumerate(blocks(t)):
                        ins = pe.matmul(ps[:, 0:V_DIM], AT[:, (i - 3) % 2, b * P:(b + 1) * P], V[:, kb, h * V_DIM:(h + 1) * V_DIM],
                                        start=(b == 0), stop=(b == len(blocks(t)) - 1))
                    T.close(ins, (L + "o", i - 3))
            pe.wait_ge(S(L + "pooled"), 4)
            i, ws = T.load(A["w_pool_group"][l].rearrange("g c d -> c g d"), (4, P), split=False)
            for g in range(4):
                ps = T.open((L + "mixed", g))
                ins = pe.matmul(ps[:, 0:n], ws[:, g, :], PP[:, g, 0:ns, POOL_PAD:POOL_PAD + SEQ], start=True, stop=True)
                T.close(ins, (L + "mixed", g))
            T.used(i)

            def branch(name, gate_col, w, kts, pair, ready):
                per = SLOT // kts // P
                for j in range(KT):
                    i, ws = T.load(rows(w_in, 0, KT, COL_G + gate_col * D + j * P, P), (KT, P))
                    tile_t(T, pe, (name + "_gate", j), ws, KT, 0, own, n)
                    T.used(i)
                    if j == 0:
                        ready()
                    if j % per == 0:
                        iy, wy = T.load(rows(w, 0, kts, j * P, per * P), (kts, per * P))
                    tile_t(T, pe, (name, j), wy, kts, j % per, both(pair, n), n)
                    if j % per == per - 1:
                        T.used(iy)

            branch(L + "yc", 2, A["w_pool_out"][l], 4, MIX, lambda: pe.wait_ge(S(L + "mixed_parts"), 4))
            branch(L + "ya", 0, A["w_conv_out"][l], 4, CS, lambda: pe.wait_ge(S(L + "conv_parts"), NCH))
            for t in tiles:
                pe.wait_ge(S(L + "o_normed"), t + 1)
                transposes(T, pe, L + "ot", t, O[:, t, :])
            branch(L + "yb", 1, A["w_attn_out"][l], 8, (OTH, OTL), lambda: pe.wait_ge(S(L + "ot_parts"), 2 * len(tiles)))
            pe.wait_ge(S(L + "merged"), KT)
            product(T, pe, L + "y", A["w_out"][l], KT, D, tiles, lefts((MTH, MTL)))
            modulation(l, 1)
            ffn_pe(T, pe, L, A["w_ffn_in"][l], A["w_ffn_out"][l], tiles, n, (UH, UL))

    @block1.scalar
    def _(act):
        act.wait_ge(S("zeroed"), 1)
        for l in range(DEPTH):
            for r, src in first_rows(l):
                act.dma_start(stage[r:r + src.shape[0], l, 0, :], src).then_inc(S("params%d" % l), 16)
            act.dma_start(stage[0:CONV_W * NCH, l, 1, :], A["conv_w"][l].rearrange("t (j p) -> (t j) p", p=P)).then_inc(S("params%d" % l), 16)

        def modulation(l, part):
            name = "L%d_mod" % l
            for s, kind, at in SECTIONS[3 * part:3 * part + 3]:
                for n in range(2):
                    key = (name + "_turn", s, n)
                    if kind == "col":
                        wait_result(act, key)
                        src = bank(key)[:, 0:8].rearrange("p (k m) -> p k m", m=2)
                        read_out(act.activation(mod[:, at, 4 * n:4 * n + 4, :], src, ACT.Copy), key)

        for l in range(DEPTH):
            for m in range(2):
                wait_result(act, ("cols", l, m))
                read_out(act.activation(cols[:, l, m, :], bank(("cols", l, m))[:, 0:P], ACT.Copy), ("cols", l, m))
        wait_read(act, ("cols", 0, 0))
        act.activation(silu_f[:, :, :].rearrange("p k m -> p m k"), cols[:, 0, 0, ROW_C:ROW_C + 16].rearrange("p (m k) -> p m k", m=2),
                       ACT.Silu).then_inc(S("silu_f"), 1)
        for l in range(DEPTH):
            act.wait_ge(S("lam_sums"), l + 1)
            act.activation(lams[:, l, 2:4], lams[:, l, 0:2], ACT.Exp).then_inc(S("lam_exps"), 1)
        modulation(0, 0)
        for l in range(DEPTH):
            ns, n, tiles = layer_tokens(l)
            L = "L%d_" % l
            if l:
                modulation(l, 0)
            keep_splitting(act, (L + "mod_turn", 2, 1, 1))
            act.wait_ge(S(L + "gains"), 1)
            norm_act(act, L + "n1", lambda t: X[:, t, :], [0, 1, 2, 3], HF, lambda k, t: gain[:, 0, k, t // 2:t // 2 + 1],
                     lambda k, t: mod[:, 0, k, t // 2:t // 2 + 1], x_ready(l, 0))
            for j in range(NCH):
                key = (L + "glu_gate", j)
                wait_result(act, key)
                if j >= 2:
                    wait_read(act, (L + "glu", j - 2))
                read_out(act.activation(SG[:, j % 2, 0:n], bank(key)[:, 0:n], ACT.Sigmoid), key)
            for j in range(4):
                key = (L + "pool", j)
                wait_result(act, key)
                read_out(act.activation(PP[:, j, 0:ns, POOL_PAD:POOL_PAD + SEQ], bank(key)[:, 0:n].rearrange("p (s t) -> p s t", s=ns), ACT.Copy), key)
            for nm, dst, w in (("q", QT, n), ("k", KTT, 2 * SEQ)):
                for j in range(8):
                    key = (L + nm, j)
                    wait_result(act, key)
                    read_out(act.activation(dst[:, j, 0:w], bank(key)[:, 0:w], ACT.Copy), key)
            for nn in range(2):
                for t in range(4):
                    key = (L + "v", nn, t)
                    wait_result(act, key)
                    read_out(act.activation(V[:, t, nn * 512:(nn + 1) * 512], bank(key), ACT.Copy), key)
            us = units_of[l]
            for i in range(len(us) + 2):
                if i < len(us):
                    t, h = us[i]
                    w = 2 * SEQ if t < 2 else SEQ
                    act.wait_ge(S(L + "maxes"), i + 1)
                    if i >= 2:
                        act.wait_ge(S(L + "probs"), i - 1)
                    for m in range(2):
                        key = (L + "s", i, m)
                        read_out(act.activation(E2[:, i % 2, m, 0:w], bank(key)[:, 0:w], ACT.Exp, bias=mx[:, i % 2, 2 + m:3 + m],
                                                scale=SCALE, accum_out=mx[:, i % 2, 4 + m:5 + m]), key)
                if i >= 2:
                    w = 2 * SEQ if us[i - 2][0] < 2 else SEQ
                    key = (L + "pt", i - 2)
                    wait_result(act, key)
                    if i >= 4:
                        wait_result(act, (L + "o", i - 4))
                    read_out(act.activation(AT[:, i % 2, 0:w], bank(key)[:, 0:w], ACT.Copy), key)
            wait_read(act, (L + "var",))
            act.activation(XN[:, 0, 0:n], XN[:, 0, 0:n], ACT.Sqrt).then_inc(S(L + "std"), 1)
            for j in range(NCH):
                act.wait_ge(S(L + "conv_normed"), j + 1)
                act.activation(CV[:, j, 0:ns, :], CV[:, j, 0:ns, :], ACT.Silu, scale=cols[:, l, 0, ROW_LG + j:ROW_LG + j + 1],
                               bias=cols[:, l, 0, ROW_LB + j:ROW_LB + j + 1]).then_inc(S(L + "conv_act"), 1)
            for g in range(4):
                key = (L + "mixed", g)
                wait_result(act, key)
                read_out(act.activation(PP[:, g, 0:ns, POOL_PAD:POOL_PAD + SEQ], bank(key)[:, 0:n].rearrange("p (s t) -> p s t", s=ns), ACT.Copy,
                                        scale=cols[:, l, 0, ROW_PS + g:ROW_PS + g + 1]), key)
            done = 0
            for nm, gc in (("yc", 2), ("ya", 0), ("yb", 1)):
                if nm == "yb":
                    for t in tiles:
                        for g in range(2):
                            key = (L + "ot", t, g)
                            wait_result(act, key)
                            if t:
                                act.wait_ge(S(L + "ot_parts"), 2 * t - 1 + g)
                            read_out(act.activation(OF[:, g, :], bank(key), ACT.Copy, scale=sub_g[:, l:l + 1]), key)
                for j in range(KT):
                    key = (L + nm + "_gate", j)
                    wait_result(act, key)
                    if done >= 2:
                        wait_read(act, (L + ("yc", "ya", "yb")[(done - 2) // KT], (done - 2) % KT))
                    c = ROW_GATE + 8 * gc + j
                    read_out(act.activation(SG[:, done % 2, 0:n], bank(key)[:, 0:n], ACT.Sigmoid, bias=cols[:, l, 0, c:c + 1]), key)
                    done += 1
            post_act(act, L, "y", tiles)
            modulation(l, 1)
            keep_splitting(act, (L + "mod_turn", 5, 1, 1))
            act.wait_ge(S(L + "gains"), 2)
            norm_act(act, L + "n2", lambda t: X[:, t, :], tiles, HF, lambda k, t: gain[:, 1, k, t // 2:t // 2 + 1],
                     lambda k, t: mod[:, 2, k, t // 2:t // 2 + 1], x_ready(l, 1))
            ffn_act(act, L, n, UT)
            post_act(act, L, "ffn", tiles)

    @block1.gpsimd
    def _(pool):
        pool.memset(TMP[:, 0:512], 0.0).then_inc(S("zeroed"), 1)
        pool.memset(ones[:], 1.0).then_inc(S("filled"), 1)
        pool.memset(half[:], -0.5).then_inc(S("filled"), 1)
        pool.memset(UP[:], 0.0).then_inc(S("filled"), 1)
        pool.memset(PP[:], 0.0).then_inc(S("filled"), 1)
        pool.wait_ge(S("filled"), 4)
        pool.wait_ge(S("zeroed"), 1)

        def bias_rows(l, part):
            for s, _, _ in SECTIONS[3 * part:3 * part + 3]:
                for n in range(2):
                    i = 12 * l + 2 * s + n
                    if i >= 2:
                        l2, s2 = (i - 2) // 12, ((i - 2) % 12) // 2
                        wait_read(pool, ("L%d_mod" % l2, s2, n))
                    src = A["b_mod"][l:l + 1, s * D + n * 512:s * D + (n + 1) * 512].broadcast_to([2, 512])
                    pool.dma_start(BM[:, n, :], src).then_inc(S("bias_row%d" % n), 16)

        def gain_row(l, part):
            if l or part:
                l2, s2 = (l, 2) if part else (l - 1, 5)
                for n in range(2):
                    for m in range(2):
                        wait_read(pool, ("L%d_mod_turn" % l2, s2, n, m))
            src = A["g_post_ffn" if part else "g_post_mix"][l:l + 1, :].broadcast_to([P, D])
            pool.dma_start(GP[:, :], src).then_inc(S("gain_row"), 16)

        gain_row(0, 0)
        bias_rows(0, 0)
        for l in range(DEPTH):
            ns, n, tiles = layer_tokens(l)
            L = "L%d_" % l
            if l:
                wait_result(pool, ("L%d_ffn" % (l - 1), 1, layer_tokens(l - 1)[2][-1]))
                pool.memset(UP[:], 0.0).then_inc(S("filled"), 1)
                pool.memset(PP[:], 0.0).then_inc(S("filled"), 1)
                gain_row(l, 0)
                bias_rows(l, 0)
            for n in range(2):
                for m in range(2):
                    wait_read(pool, (L + "mod_turn", 2, n, m))
            pool.dma_start(grid, A["grid_rope"]).then_inc(S("grid_loaded"), 16)
            pool.dma_start(counts, A["inv_counts"]).then_inc(S("counts_loaded"), 16)
            rstd_pool(pool, L + "n1", [0, 1, 2, 3], D, "_rstd")
            pool.wait_ge(S("counts_loaded"), 16 * (l + 1))
            pool.wait_ge(S("filled"), 4 + 2 * l)
            for g in range(4):
                wait_read(pool, (L + "pool", g))
                if g:
                    pool.wait_ge(S(L + "pooled"), g)
                src = PP[:, g, 0:ns, :]
                lo, hi, off = 0, SEQ + 2 * POOL_PAD, 1
                for step in range(g + 1):
                    dst = PT[:, step % 2, 0:ns, :]
                    a, b = (1, 0) if step == 0 else (2 ** (step - 1), 2 ** (step - 1))
                    lo, hi = lo + a, hi - b
                    pool.tensor_tensor(dst[:, :, lo:hi], src[:, :, lo - a:hi - a], src[:, :, lo + b:hi + b], ALU.add).then_inc(pool_step, 1)
                    count["pool"] += 1
                    pool.wait_ge(pool_step, count["pool"])
                    src = dst
                mid = PT[:, g % 2, 0:ns, POOL_PAD:POOL_PAD + SEQ]
                inside = PP[:, g, 0:ns, POOL_PAD:POOL_PAD + SEQ]
                for s in range(ns):
                    pool.tensor_tensor(mid[:, s, :], mid[:, s, :], counts[:, g, :], ALU.mult).then_inc(pool_step, 1)
                    count["pool"] += 1
                pool.wait_ge(pool_step, count["pool"])
                pool.tensor_tensor(inside, mid, inside, ALU.subtract).then_inc(S(L + "pooled"), 1)
            for t in tiles:
                pool.wait_ge(S(L + "o_squares"), t + 1)
                pool.tensor_tensor(subs[:, 2, t, :], subs[:, 1, t, :], half[:, 0:8], ALU.pow).then_inc(S(L + "o_rstd"), 1)
            rstd_pool(pool, L + "y", tiles, D, "_rstd")
            pool.wait_ge(S(L + "merged"), KT)
            gain_row(l, 1)
            bias_rows(l, 1)
            rstd_pool(pool, L + "n2", tiles, D, "_rstd")
            rstd_pool(pool, L + "ffn", tiles, D, "_rstd")

    @block1.vector
    def _(dve):
        def modulation(l, part):
            name = "L%d_mod" % l
            lst = SECTIONS[3 * part:3 * part + 3]
            todo = []

            def gates(s, n):
                for m in range(2):
                    key = (name + "_turn", s, n, m)
                    wait_result(dve, key)
                    ins = dve.tensor_tensor(G[:, m, n * 512:(n + 1) * 512], bank(key), GP[:, n * 512:(n + 1) * 512], ALU.mult)
                    read_out(ins, key)

            for s, kind, at in lst:
                for n in range(2):
                    i = 12 * l + 2 * s + n
                    key = (name, s, n)
                    wait_result(dve, key)
                    dve.wait_ge(S("bias_row%d" % n), 16 * (i // 2 + 1))
                    if i >= 2:
                        l2, s2, n2 = (i - 2) // 12, ((i - 2) % 12) // 2, i % 2
                        kind2 = SECTIONS[s2][1]
                        wait_result(dve, ("L%d_mod_turn" % l2, s2, n2) + ((1,) if kind2 == "row" else ()))
                    dve_link(dve, dve.tensor_copy(MR[:, n, :], bank(key)[0:4, :]))
                    read_out(dve.tensor_tensor(MR[0:2, n, :], MR[0:2, n, :], BM[:, n, :], ALU.add), key)
                    if kind == "row" and n == 1:
                        dve.wait_ge(S("gain_row"), 16 * (2 * l + part + 1))
                        gates(s, 0)
            gates(lst[-1][0], 1)
            for n in range(2):
                wait_read(dve, (name + "_turn", 1 + 3 * part, n))
            for m in range(2):
                ins = dve.scalar_tensor_tensor(gain[:, part, :, m], mod[:, 1 + 2 * part, :, m], 1.0,
                                               cols[:, l, 0, (ROW_FFN if part else ROW_PRE):(ROW_FFN if part else ROW_PRE) + KT], ALU.add, ALU.mult)
                if m == 0:
                    dve_link(dve, ins)
            ins.then_inc(S("L%d_gains" % l), 1)

        dve.wait_ge(S("filled"), 4)
        dve.wait_ge(S("consts"), 16 * 3)
        dve.wait_ge(S("lam_loaded"), 16 * 8)
        for l in range(DEPTH):
            for m in range(2):
                dve_link(dve, dve.tensor_tensor(lamv[:, l, 2 * m, :], lamv[:, l, 2 * m, :], lamv[:, l, 2 * m + 1, :], ALU.mult))
            dve.tensor_reduce(lams[:, l, 0:2], lamv[:, l, 0:4:2, :], AX_X, ALU.add).then_inc(S("lam_sums"), 1)
        for l in range(DEPTH):
            lam_init = 0.8 - 0.6 * math.exp(-0.3 * l)
            dve.wait_ge(S("lam_exps"), l + 1)
            dve_link(dve, dve.tensor_tensor(lams[:, l, 4:5], lams[:, l, 3:4], lams[:, l, 2:3], ALU.subtract))
            dve_link(dve, dve.tensor_scalar(lams[:, l, 5:6], lams[:, l, 4:5], -lam_init, None, ALU.add))
            wait_read(dve, ("cols", l, 0))
            dve_link(dve, dve.tensor_scalar(sub_g[:, l:l + 1], cols[:, l, 0, ROW_SUB:ROW_SUB + 1], 1.0 - lam_init, None, ALU.mult))
            wait_read(dve, ("cols", l, 1))
        dve.wait_ge(S("silu_f"), 1)
        split_value(dve, silu_c[:, :, 0:2], silu_c[:, :, 2:4], silu_f[:, :, :]).then_inc(S("silu_c"), 1)
        modulation(0, 0)
        for l in range(DEPTH):
            ns, n, tiles = layer_tokens(l)
            L = "L%d_" % l
            if l:
                modulation(l, 0)
            norm_dve(dve, L + "n1", lambda t: X[:, t, :], [0, 1, 2, 3], HF, lambda k, t: gain[:, 0, k, t // 2:t // 2 + 1],
                     lambda k, t: mod[:, 0, k, t // 2:t // 2 + 1], x_ready(l, 0))
            dve.wait_ge(S("filled"), 4 + 2 * l)
            dve.wait_ge(S("grid_loaded"), 16 * (l + 1))
            for j in range(NCH):
                key = (L + "glu", j)
                wait_read(dve, (L + "glu_gate", j))
                wait_result(dve, key)
                read_out(dve.tensor_tensor(UP[:, j, 0:ns, HALF_W:HALF_W + SEQ], bank(key)[:, 0:n].rearrange("p (s t) -> p s t", s=ns),
                                           SG[:, j % 2, 0:n].rearrange("p (s t) -> p s t", s=ns), ALU.mult), key)
            for j in range(NCH):
                wait_read(dve, (L + "glu", j))
            ropes = [("q", j) for j in range(8)] + [("k", j) for j in range(8)]
            last = [0] * NCH
            for tap in range(CONV_W):
                for j in range(NCH):
                    wt = cols[:, l, 1, tap * NCH + j:tap * NCH + j + 1]
                    src = UP[:, j, 0:ns, tap:tap + SEQ]
                    if tap == 0:
                        ins = dve.tensor_scalar(CV[:, j, 0:ns, :], src, wt, cols[:, l, 0, ROW_CB + j:ROW_CB + j + 1], ALU.mult, ALU.add)
                    else:
                        dve.wait_ge(dve_step, last[j])
                        ins = dve.scalar_tensor_tensor(CV[:, j, 0:ns, :], src, wt, CV[:, j, 0:ns, :], ALU.mult, ALU.add)
                    if tap < CONV_W - 1:
                        count["dve"] += 1
                        last[j] = count["dve"]
                        ins.then_inc(dve_step, 1)
                    else:
                        ins.then_inc(S(L + "conv"), 1)
                if tap % 2 == 1 and ropes:
                    nm, j = ropes.pop(0)
                    x = (QT if nm == "q" else KTT)[:, j, 0:SEQ]
                    rope_dve(dve, L + nm, j, x, grid[:, 0, :], grid[:, 1, :], rope_tmp[:, j % 2, :])
            for nm, j in ropes:
                x = (QT if nm == "q" else KTT)[:, j, 0:SEQ]
                rope_dve(dve, L + nm, j, x, grid[:, 0, :], grid[:, 1, :], rope_tmp[:, j % 2, :])
            key = (L + "mean",)
            wait_result(dve, key)
            dve.wait_ge(S(L + "pooled"), 4)
            dve_link(dve, dve.tensor_scalar(XN[:, 0, 0:n], bank(key)[:, 0:n], -1.0 / CONV_CH, None, ALU.mult))
            for j in range(NCH):
                ins = dve.tensor_tensor(CV[:, j, 0:ns, :], CV[:, j, 0:ns, :], XN[:, 0, 0:n].rearrange("p (s t) -> p s t", s=ns), ALU.add)
                if j == NCH - 1:
                    read_out(ins, key)
                    wait_read(dve, key)
                else:
                    dve_link(dve, ins)
            for j in range(NCH):
                dve.tensor_tensor(UP[:, j, 0:ns, HALF_W:HALF_W + SEQ], CV[:, j, 0:ns, :], CV[:, j, 0:ns, :], ALU.mult).then_inc(S(L + "conv_sq"), 1)
            us = units_of[l]

            def maxes(i):
                t, h = us[i]
                w = 2 * SEQ if t < 2 else SEQ
                for m in range(2):
                    wait_result(dve, (L + "s", i, m))
                    ins = dve.tensor_reduce(mx[:, i % 2, m:m + 1], bank((L + "s", i, m))[:, 0:w], AX_X, ALU.max)
                dve_link(dve, ins)
                dve.tensor_scalar(mx[:, i % 2, 2:4], mx[:, i % 2, 0:2], -SCALE, None, ALU.mult).then_inc(S(L + "maxes"), 1)

            def probs(i):
                w = 2 * SEQ if us[i][0] < 2 else SEQ
                for m in range(2):
                    wait_read(dve, (L + "s", i, m))
                dve_link(dve, dve.reciprocal(mx[:, i % 2, 6:8], mx[:, i % 2, 4:6]))
                dve_link(dve, dve.tensor_scalar(mx[:, i % 2, 7:8], mx[:, i % 2, 7:8], lams[:, l, 5:6], None, ALU.mult))
                if i >= 2:
                    wait_result(dve, (L + "pt", i - 2))
                dve_link(dve, dve.tensor_scalar(AA[:, i % 2, 0:w], E2[:, i % 2, 0, 0:w], mx[:, i % 2, 6:7], None, ALU.mult))
                dve.scalar_tensor_tensor(AA[:, i % 2, 0:w], E2[:, i % 2, 1, 0:w], mx[:, i % 2, 7:8], AA[:, i % 2, 0:w],
                                         ALU.mult, ALU.add).then_inc(S(L + "probs"), 1)

            def take_o(i):
                t, h = us[i]
                key = (L + "o", i)
                wait_result(dve, key)
                read_out(dve.tensor_copy(O[:, t, h * V_DIM:(h + 1) * V_DIM], bank(key)[:, 0:V_DIM]), key)

            for i in range(len(us) + 4):
                if i < len(us):
                    maxes(i)
                if i == 2:
                    key = (L + "var",)
                    wait_result(dve, key)
                    read_out(dve.tensor_scalar(XN[:, 0, 0:n], bank(key)[:, 0:n], 1.0 / CONV_CH, EPS, ALU.mult, ALU.add), key)
                if 1 <= i <= len(us):
                    probs(i - 1)
                if i >= 4:
                    take_o(i - 4)
            dve.wait_ge(S(L + "std"), 1)
            dve_link(dve, dve.reciprocal(XN[:, 1, 0:n], XN[:, 0, 0:n]))
            for j in range(NCH):
                dve.tensor_tensor(CV[:, j, 0:ns, :], CV[:, j, 0:ns, :], XN[:, 1, 0:n].rearrange("p (s t) -> p s t", s=ns),
                                  ALU.mult).then_inc(S(L + "conv_normed"), 1)
            for j in range(NCH):
                dve.wait_ge(S(L + "conv_act"), j + 1)
                flat = lambda v: v.rearrange("p (s t) -> p s t", s=ns)
                split_value(dve, flat(CS[0][:, j, 0:n]), flat(CS[1][:, j, 0:n]), CV[:, j, 0:ns, :]).then_inc(S(L + "conv_parts"), 1)
            for g in range(4):
                wait_read(dve, (L + "mixed", g))
                split_value(dve, flat(MIX[0][:, g, 0:n]), flat(MIX[1][:, g, 0:n]),
                            PP[:, g, 0:ns, POOL_PAD:POOL_PAD + SEQ]).then_inc(S(L + "mixed_parts"), 1)
            sq = TMP[:, 2048:3072]
            for t in tiles:
                for h in range(HEADS):
                    i = t * HEADS + h
                    wait_read(dve, (L + "o", i))
                dve_link(dve, dve.tensor_tensor(sq, O[:, t, :], O[:, t, :], ALU.mult))
                dve_link(dve, dve.tensor_reduce(subs[:, 0, t, :], sq.rearrange("p (h d) -> p h d", h=HEADS), AX_X, ALU.add))
                dve.tensor_scalar(subs[:, 1, t, :], subs[:, 0, t, :], 1.0 / V_DIM, EPS, ALU.mult, ALU.add).then_inc(S(L + "o_squares"), 1)
                dve.wait_ge(S(L + "o_rstd"), t + 1)
                yv = O[:, t, :].rearrange("p (h d) -> p h d", h=HEADS)
                dve.tensor_tensor(yv, yv, subs[:, 2, t, :].rearrange("p (h o) -> p h o", o=1).broadcast_to([P, HEADS, V_DIM]),
                                  ALU.mult).then_inc(S(L + "o_normed"), 1)
            done = 0
            for nm in ("yc", "ya", "yb"):
                if nm == "yb":
                    for t in tiles:
                        for g in range(2):
                            wait_read(dve, (L + "ot", t, g))
                            to = (slice(None), slice(4 * g, 4 * g + 4), slice(t * P, (t + 1) * P))
                            split_value(dve, OTH[to], OTL[to], OF[:, g, :].rearrange("p (k c) -> p k c", k=4)).then_inc(S(L + "ot_parts"), 1)
                for j in range(KT):
                    key = (L + nm, j)
                    wait_result(dve, key)
                    wait_read(dve, (L + nm + "_gate", j))
                    if nm == "yc":
                        read_out(dve.tensor_tensor(MT[:, j, 0:n], bank(key)[:, 0:n], SG[:, done % 2, 0:n], ALU.mult), key)
                    else:
                        read_out(dve.tensor_tensor(GY[:, done % 2, 0:n], bank(key)[:, 0:n], SG[:, done % 2, 0:n], ALU.mult), key)
                        wait_read(dve, key)
                        wait_read(dve, (L + "yc", j))
                        dve_link(dve, dve.tensor_tensor(MT[:, j, 0:n], MT[:, j, 0:n], GY[:, done % 2, 0:n], ALU.add))
                    if nm == "yb":
                        split_value(dve, MTH[:, j, 0:n], MTL[:, j, 0:n], MT[:, j, 0:n]).then_inc(S(L + "merged"), 1)
                    done += 1
            post_dve(dve, L, "y", tiles, 0)
            modulation(l, 1)
            norm_dve(dve, L + "n2", lambda t: X[:, t, :], tiles, HF, lambda k, t: gain[:, 1, k, t // 2:t // 2 + 1],
                     lambda k, t: mod[:, 2, k, t // 2:t // 2 + 1], x_ready(l, 1))
            ffn_dve(dve, L, n, UT, (UH, UL))
            post_dve(dve, L, "ffn", tiles, 1)

    def load_chunks(sp, first):
        for i in range(first, len(chunks)):
            c = chunks[i]
            if i - RAW[now["block"]] >= first:
                before = chunks[i - RAW[now["block"]]]
                if before["split"] is None:
                    sp.wait_ge(pe_done, before["free"])
                else:
                    sp.wait_ge(low_done, before["split"] + 1)
            w = c["shape"][1] // len(c["pieces"])
            for m, piece in enumerate(c["pieces"]):
                sp.dma_start(c["raw"][:, :, m * w:(m + 1) * w], piece).then_inc(slot_full[c["slot"]], 16)

    @block1.sync
    def _(sp):
        sp.dma_start(ident[:, :], A["ident"]).then_inc(S("consts"), 16)
        sp.dma_start(swaps[:], A["swaps"]).then_inc(S("consts"), 16)
        sp.dma_start(pick[:], A["pick"]).then_inc(S("consts"), 16)
        for l in range(DEPTH):
            for m, v in enumerate(("lam_q1", "lam_k1", "lam_q2", "lam_k2")):
                sp.dma_start(lamv[:, l, m, :], A[v][l:l + 1, :].broadcast_to([P, 64])).then_inc(S("lam_loaded"), 16)
        sp.dma_start(X[:, 0:2, :], A["x"][0].rearrange("(t p) d -> p t d", p=P)).then_inc(S("x_loaded"), 16)
        sp.dma_start(X[:, 2:4, :], A["ctx"][0].rearrange("(t p) d -> p t d", p=P)).then_inc(S("x_loaded"), 16)
        load_chunks(sp, 0)

    st.close()
    if stop_after == 1:
        with nc.Block() as b:
            @b.sync
            def _(sp):
                sp.dma_start(out[0].rearrange("(t p) d -> p t d", p=P), X[:, 0:2, :]).then_inc(S("stored"), 16)
                sp.wait_ge(S("stored"), 16)
        ctx.close()
        return

    now.update(block=1, chunk0=len(chunks), split0=len(splits))
    place[0] = common_end
    rings.append(weight_rings(1))
    NM, MD = 4, 4 * HEAD_DIM
    cols2 = sb("cols2", [P, P])
    FN = sb("FN", [P, D])
    causal = sb("causal", [P, 2, SEQ])
    dilated = sb("dilated", [P, 2, 3, SEQ])
    freqs = sb("freqs", [P, 2])
    table = sb("table", [P, 4, SEQ])
    RL = sb("RL", [P, 2, SEQ])
    WI = sb("WI", [P, 2, IDX_HEADS])
    SC = sb("SC", [P, 2, SEQ])
    TOP = sb("TOP", [P, 2, 8])
    MASK = sb("MASK", [P, 2, SEQ])
    UT2 = over(place[0], "UT2", [P, 2, 2, SEQ])
    RT = over(place[0], "RT", [P, 2, SEQ])
    SM = sb("SM", [P, 3, 3 * SEQ])
    ET = sb("ET", [P, 2, 3 * SEQ])
    mz = sb("mz", [P, 6, 4])
    HF2 = sb("HF2", [P, 2, 512])
    UH2 = over(place[0], "UH2", [P, FT, SEQ], F32R)
    UL2 = over(place[0] + FT * SEQ * 4, "UL2", [P, FT, SEQ], F32R)
    Q2 = sb("Q2", [P, 12, SEQ])
    K2 = sb("K2", [P, 8, SEQ])
    V2 = sb("V2", [P, 8, SEQ])
    stage2 = over(place[0], "stage2", [P, P])
    angle = over(place[0] + 4 * P, "angle", [P, 4, SEQ])
    turns = over(place[0] + 4 * P + 16 * SEQ, "turns", [P, 4, SEQ])
    pos_i = over(place[0] + 4 * P + 32 * SEQ, "pos_i", [P, SEQ], I32)
    pos = over(place[0] + 4 * P + 36 * SEQ, "pos", [P, SEQ])
    Y = sb("Y", [P, 2, D])
    O2H = sb("O2H", [P, 8, SEQ], F32R)
    O2L = sb("O2L", [P, 8, SEQ], F32R)
    KI = K2[:, 2, :]

    def q_slot(h):
        g = h // 3
        return 64 * (g % 2), (h % 3) + 3 * (g // 2), g

    def attention_units(e):
        us = []
        mem_q, mem_k = (10, 4) if e == 0 else (6, 6)
        for t in range(2):
            for h in range(NM):
                b = 64 * (h % 2)
                part = (Q2[b:b + 64, mem_q + h // 2, t * P:(t + 1) * P], K2[b:b + 64, mem_k + h // 2, :], SEQ)
                c = (768 if e == 0 else 256) + h * 64
                us.append((c, t, [part], [None], [V2[:, 6 + kb, h * 64:(h + 1) * 64] for kb in range(2)]))
        for t in range(2):
            w = (t + 1) * P
            if e == 0:
                for h in range(12):
                    b, j, g = q_slot(h)
                    part = (Q2[b:b + 64, j, t * P:(t + 1) * P], K2[b:b + 64, g // 2, 0:w], w)
                    us.append((h * 64, t, [part], [MASK[:, t, 0:w]], [V2[:, kb, g * 64:(g + 1) * 64] for kb in range(t + 1)]))
            else:
                for h in range(4):
                    b = 64 * (h % 2)
                    parts = [(Q2[b:b + 64, 2 * g + h // 2, t * P:(t + 1) * P], K2[b:b + 64, 2 * g + h // 2, 0:w], w) for g in range(3)]
                    us.append((h * 64, t, parts, [dilated[:, t, g, 0:w] for g in range(3)],
                               [V2[:, 2 * g + kb, h * 64:(h + 1) * 64] for g in range(3) for kb in range(t + 1)]))
        return us

    PROJ = [
        [("qi", 1280, 4, Q2, 6, 2), ("ki", 1792, 1, K2, 2, 2), ("q", 0, 6, Q2, 0, 0), ("k", 768, 2, K2, 0, 0), ("qm", 1864, 2, Q2, 10, None)],
        [("q0", 0, 2, Q2, 0, 0), ("k0", 256, 2, K2, 0, 0), ("q1", 768, 2, Q2, 2, 0), ("k1", 1024, 2, K2, 2, 0),
         ("q2", 1536, 2, Q2, 4, 0), ("k2", 1792, 2, K2, 4, 0), ("qm", 2304, 2, Q2, 6, None)],
    ]
    VALUES = [[("v", 1024, 0)], [("v0", 512, 0), ("v1", 1280, 2), ("v2", 2048, 4)]]
    MEM_K = (4, 6)
    OUT_TILES = (8, 4)

    def pname(e, n):
        return A["l%d_%s_2" % (e, n)]

    def rotations(e):
        r = []
        for nm, _, n, dst, at, tab in PROJ[e]:
            if tab is not None:
                r += [(nm, j, dst[:, at + j, :], tab) for j in range(n)]
        return r

    st = ExitStack()
    block2 = st.enter_context(nc.Block())

    @block2.tensor
    def _(pe):
        T = Tensor(pe)
        pe.wait_ge(S("norms_loaded"), 16 * 6)
        ps = T.open(("cols2",))
        T.close(pe.transpose(ps[:, 0:P], stage2[:, :], ident[:, :]), ("cols2",))
        own = both((HH, HL), SEQ)
        mem = lambda k: (HH[:, k, SEQ:2 * SEQ], HL[:, k, SEQ:2 * SEQ])
        for e in range(DEPTH):
            L = "E%d_" % e
            w_in = pname(e, "w_in")
            norm_pe(T, pe, L + "n1", [0, 1, 2, 3])
            norm_wait(pe, L + "n1", [0, 1, 2, 3])

            def pieces(nm):
                def of(j):
                    if nm == "ki":
                        return [rows(w_in, 0, KT, 1792, 64)] * 2
                    a = (j % 3) + 6 * (j // 3)
                    return [rows(w_in, 0, KT, h * 64, 64) for h in (a, a + 3)]
                return of if nm in ("ki", "q") else None

            pending = []
            for nm, c0, n, dst, at, tab in PROJ[e]:
                product_t(T, pe, L + nm, w_in, c0, n, KT, own, SEQ, source=pieces(nm))
                if nm == "ki":
                    i, ws = T.load(rows(w_in, 0, KT, 1856, IDX_HEADS), (KT, IDX_HEADS))
                    for t in range(2):
                        ps = T.open((L + "wi", t))
                        for k in range(KT):
                            ins = multiply(pe, ps[:, 0:IDX_HEADS], lefts((HH, HL))(k, t), cut2(ws, slice(None), k), k == 0, k == KT - 1)
                        T.close(ins, (L + "wi", t))
                    T.used(i)
                for pn, pn_n, pdst, pat, ptab in pending:
                    for j in range(pn_n):
                        rope_pe(T, pe, L + pn, j, pdst[:, pat + j, :], swaps[:, 1 + (ptab == 2), :])
                pending = [] if tab is None else [(nm, n, dst, at, tab)]
            for nm, c0, _ in VALUES[e]:
                product(T, pe, L + nm, w_in[:, c0:c0 + MD], KT, MD, [0, 1], lefts((HH, HL)))
            product_t(T, pe, L + "km", pname(e, "w_mem_kv"), 0, 2, KT, mem, SEQ)
            product(T, pe, L + "vm", pname(e, "w_mem_kv")[:, MD:2 * MD], KT, MD, [2, 3], lefts((HH, HL)))
            if e == 0:
                pe.wait_ge(S(L + "qi_roped"), 4)
                pe.wait_ge(S(L + "ki_roped"), 1)
                for t in range(2):
                    for h in range(IDX_HEADS):
                        b = 64 * (h % 2)
                        ps = T.open((L + "is", t, h))
                        T.close(pe.matmul(ps[:, 0:(t + 1) * P], Q2[b:b + 64, 6 + h // 2, t * P:(t + 1) * P], KI[b:b + 64, 0:(t + 1) * P],
                                          start=True, stop=True), (L + "is", t, h))
            us = attention_units(e)
            for nm, _, n, _, _, tab in PROJ[e]:
                if tab is None:
                    for j in range(n):
                        wait_read(pe, (L + nm, j))
                else:
                    pe.wait_ge(S(L + nm + "_roped"), n)
            for j in range(2):
                wait_read(pe, (L + "km", j))
                wait_read(pe, (L + "vm", 0, 2 + j))
                for nm, _, _ in VALUES[e]:
                    wait_read(pe, (L + nm, 0, j))
            for i in range(len(us) + 3):
                if i < len(us):
                    _, _, parts, _, _ = us[i]
                    for m, (q, k, w) in enumerate(parts):
                        if m * w % 512 == 0:
                            ps = T.open((L + "s", i, m * w // 512))
                        c = m * w % 512
                        ins = pe.matmul(ps[:, c:c + w], q, k, start=True, stop=True)
                        if m == len(parts) - 1 or (m + 1) * w % 512 == 0:
                            T.close(ins, (L + "s", i, m * w // 512))
                if 2 <= i < len(us) + 2:
                    nb = len(us[i - 2][4])
                    pe.wait_ge(S(L + "exps"), i - 1)
                    for b in range(nb):
                        if b % 4 == 0:
                            ps = T.open((L + "pt", i - 2, b // 4))
                        ins = pe.transpose(ps[:, b % 4 * P:(b % 4 + 1) * P], SM[:, (i - 2) % 3, b * P:(b + 1) * P], ident[:, :])
                        if b == nb - 1 or b % 4 == 3:
                            T.close(ins, (L + "pt", i - 2, b // 4))
                if i >= 3:
                    vs = us[i - 3][4]
                    for b in range(0, len(vs), 4):
                        wait_read(pe, (L + "pt", i - 3, b // 4))
                    ps = T.open((L + "o", i - 3))
                    for b, v in enumerate(vs):
                        ins = pe.matmul(ps[:, 0:64], ET[:, (i - 3) % 2, b * P:(b + 1) * P], v, start=(b == 0), stop=(b == len(vs) - 1))
                    T.close(ins, (L + "o", i - 3))
            for t in range(2):
                for i, u in enumerate(us):
                    if u[1] == t:
                        wait_read(pe, (L + "o", i))
                for g in range(OUT_TILES[e] // 4):
                    ps = T.open((L + "ot", t, g))
                    for k in range(4):
                        ins = pe.transpose(ps[:, k * P:(k + 1) * P], Y[:, t, (4 * g + k) * P:(4 * g + k + 1) * P], ident[:, :])
                    T.close(ins, (L + "ot", t, g))
            pe.wait_ge(S(L + "ot_parts"), 2 * (OUT_TILES[e] // 4))
            product(T, pe, L + "y", pname(e, "w_out"), OUT_TILES[e], D, [0, 1], lefts((O2H, O2L)))
            ffn_pe(T, pe, L, pname(e, "w_gate_up"), pname(e, "w_down"), [0, 1], SEQ, (UH2, UL2))

    def x2_ready(e, which):
        def wait(eng, t):
            if which == 0 and e == 0:
                eng.wait_ge(S("mem_loaded"), 16)
            elif which == 0 and t >= 2:
                pass
            else:
                name = "E%d_y" % e if which else "E%d_ffn" % (e - 1)
                for nn in range(2):
                    wait_read(eng, (name, nn, t))
        return wait

    def gain2(e, which, mem_which=None):
        def col(k, t):
            c = 24 * e + 8 * (mem_which if mem_which is not None and t >= 2 else which) + k
            return cols2[:, c:c + 1]
        return col

    @block2.scalar
    def _(act):
        act.wait_ge(S("zeroed"), 2)
        for e in range(DEPTH):
            for r, nm in enumerate(("norm_mix", "norm_mem", "norm_ffn")):
                r0 = 24 * e + 8 * r
                act.dma_start(stage2[r0:r0 + 8, :], pname(e, nm).rearrange("(r p) -> r p", p=P)).then_inc(S("norms_loaded"), 16)
        wait_result(act, ("cols2",))
        read_out(act.activation(cols2[:, :], bank(("cols2",))[:, 0:P], ACT.Copy), ("cols2",))
        wait_read(act, ("cols2",))
        act.wait_ge(S("angles"), 4)
        act.activation(table[:], angle[:], ACT.Sin).then_inc(S("tables"), 1)
        for e in range(DEPTH):
            L = "E%d_" % e
            norm_act(act, L + "n1", lambda t: X[:, t, :], [0, 1, 2, 3], HF2, gain2(e, 0, 1), None, x2_ready(e, 0))

            def copy(key, dst, width, scale=1.0):
                wait_result(act, key)
                read_out(act.activation(dst, bank(key)[:, 0:width], ACT.Copy, scale=scale), key)

            for nm, _, n, dst, at, _ in PROJ[e]:
                for j in range(n):
                    copy((L + nm, j), dst[:, at + j, :], SEQ)
                if nm == "ki":
                    for t in range(2):
                        copy((L + "wi", t), WI[:, t, :], IDX_HEADS, IDX_HEADS ** -0.5 * HEAD_DIM ** -0.5)
            for nm, _, at in VALUES[e]:
                for t in range(2):
                    copy((L + nm, 0, t), V2[:, at + t, :], MD)
            for j in range(2):
                copy((L + "km", j), K2[:, MEM_K[e] + j, :], SEQ)
            for t in range(2):
                copy((L + "vm", 0, 2 + t), V2[:, 6 + t, :], MD)
            if e == 0:
                for t in range(2):
                    for h in range(IDX_HEADS):
                        key = (L + "is", t, h)
                        i = IDX_HEADS * t + h
                        wait_result(act, key)
                        if i >= 2:
                            act.wait_ge(S("scored"), i - 1)
                        read_out(act.activation(RL[:, i % 2, 0:(t + 1) * P], bank(key)[:, 0:(t + 1) * P], ACT.Relu), key)
            us = attention_units(e)
            for i in range(len(us) + 2):
                if i < len(us):
                    w = P * len(us[i][4])
                    act.wait_ge(S(L + "maxes"), i + 1)
                    if i >= 6:
                        wait_read(act, (L + "o", i - 6))
                    act.activation(SM[:, i % 3, 0:w], SM[:, i % 3, 0:w], ACT.Exp, bias=mz[:, i % 6, 1:2],
                                   accum_out=mz[:, i % 6, 2:3]).then_inc(S(L + "exps"), 1)
                if i >= 2:
                    nb = len(us[i - 2][4])
                    if i >= 4:
                        wait_result(act, (L + "o", i - 4))
                    for b in range(0, nb, 4):
                        key = (L + "pt", i - 2, b // 4)
                        w = P * min(4, nb - b)
                        wait_result(act, key)
                        read_out(act.activation(ET[:, i % 2, b * P:b * P + w], bank(key)[:, 0:w], ACT.Copy), key)
            for t in range(2):
                for g in range(OUT_TILES[e] // 4):
                    key = (L + "ot", t, g)
                    wait_result(act, key)
                    n = t * (OUT_TILES[e] // 4) + g
                    if n >= 2:
                        act.wait_ge(S(L + "ot_parts"), n - 1)
                    read_out(act.activation(HF2[:, n % 2, :], bank(key), ACT.Copy), key)
            norm_act(act, L + "n2", lambda t: X[:, t, :], [0, 1], HF2, gain2(e, 2), None, x2_ready(e, 1))
            ffn_act(act, L, SEQ, UT2)
        c = norm_cols("final")
        for t in range(2):
            x2_ready(2, 0)(act, t)
            act.activation(XN[:, t, :], X[:, t, :], ACT.Square, accum_out=ss[:, c + t:c + t + 1]).then_inc(S("final_squares"), 1)

    @block2.gpsimd
    def _(pool):
        pool.memset(stage2[:], 0.0).then_inc(S("zeroed"), 1)
        pool.dma_start(FN[:, :], A["final_norm_2"].rearrange("(o d) -> o d", o=1).broadcast_to([P, D])).then_inc(S("final_gain"), 16)
        for e in range(DEPTH):
            L = "E%d_" % e
            rstd_pool(pool, L + "n1", [0, 1, 2, 3], D, "_rstd")
            rstd_pool(pool, L + "n2", [0, 1], D, "_rstd")
        rstd_pool(pool, "final", [0, 1], D, "_rstd")

    def add_rows(dve, name):
        for nn in range(2):
            for t in range(2):
                key = (name, nn, t)
                wait_result(dve, key)
                x = X[:, t, nn * 512:(nn + 1) * 512]
                read_out(dve.tensor_tensor(x, x, bank(key), ALU.add), key)

    @block2.vector
    def _(dve):
        TWO_PI_A, TWO_PI_B = 6.28125, 0.0019350051879882812
        TWO_PI_C = 2 * math.pi - TWO_PI_A - TWO_PI_B
        WHOLE = 12582912.0
        dve.wait_ge(S("tables_loaded"), 16 * 5)
        dve_link(dve, dve.tensor_copy(pos[:, :], pos_i[:, :]))
        for r in range(4):
            ahead = 0.25 if r % 2 == 0 else 0.0
            f = freqs[:, r // 2:r // 2 + 1]
            a, k = angle[:, r, :], turns[:, r, :]
            dve_link(dve, dve.tensor_scalar(a, pos[:, :], f, None, ALU.mult))
            dve_link(dve, dve.tensor_scalar(k, a, 0.5 / math.pi, ahead, ALU.mult, ALU.add))
            dve_link(dve, dve.tensor_scalar(k, k, WHOLE, None, ALU.add))
            dve_link(dve, dve.tensor_scalar(k, k, -WHOLE, None, ALU.add))
            for part in (TWO_PI_A, TWO_PI_B, TWO_PI_C):
                dve_link(dve, dve.scalar_tensor_tensor(a, k, -part, a, ALU.mult, ALU.add))
            if r % 2 == 0:
                dve_link(dve, dve.tensor_scalar(a, a, 0.5 * math.pi, None, ALU.add))
            dve.tensor_scalar(a, a, 3.1415925, -3.1415925, ALU.min, ALU.max).then_inc(S("angles"), 1)
        wait_read(dve, ("cols2",))
        for e in range(DEPTH):
            L = "E%d_" % e
            norm_dve(dve, L + "n1", lambda t: X[:, t, :], [0, 1, 2, 3], HF2, gain2(e, 0, 1), None, x2_ready(e, 0))
            if e == 0:
                dve.wait_ge(S("tables"), 1)
            for n, (nm, j, x, tab) in enumerate(rotations(e)):
                rope_dve(dve, L + nm, j, x, table[:, tab, :], table[:, tab + 1, :], RT[:, n % 2, :])
            if e == 0:
                for t in range(2):
                    w = (t + 1) * P
                    wait_read(dve, (L + "wi", t))
                    for h in range(IDX_HEADS):
                        i = IDX_HEADS * t + h
                        wait_read(dve, (L + "is", t, h))
                        if h == 0:
                            ins = dve.scalar_tensor_tensor(SC[:, t, 0:w], RL[:, i % 2, 0:w], WI[:, t, h:h + 1], causal[:, t, 0:w], ALU.mult, ALU.add)
                        else:
                            dve.wait_ge(S("scored"), i)
                            ins = dve.scalar_tensor_tensor(SC[:, t, 0:w], RL[:, i % 2, 0:w], WI[:, t, h:h + 1], SC[:, t, 0:w], ALU.mult, ALU.add)
                        ins.then_inc(S("scored"), 1)
                    dve.wait_ge(S("scored"), IDX_HEADS * (t + 1))
                for r in range(N_SEL // 8):
                    for t in range(2):
                        w = (t + 1) * P
                        dve_link(dve, dve.max(TOP[:, t, :], SC[:, t, 0:w]))
                    for t in range(2):
                        w = (t + 1) * P
                        dve_link(dve, dve.match_replace(SC[:, t, 0:w], TOP[:, t, :], SC[:, t, 0:w], TAKEN))
                for t in range(2):
                    w = (t + 1) * P
                    dve_link(dve, dve.tensor_scalar(MASK[:, t, 0:w], SC[:, t, 0:w], 0.5 * TAKEN, NEG, ALU.is_gt, ALU.mult))
                    dve_link(dve, dve.tensor_tensor(MASK[:, t, 0:w], MASK[:, t, 0:w], causal[:, t, 0:w], ALU.add))
            us = attention_units(e)

            def maxes(i):
                _, _, parts, masks, _ = us[i]
                if i >= 3:
                    for b in range(0, len(us[i - 3][4]), 4):
                        wait_result(dve, (L + "pt", i - 3, b // 4))
                for m, (_, _, w) in enumerate(parts):
                    key = (L + "s", i, m * w // 512)
                    c = m * w % 512
                    if c == 0:
                        wait_result(dve, key)
                    src, dst = bank(key)[:, c:c + w], SM[:, i % 3, m * w:(m + 1) * w]
                    if masks[m] is None:
                        ins = dve.tensor_scalar(dst, src, SCALE, None, ALU.mult)
                    else:
                        ins = dve.scalar_tensor_tensor(dst, src, SCALE, masks[m], ALU.mult, ALU.add)
                    if m == len(parts) - 1 or (m + 1) * w % 512 == 0:
                        read_out(ins, key)
                        wait_read(dve, key)
                    else:
                        dve_link(dve, ins)
                dve_link(dve, dve.tensor_reduce(mz[:, i % 6, 0:1], SM[:, i % 3, 0:sum(p[2] for p in parts)], AX_X, ALU.max))
                dve.tensor_scalar(mz[:, i % 6, 1:2], mz[:, i % 6, 0:1], -1.0, None, ALU.mult).then_inc(S(L + "maxes"), 1)

            def take_o(i):
                c, t, _, _, _ = us[i]
                key = (L + "o", i)
                wait_result(dve, key)
                dve.wait_ge(S(L + "exps"), i + 1)
                dve_link(dve, dve.reciprocal(mz[:, i % 6, 3:4], mz[:, i % 6, 2:3]))
                read_out(dve.tensor_scalar(Y[:, t, c:c + 64], bank(key)[:, 0:64], mz[:, i % 6, 3:4], None, ALU.mult), key)

            for i in range(len(us) + 4):
                if i < len(us):
                    maxes(i)
                if i >= 4:
                    take_o(i - 4)
            for t in range(2):
                for g in range(OUT_TILES[e] // 4):
                    n = t * (OUT_TILES[e] // 4) + g
                    wait_read(dve, (L + "ot", t, g))
                    to = (slice(None), slice(4 * g, 4 * g + 4), slice(t * P, (t + 1) * P))
                    split_value(dve, O2H[to], O2L[to], HF2[:, n % 2, :].rearrange("p (k c) -> p k c", k=4)).then_inc(S(L + "ot_parts"), 1)
            add_rows(dve, L + "y")
            norm_dve(dve, L + "n2", lambda t: X[:, t, :], [0, 1], HF2, gain2(e, 2), None, x2_ready(e, 1))
            ffn_dve(dve, L, SEQ, UT2, (UH2, UL2))
            add_rows(dve, L + "ffn")
        c = norm_cols("final")
        dve.wait_ge(S("final_gain"), 16)
        for t in range(2):
            dve.wait_ge(S("final_rstd"), t + 1)
            dve.scalar_tensor_tensor(Y[:, t, :], X[:, t, :], rstd[:, c + t:c + t + 1], FN[:, :], ALU.mult, ALU.mult).then_inc(S("final"), 1)

    @block2.sync
    def _(sp):
        sp.dma_start(X[:, 2:4, :], A["mem_2"][0].rearrange("(t p) d -> p t d", p=P)).then_inc(S("mem_loaded"), 16)
        sp.dma_start(causal[:], A["causal"].rearrange("t p k -> p t k")).then_inc(S("tables_loaded"), 16)
        for t in range(2):
            sp.dma_start(dilated[:, t, :, :], A["dilated"][t]).then_inc(S("tables_loaded"), 16)
        sp.dma_start(freqs[:], A["freqs"]).then_inc(S("tables_loaded"), 16)
        sp.dma_start(pos_i[:], A["positions_2"][0:1, :].broadcast_to([P, SEQ])).then_inc(S("tables_loaded"), 16)
        load_chunks(sp, now["chunk0"])
        for t in range(2):
            sp.wait_ge(S("final"), t + 1)
            sp.dma_start(out[0, t * P:(t + 1) * P, :], Y[:, t, :]).then_inc(S("stored"), 16)
        sp.wait_ge(S("stored"), 32)

    st.close()
    ctx.close()


def kernel(**inputs):
    import numpy as _np
    import concourse.bacc as _bacc
    from concourse import mybir as _mybir
    from concourse.bass_utils import run_bass_kernel_spmd as _run

    nc = _bacc.Bacc("TRN2", target_bir_lowering=False, num_devices=1)
    arrays, args = {}, {}
    for name, a in list(inputs.items()) + list(shape_constants().items()):
        a = _np.ascontiguousarray(a)
        arrays[f"in_{name}_dram"] = a
        args[name] = nc.dram_tensor(f"in_{name}_dram", a.shape, _mybir.dt.from_np(a.dtype), kind="ExternalInput").ap()
    out = nc.dram_tensor("out_0_dram", (1, SEQ, D), F32, kind="ExternalOutput").ap()
    build(nc, args, out, STOP)
    r = _run(nc, [arrays], core_ids=[0])
    return r.results[0]["out_0_dram"]


STOP = 9
```

```python
from contextlib import ExitStack
import math

import numpy as np

import concourse.bass as bass
from concourse import mybir

F32 = mybir.dt.float32
F32R = mybir.dt.float32r
I32 = mybir.dt.int32
ALU = mybir.AluOpType
ACT = mybir.ActivationFunctionType
AX_X = mybir.AxisListType.X

P = 128
D = 1024
KT = D // P
SEQ = 256
DEPTH = 2
GRID_W = 64
EPS = 1e-6
CONV_CH, CONV_W = 512, 31
HALF_W = CONV_W // 2
HEADS, HEAD_DIM, V_DIM = 8, 64, 128
POOL_CH = 512
POOL_PAD = 8
NCH = CONV_CH // P
D_FF = 2816
FT = D_FF // P
COL_Q = 2 * CONV_CH
COL_K = COL_Q + 1024
COL_V = COL_K + 1024
COL_P = COL_V + 1024
COL_G = COL_P + POOL_CH
NEG = -1e30
TAKEN = -3e38
N_SEL = 64
IDX_HEADS = 8
SCALE = HEAD_DIM ** -0.5
BANKS = 8
SLOT = 1024
RAW = (3, 5)
SPLIT = (3, 4)
AHEAD = 2

ROW_PRE, ROW_FFN, ROW_GATE = 0, 8, 16
ROW_CB, ROW_LG, ROW_LB, ROW_PS, ROW_SUB = 40, 44, 48, 52, 56


def shape_constants():
    f = np.float32
    d = np.arange(P)
    t = np.arange(SEQ)
    inv = f(10000.0) ** (-np.arange(0, 32, 2, dtype=f) / f(32))
    pos = np.where((d % 64 < 32)[:, None], (t // GRID_W)[None, :], (t % GRID_W)[None, :]).astype(f)
    ang = pos * inv[d % 16][:, None]

    def swap(half, rot):
        m = np.zeros((P, P), f)
        for i in range(P):
            r = i % 64
            if r % rot < half and r < (64 if rot == 32 and half == 16 else rot):
                m[i + half, i] = -1
            elif r < (64 if rot == 32 and half == 16 else rot):
                m[i - half, i] = 1
        return m

    idx_swap = swap(16, 32)
    idx_swap[:, d % 64 >= 32] = 0
    counts = np.zeros((4, SEQ), f)
    for g, w in enumerate((2, 4, 8, 16)):
        counts[g] = 1 / (np.clip(t + w // 2, 0, SEQ) - np.clip(t - w // 2, 0, SEQ)).astype(f)
    q = np.arange(SEQ)
    causal = np.where(q[None, :] <= q[:, None], 0, NEG).astype(f)
    dil = np.stack([np.where((q[None, :] <= q[:, None]) & ((q[:, None] - q[None, :]) % r == 0)
                             & ((q[:, None] - q[None, :]) // r <= P), 0, NEG).astype(f)
                    for r in (1, 4, 16)], 1)
    freq = f(10000.0) ** (-np.arange(32, dtype=f) / f(32))
    ifreq = f(10000.0) ** (-np.arange(16, dtype=f) / f(16))
    freqs = np.stack([freq[d % 32], np.where(d % 64 < 32, ifreq[d % 16], 0).astype(f)], 1)
    sel = np.tile(np.eye(2, dtype=f), (2, 1))
    return {
        "ident": np.eye(P, dtype=f), "swaps": np.stack([swap(16, 32), swap(32, 64), idx_swap], 1),
        "grid_rope": np.stack([np.cos(ang), np.sin(ang)], 1).astype(f),
        "inv_counts": np.ascontiguousarray(np.broadcast_to(counts, (P, 4, SEQ))),
        "causal": causal.reshape(2, P, SEQ), "dilated": dil.reshape(2, P, 3, SEQ),
        "freqs": freqs, "pick": sel,
    }


def build(nc, A, out):
    ctx = ExitStack()
    sems = {}

    def S(name):
        if name not in sems:
            sems[name] = ctx.enter_context(nc.semaphore(name))
        return sems[name]

    place = [(nc.sbuf_base + 31) // 32 * 32]

    def sb(name, shape, dt=F32):
        t = nc.alloc_sbuf_tensor_at(name, shape, dt, offset=place[0])
        place[0] += (4 * math.prod(shape[1:]) + 31) // 32 * 32
        assert place[0] <= nc.sbuf_usable_end, (name, place[0])
        return t

    def over(offset, name, shape, dt=F32):
        assert offset + 4 * math.prod(shape[1:]) <= nc.sbuf_usable_end, name
        return nc.alloc_sbuf_tensor_at(name, shape, dt, offset=offset)

    PS = ctx.enter_context(nc.psum_tensor("PS", [P, BANKS, 512], F32))
    pe_done, act_step, dve_step, pool_step = S("pe_done"), S("act_step"), S("dve_step"), S("pool_step")
    high_done, low_done = S("high_done"), S("low_done")
    bank_read = [S(f"bank_read{b}") for b in range(BANKS)]
    slot_full = [S(f"slot_full{s}") for s in range(max(RAW))]
    uses, milestones, bank_no, bank_used = {}, {}, [0, 0], [0] * BANKS
    chunks, loads = [], [0] * max(RAW)
    splits, chunk_of = [], {}
    now = {"block": 0, "chunk0": 0, "split0": 0, "act": 0, "dve": 0}
    count = {"act": 0, "dve": 0, "pool": 0}

    X = sb("X", [P, 4, D])
    XN = sb("XN", [P, 2, D])
    at_h = place[0]
    HH = sb("HH", [P, KT, 2 * SEQ], F32R)
    HL = sb("HL", [P, KT, 2 * SEQ], F32R)
    YY = over(at_h, "YY", [P, 4, D])
    ident = sb("ident", [P, P])
    swaps = sb("swaps", [P, 3, P])
    ones = sb("ones", [P, P])
    half = sb("half", [P, 8])
    ss = sb("ss", [P, 80])
    ms = sb("ms", [P, 80])
    rstd = sb("rstd", [P, 80])
    cols2 = sb("cols2", [P, 48])
    common_end = place[0]

    def weight_rings(b):
        return ([sb("raw%d_%d" % (b, i), [P, SLOT]) for i in range(RAW[b])],
                [sb("split%d_%d" % (b, i), [P, 2, SLOT], F32R) for i in range(SPLIT[b])])

    rings = [weight_rings(0)]
    stat_col = {}


    def bank(key):
        return PS[:, uses[key][0], :]

    def wait_result(eng, key):
        keep_splitting(eng, key)
        eng.wait_ge(pe_done, milestones[key])

    def read_out(ins, key):
        ins.then_inc(bank_read[uses[key][0]], 1)

    def wait_read(eng, key):
        keep_splitting(eng, key)
        eng.wait_ge(bank_read[uses[key][0]], uses[key][1] + 1)

    class Tensor:

        def __init__(self, pe):
            self.pe = pe

        def open(self, key):
            if key[0] == "mod":
                b = BANKS - 1
            else:
                b = bank_no[0] % (BANKS - 1)
                bank_no[0] += 1
            uses[key] = b, bank_used[b]
            if bank_used[b]:
                self.pe.wait_ge(bank_read[b], bank_used[b])
            bank_used[b] += 1
            return PS[:, b, :]

        def close(self, ins, key):
            bank_no[1] += 1
            milestones[key] = bank_no[1]
            chunk_of[key] = len(chunks) - 1
            ins.then_inc(pe_done, 1)

        def mark(self, ins):
            bank_no[1] += 1
            ins.then_inc(pe_done, 1)

        def load(self, src, shape, split=True):
            i = len(chunks)
            b = now["block"]
            s = (i - now["chunk0"]) % RAW[b]
            pieces = src if isinstance(src, list) else [src]
            loads[s] += 16 * len(pieces)
            c = {"pieces": pieces, "shape": shape, "slot": s, "raw": view(rings[b][0][s][:, :], shape), "full": loads[s],
                 "free": None, "split": None}
            chunks.append(c)
            if not split:
                self.pe.wait_ge(slot_full[s], loads[s])
                return c, c["raw"]
            k = c["split"] = len(splits)
            two = rings[b][1][(k - now["split0"]) % SPLIT[b]]
            c["high"], c["low"] = view(two[:, 0, :], shape), view(two[:, 1, :], shape)
            splits.append(c)
            self.pe.wait_ge(low_done, k + 1)
            return c, (c["high"], c["low"])

        def used(self, c):
            c["free"] = bank_no[1]

    def view(t, shape):
        a, b = shape
        return t[:, 0:a * b].rearrange("p (a b) -> p a b", a=a)

    def rows(w, k0, nk, c0, nc_):
        return w[k0 * P:(k0 + nk) * P, c0:c0 + nc_].rearrange("(k p) c -> p k c", p=P)

    def keep_splitting(eng, key):
        if eng is nc.scalar or eng is nc.vector:
            split_until(eng, chunk_of[key] + AHEAD)

    def split_until(eng, last):
        who = "act" if eng is nc.scalar else "dve"
        b = now["block"]
        while now[who] < len(splits) and chunks.index(splits[now[who]]) <= last:
            k = now[who]
            c = splits[k]
            now[who] = k + 1
            if who == "act":
                eng.wait_ge(slot_full[c["slot"]], c["full"])
                if k - SPLIT[b] >= now["split0"]:
                    eng.wait_ge(pe_done, splits[k - SPLIT[b]]["free"])
                eng.activation(c["high"], c["raw"], ACT.Copy).then_inc(high_done, 1)
            else:
                eng.wait_ge(high_done, k + 1)
                eng.tensor_tensor(c["low"], c["raw"], c["high"].bitcast(F32), ALU.subtract).then_inc(low_done, 1)

    def split_value(dve, high, low, value):
        dve_link(dve, dve.tensor_copy(high, value))
        return dve.tensor_tensor(low, value, high.bitcast(F32), ALU.subtract)


    def multiply(pe, out, a, b, first, last):
        pe.matmul(out, a[0], b[0], start=first, stop=False)
        pe.matmul(out, a[0], b[1], start=False, stop=False)
        return pe.matmul(out, a[1], b[0], start=False, stop=last)

    def cut2(pair, *index):
        return pair[0][index], pair[1][index]

    def tile_t(T, pe, key, ws, kts, c, rhs, n):
        ps = T.open(key)
        for k in range(kts):
            ins = multiply(pe, ps[:, 0:n], cut2(ws, slice(None), k, slice(c * P, (c + 1) * P)), rhs(k), k == 0, k == kts - 1)
        T.close(ins, key)

    def product_t(T, pe, name, w, c0, tiles, kts, rhs, n, source=None, before=None):
        per = SLOT // kts // P
        for j in range(tiles):
            if j % per == 0:
                src = source(j) if source else rows(w, 0, kts, c0 + j * P, per * P)
                i, ws = T.load(src, (kts, per * P))
            if before:
                before(j)
            tile_t(T, pe, (name, j), ws, kts, j % per, rhs, n)
            if j % per == per - 1:
                T.used(i)

    def product(T, pe, name, w, kts, cols, tiles, lhs, before=None):
        width = min(512, cols)
        step = SLOT // width
        for n in range(cols // width):
            ps = {}
            for k0 in range(0, kts, step):
                i, ws = T.load(rows(w, k0, step, n * width, width), (step, width))
                if k0 == 0:
                    for t in tiles:
                        ps[t] = T.open((name, n, t))
                for k in range(k0, k0 + step):
                    if before and n == 0:
                        before(k)
                    for t in tiles:
                        ins = multiply(pe, ps[t][:, 0:width], lhs(k, t), cut2(ws, slice(None), k - k0), k == 0, k == kts - 1)
                        if k == kts - 1:
                            T.close(ins, (name, n, t))
                if k0 + step < kts:
                    T.mark(ins)
                T.used(i)


    def norm_cols(name):
        if name not in stat_col:
            stat_col[name] = 4 * (len(stat_col) % 20)
        return stat_col[name]

    def norm_act(act, name, src, tiles, hf, scale, bias, ready):
        c = norm_cols(name)
        for n, t in enumerate(tiles):
            ready(act, t)
            if n >= 2:
                wait_result(act, (name, tiles[n - 2], 1))
            act.activation(XN[:, n % 2, :], src(t), ACT.Square,
                           accum_out=ss[:, c + n:c + n + 1]).then_inc(S(name + "_squares"), 1)
            if n >= 1:
                if n >= 2:
                    act.wait_ge(S(name + "_parts"), 2 * (n - 2) + 1)
                columns(act, name, tiles[n - 1], 0, hf, scale, bias)
        if len(tiles) >= 2:
            act.wait_ge(S(name + "_parts"), 2 * (len(tiles) - 2) + 1)
        columns(act, name, tiles[-1], 0, hf, scale, bias)

    def columns(eng, name, t, g, hf, scale, bias):
        key = (name, t, g)
        wait_result(eng, key)
        for k in range(4 * g, 4 * g + 4):
            src = bank(key)[:, (k % 4) * P:(k % 4 + 1) * P]
            dst = hf[:, g, (k % 4) * P:(k % 4 + 1) * P]
            if eng is nc.scalar:
                ins = eng.activation(dst, src, ACT.Identity, scale=scale(k, t), bias=bias(k, t) if bias else 0.0)
            elif bias:
                ins = eng.tensor_scalar(dst, src, scale(k, t), bias(k, t), ALU.mult, ALU.add)
            else:
                ins = eng.tensor_scalar(dst, src, scale(k, t), None, ALU.mult)
        read_out(ins, key)

    def rstd_pool(pool, name, tiles, width, sem):
        c = norm_cols(name)
        for n, t in enumerate(tiles):
            pool.wait_ge(S(name + "_squares"), n + 1)
            pool.tensor_scalar(ms[:, c + n:c + n + 1], ss[:, c + n:c + n + 1], 1.0 / width, EPS, ALU.mult,
                               ALU.add).then_inc(pool_step, 1)
            count["pool"] += 1
            pool.wait_ge(pool_step, count["pool"])
            pool.tensor_tensor(rstd[:, c + n:c + n + 1], ms[:, c + n:c + n + 1], half[:, 0:1],
                               ALU.pow).then_inc(S(name + sem), 1)

    def norm_dve(dve, name, src, tiles, hf, scale, bias, ready):
        c = norm_cols(name)

        def parts(n, t):
            if n:
                dve.wait_ge(S(name + "_parts"), 2 * n)
            columns(dve, name, t, 1, hf, scale, bias)
            for g in range(2):
                wait_read(dve, (name, t, g))
                to = (slice(None), slice(4 * g, 4 * g + 4), slice(t * P, (t + 1) * P))
                split_value(dve, HH[to], HL[to], hf[:, g, :].rearrange("p (k c) -> p k c", k=4)).then_inc(S(name + "_parts"), 1)

        for n, t in enumerate(tiles):
            ready(dve, t)
            dve.wait_ge(S(name + "_rstd"), n + 1)
            dve.tensor_scalar(XN[:, n % 2, :], src(t), rstd[:, c + n:c + n + 1], None,
                              ALU.mult).then_inc(S(name + "_xn"), 1)
            if n >= 1:
                parts(n - 1, tiles[n - 1])
        parts(len(tiles) - 1, tiles[-1])

    def norm_pe(T, pe, name, tiles):
        for n, t in enumerate(tiles):
            pe.wait_ge(S(name + "_xn"), n + 1)
            transposes(T, pe, name, t, XN[:, n % 2, :])

    def transposes(T, pe, name, t, src):
        for g in range(2):
            ps = T.open((name, t, g))
            for k in range(4):
                c = (4 * g + k) * P
                ins = pe.transpose(ps[:, k * P:(k + 1) * P], src[:, c:c + P], ident[:, :])
            T.close(ins, (name, t, g))

    def norm_wait(eng, name, tiles):
        eng.wait_ge(S(name + "_parts"), 2 * len(tiles))

    def dve_link(dve, ins):
        count["dve"] += 1
        ins.then_inc(dve_step, 1)
        dve.wait_ge(dve_step, count["dve"])

    def act_link(act, ins):
        count["act"] += 1
        ins.then_inc(act_step, 1)
        act.wait_ge(act_step, count["act"])


    def rope_pe(T, pe, name, j, x, swap):
        wait_read(pe, (name, j))
        ps = T.open((name + "_rot", j))
        T.close(pe.matmul(ps[:, 0:SEQ], swap, x, start=True, stop=True), (name + "_rot", j))

    def rope_dve(dve, name, j, x, cos, sin, tmp):
        key = (name + "_rot", j)
        wait_result(dve, key)
        read_out(dve.tensor_tensor(tmp, bank(key)[:, 0:SEQ], sin, ALU.mult), key)
        wait_read(dve, key)
        dve_link(dve, dve.tensor_tensor(x, x, cos, ALU.mult))
        dve.tensor_tensor(x, x, tmp, ALU.add).then_inc(S(name + "_roped"), 1)

    cols = sb("cols", [P, 2, 2, P])
    cols_mod = sb("cols_mod", [P, P])
    G = sb("G", [P, 2, D])
    pick = sb("pick", [4, 2])
    silu_f = sb("silu_f", [P, KT, 2])
    silu_c = sb("silu_c", [P, KT, 4], F32R)
    mod = sb("mod", [P, DEPTH, 6, KT, 2])
    gain = sb("gain", [P, DEPTH, 2, KT, 2])
    sub_g = sb("sub_g", [P, 2])
    lams = sb("lams", [P, 2, 8])
    mx = sb("mx", [P, 2, 8])
    subs = sb("subs", [P, 3, 4, 8])
    hidden_at = place[0]
    at_q = place[0]
    QT = sb("QT", [P, 8, 2 * SEQ])
    at_k = place[0]
    KTT = sb("KTT", [P, 8, 2 * SEQ])
    at_v = place[0]
    V = sb("V", [P, 4, D])
    at_o = place[0]
    O = over(at_o, "O", [P, 4, D])
    place[0] += 2 * D * 4
    UP = sb("UP", [P, NCH, 2, SEQ + 2 * HALF_W])
    CV = sb("CV", [P, NCH, 2, SEQ])
    PP = sb("PP", [P, 4, 2, SEQ + 2 * POOL_PAD])
    at_tmp = place[0]
    TMP = sb("TMP", [P, 4096])
    MT = over(at_q, "MT", [P, KT, 2 * SEQ])
    MTL = over(at_q, "MTL", [P, KT, 2 * SEQ], F32R)
    MTH = over(at_o, "MTH", [P, KT, 2 * SEQ], F32R)
    OTH = over(at_k, "OTH", [P, KT, 2 * SEQ], F32R)
    OTL = over(at_v, "OTL", [P, KT, 2 * SEQ], F32R)
    MIX = [over(at_k + 8192 * i, "MIX%d" % i, [P, 4, 2 * SEQ], F32R) for i in range(2)]
    CS = [over(at_v + 8192 * i, "CS%d" % i, [P, NCH, 2 * SEQ], F32R) for i in range(2)]
    UH = over(hidden_at, "UH", [P, FT, 2 * SEQ], F32R)
    UL = over(hidden_at + FT * 2 * SEQ * 4, "UL", [P, FT, 2 * SEQ], F32R)
    UT = over(hidden_at + 2 * FT * 2 * SEQ * 4, "UT", [P, 2, 2, 2 * SEQ])
    PT = XN[:, :, 0:2 * (SEQ + 2 * POOL_PAD)].rearrange("p b (s t) -> p b s t", s=2)
    MR = XN[0:4, 0, :].rearrange("p (b k) -> p b k", b=2)
    diagonal = XN[:, 1, :].rearrange("p (b k) -> p b k", b=2)
    stage = TMP[:, 0:512].rearrange("p (l m k) -> p l m k", l=2, m=2)
    lamv = TMP[:, 512:1024].rearrange("p (l m k) -> p l m k", l=2, m=4)
    stage_mod = TMP[:, 1024:1152]
    stage_norms = TMP[0:48, 1280:1408]
    stage_c = TMP[0:2 * KT, 1152:1280]
    HF = TMP[:, 0:1024].rearrange("p (b k) -> p b k", b=2)
    SG = TMP[:, 0:1024].rearrange("p (b k) -> p b k", b=2)
    E2 = TMP[:, 0:2048].rearrange("p (b i k) -> p b i k", b=2, i=2)
    GY = TMP[:, 1024:2048].rearrange("p (b k) -> p b k", b=2)
    rope_tmp = TMP[:, 1024:2048].rearrange("p (b k) -> p b k", b=4)
    grid = TMP[:, 2560:3072].rearrange("p (b k) -> p b k", b=2)
    AA = TMP[:, 2048:3072].rearrange("p (b k) -> p b k", b=2)
    OF = TMP[:, 3072:4096].rearrange("p (b k) -> p b k", b=2)
    AT = TMP[:, 3072:4096].rearrange("p (b k) -> p b k", b=2)
    counts = TMP[:, 3072:4096].rearrange("p (g k) -> p g k", g=4)

    def both(pair, n):
        return lambda k: (pair[0][:, k, 0:n], pair[1][:, k, 0:n])

    def lefts(pair):
        return lambda k, t: (pair[0][:, k, t * P:(t + 1) * P], pair[1][:, k, t * P:(t + 1) * P])

    def first_rows(l):
        v = lambda n: A[n][l].rearrange("(r p) -> r p", p=P)
        lst = [(ROW_PRE, v("g_pre_mix")), (ROW_FFN, v("g_pre_ffn")), (ROW_GATE, v("b_gate")), (ROW_CB, v("conv_b")),
               (ROW_LG, v("conv_ln_g")), (ROW_LB, v("conv_ln_b")), (ROW_PS, v("pool_scale")), (ROW_SUB, v("subln_g"))]
        return lst

    def layer_tokens(l):
        ns = 2 if l < DEPTH - 1 else 1
        return ns, ns * SEQ, list(range(2 * ns))

    def param_loads():
        lst = []
        for l in range(DEPTH):
            lst += [(stage[r:r + src.shape[0], l, 0, :], src) for r, src in first_rows(l)]
            lst.append((stage[0:CONV_W * NCH, l, 1, :], A["conv_w"][l].rearrange("t (j p) -> (t j) p", p=P)))
        for r, src in ((0, A["g_post_mix"]), (16, A["g_post_ffn"]), (32, A["b_mod"])):
            src = src.rearrange("l (r p) -> (l r) p", p=P)
            lst.append((stage_mod[r:r + src.shape[0], :], src))
        for e in range(DEPTH):
            for r, nm in enumerate(("norm_mix", "norm_mem", "norm_ffn")):
                r0 = 24 * e + 8 * r
                lst.append((stage_norms[r0:r0 + 8, :], A["l%d_%s_2" % (e, nm)].rearrange("(r p) -> r p", p=P)))
        return lst

    PARAM_LOADS = len(param_loads())

    GROUP = KT // 2
    SHIFT_1, SCALE_1, GATE_1, SHIFT_2, SCALE_2, GATE_2 = range(6)
    groups = [(l, s, n) for l in range(DEPTH) for s in range(6) for n in range(2)]
    phases = {"start": groups[0:4], "L0_branches": groups[4:10], "L0_ffn": groups[10:21], "L1_branches": groups[21:24]}

    def mod_step(phase, point):
        if phase == "L1_branches":
            point = point // 2 if point % 2 else None
        if phase not in phases or point is None or point >= GROUP * len(phases[phase]):
            return None
        return point

    def mod_pe(T, pe, phase, point):
        q = mod_step(phase, point)
        if q is None:
            return
        if q % GROUP == 1 and q > GROUP:
            mod_turn(T, pe, phases[phase][q // GROUP - 1])
        l, sec, n = group = phases[phase][q // GROUP]
        k0 = 2 * (q % GROUP)
        i, ws = T.load(rows(A["w_mod"][l], k0, 2, sec * D + n * 512, 512), (2, 512))
        if k0 == 0:
            T.open(("mod",) + group)
        for k in range(2):
            for part in range(2):
                ins = pe.matmul(bank(("mod",) + group)[0:4, :], silu_c[:, k0 + k, :], ws[part][:, k, :],
                                start=(k0 + k + part == 0), stop=(k0 + k + part == KT))
        if k0 < KT - 2:
            T.mark(ins)
        else:
            T.close(ins, ("mod",) + group)
        T.used(i)

    def mod_turn(T, pe, group):
        wait_read(pe, ("mod",) + group)
        ps = T.open(("turn",) + group)
        row = MR[:, groups.index(group) % 2, :]
        for k in range(4):
            ins = pe.matmul(ps[:, 2 * k:2 * k + 2], row[:, k * P:(k + 1) * P], pick[:, :], start=True, stop=True)
        T.close(ins, ("turn",) + group)

    def mod_act(act, phase, point):
        q = mod_step(phase, point)
        if q is None or q % GROUP != GROUP - 1:
            return
        group = phases[phase][q // GROUP]
        g = groups.index(group)
        wait_result(act, ("mod",) + group)
        if g >= 2:
            wait_result(act, ("turn",) + groups[g - 2])
        read_out(act.activation(MR[:, g % 2, :], bank(("mod",) + group)[0:4, :], ACT.Copy), ("mod",) + group)

    def mod_dve(dve, phase, point):
        q = mod_step(phase, point)
        if q is not None and q % GROUP == 1 and q > GROUP:
            mod_columns(dve, phases[phase][q // GROUP - 1])

    def mod_columns(dve, group):
        l, sec, n = group
        key = ("turn",) + group
        wait_result(dve, key)
        b = 32 + 48 * l + 8 * sec + 4 * n
        read_out(dve.tensor_tensor(mod[:, l, sec, 4 * n:4 * n + 4, :], bank(key)[:, 0:8].rearrange("p (k m) -> p k m", m=2),
                                   cols_mod[:, b:b + 4].rearrange("p (k o) -> p k o", o=1).broadcast_to([P, 4, 2]), ALU.add), key)
        if n == 0 or sec in (SHIFT_1, SHIFT_2):
            return
        wait_read(dve, ("turn", l, sec, 0))
        wait_read(dve, key)
        if sec in (SCALE_1, SCALE_2):
            part = int(sec == SCALE_2)
            for half_ in range(2):
                wait_read(dve, ("turn", l, sec - 1, half_))
            g0 = ROW_FFN if part else ROW_PRE
            for m in range(2):
                ins = dve.scalar_tensor_tensor(gain[:, l, part, :, m], mod[:, l, sec, :, m], 1.0, cols[:, l, 0, g0:g0 + KT], ALU.add, ALU.mult)
                if m == 0:
                    dve_link(dve, ins)
            ins.then_inc(S("L%d_gains" % l), 1)
        else:
            c = 16 * (sec == GATE_2) + 8 * l
            gate = mod[:, l, sec, :, :]
            dve.tensor_tensor(gate, gate, cols_mod[:, c:c + KT].rearrange("p (k o) -> p k o", o=1).broadcast_to([P, KT, 2]),
                              ALU.mult).then_inc(S("gates"), 1)


    def gate_parts(l, part):
        return [(l, part, m, h) for m in range(layer_tokens(l)[0]) for h in range(2)]

    def gates_dve(dve, l, part):
        dve.wait_ge(S("gates"), 2 * l + part + 1)
        for _, _, m, h in gate_parts(l, part):
            if m:
                wait_result(dve, ("gate", l, part, m - 1, h))
            for k in range(4):
                kt = 4 * h + k
                dve.tensor_scalar(diagonal[:, h, k * P:(k + 1) * P], ident[:, :], mod[:, l, GATE_2 if part else GATE_1, kt, m:m + 1],
                                  None, ALU.mult).then_inc(S("diagonals"), 1)

    def gates_pe(T, pe, l, part):
        for key in gate_parts(l, part):
            gate_count[0] += 4
            pe.wait_ge(S("diagonals"), gate_count[0])
            ps = T.open(("gate",) + key)
            T.close(pe.matmul(ps, ones[:, :], diagonal[:, key[3], :], start=True, stop=True), ("gate",) + key)

    def gates_act(act, l, part):
        for key in gate_parts(l, part):
            wait_result(act, ("gate",) + key)
            _, _, m, h = key
            read_out(act.activation(G[:, m, h * 512:(h + 1) * 512], bank(("gate",) + key), ACT.Copy), ("gate",) + key)

    gate_count = [0]
    nothing = lambda *args: None

    ROPES = [("q", j) for j in range(8)] + [("k", j) for j in range(8)]
    units_of = {l: [(t, h) for t in layer_tokens(l)[2] for h in range(HEADS)] for l in range(DEPTH)}

    def ffn_pe(T, pe, L, w_up, w_down, tiles, n, U, fill=nothing, then=nothing):
        norm_pe(T, pe, L + "n2", tiles)
        norm_wait(pe, L + "n2", tiles)
        for j in range(FT):
            for nm, c0 in (("ffn_gate", 0), ("ffn_up", D_FF)):
                i, ws = T.load(rows(w_up, 0, KT, c0 + j * P, P), (KT, P))
                tile_t(T, pe, (L + nm, j), ws, KT, 0, both((HH, HL), n), n)
                T.used(i)
                fill(2 * j + (nm == "ffn_up"))
        then()
        product(T, pe, L + "ffn", w_down, FT, D, tiles, lefts(U), before=lambda k: pe.wait_ge(S(L + "hidden"), k + 1))

    def ffn_act(act, L, n, tmp, fill=nothing):
        for j in range(FT):
            key = (L + "ffn_gate", j)
            wait_result(act, key)
            if j >= 2:
                wait_read(act, (L + "ffn_up", j - 2))
            read_out(act.activation(tmp[:, 0, j % 2, 0:n], bank(key)[:, 0:n], ACT.Silu), key)
            fill(2 * j)
            fill(2 * j + 1)

    def ffn_dve(dve, L, n, tmp, U, fill=nothing):
        for j in range(FT):
            fill(2 * j)
            key = (L + "ffn_up", j)
            wait_read(dve, (L + "ffn_gate", j))
            wait_result(dve, key)
            value = tmp[:, 1, j % 2, 0:n]
            if j >= 2:
                dve.wait_ge(S(L + "hidden"), j - 1)
            read_out(dve.tensor_tensor(value, tmp[:, 0, j % 2, 0:n], bank(key)[:, 0:n], ALU.mult), key)
            wait_read(dve, key)
            split_value(dve, U[0][:, j, 0:n], U[1][:, j, 0:n], value).then_inc(S(L + "hidden"), 1)
            fill(2 * j + 1)

    def post_act(act, L, name, tiles):
        c = norm_cols(L + name), norm_cols(L + name + "_half")
        for nn in range(2):
            for n, t in enumerate(tiles):
                k = nn * len(tiles) + n
                wait_result(act, (L + name, nn, t))
                if k >= 4:
                    act.wait_ge(S(L + name + "_squares"), k - 3)
                act.activation(XN[:, k % 4 // 2, k % 2 * 512:k % 2 * 512 + 512], bank((L + name, nn, t)), ACT.Square,
                               accum_out=ss[:, c[nn] + n:c[nn] + n + 1]).then_inc(S(L + name + "_squares"), 1)
        act.wait_ge(S(L + name + "_squares"), 2 * len(tiles))

    def post_pool(pool, L, name, tiles):
        c, c2 = norm_cols(L + name), norm_cols(L + name + "_half")
        for n, t in enumerate(tiles):
            pool.wait_ge(S(L + name + "_squares"), len(tiles) + n + 1)
            pool.tensor_tensor(ms[:, c2 + n:c2 + n + 1], ss[:, c + n:c + n + 1], ss[:, c2 + n:c2 + n + 1], ALU.add).then_inc(pool_step, 1)
            pool.wait_ge(pool_step, count["pool"] + 1)
            pool.tensor_scalar(ms[:, c + n:c + n + 1], ms[:, c2 + n:c2 + n + 1], 1.0 / D, EPS, ALU.mult, ALU.add).then_inc(pool_step, 1)
            count["pool"] += 2
            pool.wait_ge(pool_step, count["pool"])
            pool.tensor_tensor(rstd[:, c + n:c + n + 1], ms[:, c + n:c + n + 1], half[:, 0:1],
                               ALU.pow).then_inc(S(L + name + "_rstd"), 1)

    def post_dve(dve, L, name, tiles, which):
        c = norm_cols(L + name)
        for key in gate_parts(int(L[1]), which):
            wait_read(dve, ("gate",) + key)
        for nn in range(2):
            to = slice(nn * 512, (nn + 1) * 512)
            for n, t in enumerate(tiles):
                key = (L + name, nn, t)
                wait_result(dve, key)
                dve.wait_ge(S(L + name + "_squares"), nn * len(tiles) + n + 1)
                read_out(dve.tensor_tensor(YY[:, t, to], bank(key), G[:, t // 2, to], ALU.mult), key)
        for n, t in enumerate(tiles):
            for nn in range(2):
                wait_read(dve, (L + name, nn, t))
            dve.wait_ge(S(L + name + "_rstd"), n + 1)
            dve.scalar_tensor_tensor(X[:, t, :], YY[:, t, :], rstd[:, c + n:c + n + 1], X[:, t, :], ALU.mult,
                                     ALU.add).then_inc(S(L + name + "_added"), 1)

    def x_ready(l, which):
        def wait(eng, t):
            if which == 0 and l == 0:
                eng.wait_ge(S("x_loaded"), 16 * 2)
            else:
                eng.wait_ge(S(("L%d_ffn_added" % (l - 1)) if which == 0 else "L%d_y_added" % l), t + 1)
        return wait

    st = ExitStack()
    block1 = st.enter_context(nc.Block())

    @block1.tensor
    def _(pe):
        T = Tensor(pe)

        def turn_params(src, key, loaded):
            pe.wait_ge(S("params_loaded"), 16 * loaded)
            T.open(key)
            rows_ = src.shape[0]
            T.close(pe.transpose(bank(key)[:, 0:rows_], src, ident[0:rows_, 0:rows_]), key)

        pe.wait_ge(S("consts"), 16 * 2)
        pe.wait_ge(S("c_loaded"), 16 * 2)
        T.open(("c",))
        T.close(pe.transpose(bank(("c",))[:, 0:2 * KT], stage_c, ident[0:2 * KT, 0:2 * KT]), ("c",))
        pe.wait_ge(S("silu_c"), 1)
        for q in range(GROUP * len(phases["start"])):
            mod_pe(T, pe, "start", q)
        turn_params(stage_mod, ("cols", 2, 0), PARAM_LOADS)
        for l in range(DEPTH):
            for m in range(2):
                turn_params(stage[:, l, m, :], ("cols", l, m), PARAM_LOADS)
        turn_params(stage_norms, ("cols", 3, 0), PARAM_LOADS)
        mod_turn(T, pe, phases["start"][-1])
        pe.wait_ge(S("swaps_loaded"), 16)
        for l in range(DEPTH):
            ns, n, tiles = layer_tokens(l)
            L = "L%d_" % l
            norm_pe(T, pe, L + "n1", [0, 1, 2, 3])
            norm_wait(pe, L + "n1", [0, 1, 2, 3])
            w_in = A["w_in"][l]
            own = both((HH, HL), n)
            for j in range(NCH):
                for nm, c0 in (("glu_gate", CONV_CH), ("glu", 0)):
                    i, ws = T.load(rows(w_in, 0, KT, c0 + j * P, P), (KT, P))
                    tile_t(T, pe, (L + nm, j), ws, KT, 0, own, n)
                    T.used(i)
            product_t(T, pe, L + "pool", w_in, COL_P, 4, KT, own, n)

            def turn_q(j):
                if j >= 1:
                    rope_pe(T, pe, L + "q", j - 1, QT[:, j - 1, 0:SEQ], swaps[:, 0, :])

            def turn_k(j):
                if j == 0:
                    rope_pe(T, pe, L + "q", 7, QT[:, 7, 0:SEQ], swaps[:, 0, :])
                else:
                    rope_pe(T, pe, L + "k", j - 1, KTT[:, j - 1, 0:SEQ], swaps[:, 0, :])

            product_t(T, pe, L + "q", w_in, COL_Q, 8, KT, own, n, before=turn_q)
            product_t(T, pe, L + "k", w_in, COL_K, 8, KT, both((HH, HL), 2 * SEQ), 2 * SEQ, before=turn_k)
            rope_pe(T, pe, L + "k", 7, KTT[:, 7, 0:SEQ], swaps[:, 0, :])
            product(T, pe, L + "v", w_in[:, COL_V:COL_P], KT, D, [0, 1, 2, 3], lefts((HH, HL)))
            pe.wait_ge(S(L + "conv"), NCH)
            ps = T.open((L + "mean",))
            for j in range(NCH):
                ins = pe.matmul(ps[:, 0:n], ones[:, :], CV[:, j, 0:ns, :], start=(j == 0), stop=(j == NCH - 1))
            T.close(ins, (L + "mean",))
            pe.wait_ge(S(L + "pooled"), 4)
            i, ws = T.load(A["w_pool_group"][l].rearrange("g c d -> c g d"), (4, P), split=False)
            for g in range(4):
                ps = T.open((L + "mixed", g))
                ins = pe.matmul(ps[:, 0:n], ws[:, g, :], PP[:, g, 0:ns, POOL_PAD:POOL_PAD + SEQ], start=True, stop=True)
                T.close(ins, (L + "mixed", g))
            T.used(i)
            us = units_of[l]
            pe.wait_ge(S(L + "q_roped"), 8)
            pe.wait_ge(S(L + "k_roped"), 8)
            for j in range(4, 8):
                wait_read(pe, (L + "k", j))
            for t in range(4):
                wait_read(pe, (L + "v", 1, t))
                wait_read(pe, (L + "v", 0, t))

            def blocks(t):
                return [0, 1, 2, 3] if t < 2 else [2, 3]

            for i in range(len(us) + 3):
                if i < len(us):
                    t, h = us[i]
                    k0, k1 = (0, 2 * SEQ) if t < 2 else (SEQ, 2 * SEQ)
                    for m in range(2):
                        ps = T.open((L + "s", i, m))
                        T.close(pe.matmul(ps[:, 0:k1 - k0], QT[64 * m:64 * m + 64, h, t * P:(t + 1) * P],
                                          KTT[64 * m:64 * m + 64, h, k0:k1], start=True, stop=True), (L + "s", i, m))
                if i == 1:
                    pe.wait_ge(S(L + "conv_sq"), NCH)
                    ps = T.open((L + "var",))
                    for j in range(NCH):
                        ins = pe.matmul(ps[:, 0:n], ones[:, :], UP[:, j, 0:ns, HALF_W:HALF_W + SEQ], start=(j == 0), stop=(j == NCH - 1))
                    T.close(ins, (L + "var",))
                if 2 <= i < len(us) + 2:
                    t, h = us[i - 2]
                    pe.wait_ge(S(L + "probs"), i - 1)
                    ps = T.open((L + "pt", i - 2))
                    for b in range(len(blocks(t))):
                        ins = pe.transpose(ps[:, b * P:(b + 1) * P], AA[:, i % 2, b * P:(b + 1) * P], ident[:, :])
                    T.close(ins, (L + "pt", i - 2))
                if i >= 3:
                    t, h = us[i - 3]
                    wait_read(pe, (L + "pt", i - 3))
                    ps = T.open((L + "o", i - 3))
                    for b, kb in enumerate(blocks(t)):
                        ins = pe.matmul(ps[:, 0:V_DIM], AT[:, (i - 3) % 2, b * P:(b + 1) * P], V[:, kb, h * V_DIM:(h + 1) * V_DIM],
                                        start=(b == 0), stop=(b == len(blocks(t)) - 1))
                    T.close(ins, (L + "o", i - 3))
            def branch(name, number, gate_col, w, kts, pair, ready):
                for j in range(KT):
                    i, ws = T.load(rows(w_in, 0, KT, COL_G + gate_col * D + j * P, P), (KT, P))
                    tile_t(T, pe, (name + "_gate", j), ws, KT, 0, own, n)
                    T.used(i)
                    if j == 0:
                        ready()
                    iy, wy = T.load(rows(w, 0, kts, j * P, P), (kts, P))
                    tile_t(T, pe, (name, j), wy, kts, 0, both(pair, n), n)
                    T.used(iy)
                    mod_pe(T, pe, L + "branches", KT * number + j)

            branch(L + "yc", 0, 2, A["w_pool_out"][l], 4, MIX, lambda: pe.wait_ge(S(L + "mixed_parts"), 4))
            branch(L + "ya", 1, 0, A["w_conv_out"][l], 4, CS, lambda: pe.wait_ge(S(L + "conv_parts"), NCH))
            gates_pe(T, pe, l, 0)
            for t in tiles:
                pe.wait_ge(S(L + "o_normed"), t + 1)
                transposes(T, pe, L + "ot", t, O[:, t, :])
            branch(L + "yb", 2, 1, A["w_attn_out"][l], 8, (OTH, OTL), lambda: pe.wait_ge(S(L + "ot_parts"), 2 * len(tiles)))
            mod_turn(T, pe, phases[L + "branches"][-1])
            pe.wait_ge(S(L + "merged"), KT)
            product(T, pe, L + "y", A["w_out"][l], KT, D, tiles, lefts((MTH, MTL)))

            def then():
                if L + "ffn" in phases:
                    mod_turn(T, pe, phases[L + "ffn"][-1])
                gates_pe(T, pe, l, 1)

            ffn_pe(T, pe, L, A["w_ffn_in"][l], A["w_ffn_out"][l], tiles, n, (UH, UL), lambda p: mod_pe(T, pe, L + "ffn", p), then)

    @block1.scalar
    def _(act):
        for m, nm in enumerate(("c", "c_ctx")):
            src = A[nm] if nm == "c_ctx" else A[nm][0]
            act.dma_start(stage_c[KT * m:KT * m + KT, :], src.rearrange("(r p) -> r p", p=P)).then_inc(S("c_loaded"), 16)
        act.wait_ge(pe_done, milestones[("c",)])
        read_out(act.activation(silu_f[:, :, :].rearrange("p k m -> p m k"), bank(("c",))[:, 0:2 * KT].rearrange("p (m k) -> p m k", m=2),
                                ACT.Silu), ("c",))
        for q in range(GROUP * len(phases["start"])):
            mod_act(act, "start", q)
        for l, m in ((2, 0), (0, 0), (0, 1), (1, 0), (1, 1), (3, 0)):
            key = ("cols", l, m)
            dst = cols2[:, :] if l == 3 else cols_mod[:, :] if l == 2 else cols[:, l, m, :]
            wait_result(act, key)
            read_out(act.activation(dst, bank(key)[:, 0:dst.shape[-1]], ACT.Copy), key)
        keep_splitting(act, ("turn",) + phases["start"][-1])
        for l in range(DEPTH):
            ns, n, tiles = layer_tokens(l)
            L = "L%d_" % l
            keep_splitting(act, ("turn", l, SCALE_1, 1))
            act.wait_ge(S(L + "gains"), 1)
            norm_act(act, L + "n1", lambda t: X[:, t, :], [0, 1, 2, 3], HF, lambda k, t: gain[:, l, 0, k, t // 2:t // 2 + 1],
                     lambda k, t: mod[:, l, SHIFT_1, k, t // 2:t // 2 + 1], x_ready(l, 0))
            if l == 0:
                for m in range(DEPTH):
                    act.wait_ge(S("lam_sums"), m + 1)
                    act.activation(lams[:, m, 2:4], lams[:, m, 0:2], ACT.Exp).then_inc(S("lam_exps"), 1)
            for j in range(NCH):
                key = (L + "glu_gate", j)
                wait_result(act, key)
                if j >= 2:
                    wait_read(act, (L + "glu", j - 2))
                read_out(act.activation(SG[:, j % 2, 0:n], bank(key)[:, 0:n], ACT.Sigmoid), key)
            for j in range(4):
                key = (L + "pool", j)
                wait_result(act, key)
                read_out(act.activation(PP[:, j, 0:ns, POOL_PAD:POOL_PAD + SEQ], bank(key)[:, 0:n].rearrange("p (s t) -> p s t", s=ns), ACT.Copy), key)
            for nm, dst, w in (("q", QT, n), ("k", KTT, 2 * SEQ)):
                for j in range(8):
                    key = (L + nm, j)
                    wait_result(act, key)
                    read_out(act.activation(dst[:, j, 0:w], bank(key)[:, 0:w], ACT.Copy, scale=-SCALE if nm == "q" else 1.0), key)
            for nn in range(2):
                for t in range(4):
                    key = (L + "v", nn, t)
                    wait_result(act, key)
                    read_out(act.activation(V[:, t, nn * 512:(nn + 1) * 512], bank(key), ACT.Copy), key)
            for g in range(4):
                key = (L + "mixed", g)
                wait_result(act, key)
                read_out(act.activation(PP[:, g, 0:ns, POOL_PAD:POOL_PAD + SEQ], bank(key)[:, 0:n].rearrange("p (s t) -> p s t", s=ns), ACT.Copy,
                                        scale=cols[:, l, 0, ROW_PS + g:ROW_PS + g + 1]), key)
            us = units_of[l]
            for i in range(len(us) + 4):
                if i == 3:
                    wait_read(act, (L + "var",))
                    act.activation(XN[:, 0, 0:n], XN[:, 0, 0:n], ACT.Sqrt).then_inc(S(L + "std"), 1)
                if i == 6:
                    for j in range(NCH):
                        act.wait_ge(S(L + "conv_normed"), j + 1)
                        act.activation(CV[:, j, 0:ns, :], CV[:, j, 0:ns, :], ACT.Silu, scale=cols[:, l, 0, ROW_LG + j:ROW_LG + j + 1],
                                       bias=cols[:, l, 0, ROW_LB + j:ROW_LB + j + 1]).then_inc(S(L + "conv_act"), 1)
                if i < len(us):
                    t, h = us[i]
                    w = 2 * SEQ if t < 2 else SEQ
                    act.wait_ge(S(L + "maxes"), i + 1)
                    if i >= 2:
                        act.wait_ge(S(L + "probs"), i - 1)
                    for m in range(2):
                        key = (L + "s", i, m)
                        read_out(act.activation(E2[:, i % 2, m, 0:w], bank(key)[:, 0:w], ACT.Exp, bias=mx[:, i % 2, m:m + 1],
                                                scale=-1.0, accum_out=mx[:, i % 2, 4 + m:5 + m]), key)
                if 2 <= i < len(us) + 2:
                    w = 2 * SEQ if us[i - 2][0] < 2 else SEQ
                    key = (L + "pt", i - 2)
                    wait_result(act, key)
                    if i >= 4:
                        wait_result(act, (L + "o", i - 4))
                    read_out(act.activation(AT[:, i % 2, 0:w], bank(key)[:, 0:w], ACT.Copy), key)
                if i >= 4:
                    t, h = us[i - 4]
                    key = (L + "o", i - 4)
                    wait_result(act, key)
                    read_out(act.activation(O[:, t, h * V_DIM:(h + 1) * V_DIM], bank(key)[:, 0:V_DIM], ACT.Copy), key)
            done = 0
            for nm, gc in (("yc", 2), ("ya", 0), ("yb", 1)):
                if nm == "yb":
                    for t in tiles:
                        for g in range(2):
                            key = (L + "ot", t, g)
                            wait_result(act, key)
                            if t:
                                act.wait_ge(S(L + "ot_parts"), 2 * t - 1 + g)
                            read_out(act.activation(OF[:, g, :], bank(key), ACT.Copy, scale=sub_g[:, l:l + 1]), key)
                for j in range(KT):
                    key = (L + nm + "_gate", j)
                    wait_result(act, key)
                    if done >= 2:
                        wait_read(act, (L + ("yc", "ya", "yb")[(done - 2) // KT], (done - 2) % KT))
                    c = ROW_GATE + 8 * gc + j
                    read_out(act.activation(SG[:, done % 2, 0:n], bank(key)[:, 0:n], ACT.Sigmoid, bias=cols[:, l, 0, c:c + 1]), key)
                    done += 1
                    mod_act(act, L + "branches", done - 1)
                if nm == "ya":
                    gates_act(act, l, 0)
            wait_result(act, ("turn",) + phases[L + "branches"][-1])
            post_act(act, L, "y", tiles)
            keep_splitting(act, ("turn", l, SCALE_2, 1))
            act.wait_ge(S(L + "gains"), 2)
            norm_act(act, L + "n2", lambda t: X[:, t, :], tiles, HF, lambda k, t: gain[:, l, 1, k, t // 2:t // 2 + 1],
                     lambda k, t: mod[:, l, SHIFT_2, k, t // 2:t // 2 + 1], x_ready(l, 1))
            ffn_act(act, L, n, UT, lambda p: mod_act(act, L + "ffn", p))
            gates_act(act, l, 1)
            post_act(act, L, "ffn", tiles)

    @block1.gpsimd
    def _(pool):
        pool.memset(TMP[:, 0:512], 0.0).then_inc(S("zeroed"), 1)
        for l in range(DEPTH):
            for m, v in enumerate(("lam_q1", "lam_k1", "lam_q2", "lam_k2")):
                pool.dma_start(lamv[:, l, m, :], A[v][l:l + 1, :].broadcast_to([P, 64])).then_inc(S("lam_loaded"), 16)
        pool.dma_start(swaps[:], A["swaps"]).then_inc(S("swaps_loaded"), 16)
        pool.memset(ones[:], 1.0).then_inc(S("filled"), 1)
        pool.memset(half[:], -0.5).then_inc(S("filled"), 1)
        pool.memset(UP[:], 0.0).then_inc(S("filled"), 1)
        pool.memset(PP[:], 0.0).then_inc(S("filled"), 1)
        pool.wait_ge(S("filled"), 4)
        pool.wait_ge(S("zeroed"), 1)

        for l in range(DEPTH):
            ns, n, tiles = layer_tokens(l)
            L = "L%d_" % l
            if l:
                wait_result(pool, ("L%d_ffn" % (l - 1), 1, layer_tokens(l - 1)[2][-1]))
                pool.memset(UP[:], 0.0).then_inc(S("filled"), 1)
                pool.memset(PP[:], 0.0).then_inc(S("filled"), 1)
            pool.dma_start(grid, A["grid_rope"]).then_inc(S("grid_loaded"), 16)
            pool.dma_start(counts, A["inv_counts"]).then_inc(S("counts_loaded"), 16)
            rstd_pool(pool, L + "n1", [0, 1, 2, 3], D, "_rstd")
            if l == DEPTH - 1:
                norm_wait(pool, L + "n1", [0, 1, 2, 3])
                pool.dma_start(X[:, 2:4, :], A["mem_2"][0].rearrange("(t p) d -> p t d", p=P)).then_inc(S("mem_loaded"), 16)
            pool.wait_ge(S("counts_loaded"), 16 * (l + 1))
            pool.wait_ge(S("filled"), 4 + 2 * l)
            for g in range(4):
                wait_read(pool, (L + "pool", g))
                if g:
                    pool.wait_ge(S(L + "pooled"), g)
                src = PP[:, g, 0:ns, :]
                lo, hi, off = 0, SEQ + 2 * POOL_PAD, 1
                for step in range(g + 1):
                    dst = PT[:, step % 2, 0:ns, :]
                    a, b = (1, 0) if step == 0 else (2 ** (step - 1), 2 ** (step - 1))
                    lo, hi = lo + a, hi - b
                    pool.tensor_tensor(dst[:, :, lo:hi], src[:, :, lo - a:hi - a], src[:, :, lo + b:hi + b], ALU.add).then_inc(pool_step, 1)
                    count["pool"] += 1
                    pool.wait_ge(pool_step, count["pool"])
                    src = dst
                mid = PT[:, g % 2, 0:ns, POOL_PAD:POOL_PAD + SEQ]
                inside = PP[:, g, 0:ns, POOL_PAD:POOL_PAD + SEQ]
                for s in range(ns):
                    pool.tensor_tensor(mid[:, s, :], mid[:, s, :], counts[:, g, :], ALU.mult).then_inc(pool_step, 1)
                    count["pool"] += 1
                pool.wait_ge(pool_step, count["pool"])
                pool.tensor_tensor(inside, mid, inside, ALU.subtract).then_inc(S(L + "pooled"), 1)
            pool.wait_ge(S("grid_loaded"), 16 * (l + 1))
            for i, (nm, j) in enumerate(ROPES):
                key = (L + nm + "_rot", j)
                x = (QT if nm == "q" else KTT)[:, j, 0:SEQ]
                wait_result(pool, key)
                pool.tensor_tensor(x, x, grid[:, 0, :], ALU.mult).then_inc(pool_step, 1)
                count["pool"] += 1
                pool.wait_ge(pool_step, count["pool"])
                wait_read(pool, key)
                pool.tensor_tensor(x, x, rope_tmp[:, i % 4, :], ALU.add).then_inc(S(L + nm + "_roped"), 1)
            for t in tiles:
                pool.wait_ge(S(L + "o_squares"), t + 1)
                pool.tensor_tensor(subs[:, 2, t, :], subs[:, 1, t, :], half[:, 0:8], ALU.pow).then_inc(S(L + "o_rstd"), 1)
            post_pool(pool, L, "y", tiles)
            rstd_pool(pool, L + "n2", tiles, D, "_rstd")
            post_pool(pool, L, "ffn", tiles)

    @block1.vector
    def _(dve):
        dve.wait_ge(bank_read[uses[("c",)][0]], 1)
        split_value(dve, silu_c[:, :, 0:2], silu_c[:, :, 2:4], silu_f[:, :, :]).then_inc(S("silu_c"), 1)
        dve.wait_ge(S("consts"), 16 * 2)
        split_until(dve, GROUP)
        dve.wait_ge(S("lam_loaded"), 16 * 8)
        for l in range(DEPTH):
            for m in range(2):
                dve_link(dve, dve.tensor_tensor(lamv[:, l, 2 * m, :], lamv[:, l, 2 * m, :], lamv[:, l, 2 * m + 1, :], ALU.mult))
            dve.tensor_reduce(lams[:, l, 0:2], lamv[:, l, 0:4:2, :], AX_X, ALU.add).then_inc(S("lam_sums"), 1)
        wait_read(dve, ("cols", 2, 0))
        wait_read(dve, ("cols", 0, 0))
        for group in phases["start"]:
            mod_columns(dve, group)
        wait_read(dve, ("cols", 1, 0))
        wait_read(dve, ("cols", 3, 0))
        dve.wait_ge(S("filled"), 4)
        for l in range(DEPTH):
            ns, n, tiles = layer_tokens(l)
            L = "L%d_" % l
            norm_dve(dve, L + "n1", lambda t: X[:, t, :], [0, 1, 2, 3], HF, lambda k, t: gain[:, l, 0, k, t // 2:t // 2 + 1],
                     lambda k, t: mod[:, l, SHIFT_1, k, t // 2:t // 2 + 1], x_ready(l, 0))
            if l == 0:
                for m in range(DEPTH):
                    lam_init = 0.8 - 0.6 * math.exp(-0.3 * m)
                    dve.wait_ge(S("lam_exps"), m + 1)
                    dve_link(dve, dve.tensor_tensor(lams[:, m, 4:5], lams[:, m, 3:4], lams[:, m, 2:3], ALU.subtract))
                    dve_link(dve, dve.tensor_scalar(lams[:, m, 5:6], lams[:, m, 4:5], -lam_init, None, ALU.add))
                    dve_link(dve, dve.tensor_scalar(sub_g[:, m:m + 1], cols[:, m, 0, ROW_SUB:ROW_SUB + 1], 1.0 - lam_init, None, ALU.mult))
                    wait_read(dve, ("cols", m, 1))
            dve.wait_ge(S("filled"), 4 + 2 * l)
            dve.wait_ge(S("grid_loaded"), 16 * (l + 1))
            for j in range(NCH):
                key = (L + "glu", j)
                wait_read(dve, (L + "glu_gate", j))
                wait_result(dve, key)
                read_out(dve.tensor_tensor(UP[:, j, 0:ns, HALF_W:HALF_W + SEQ], bank(key)[:, 0:n].rearrange("p (s t) -> p s t", s=ns),
                                           SG[:, j % 2, 0:n].rearrange("p (s t) -> p s t", s=ns), ALU.mult), key)
            for j in range(NCH):
                wait_read(dve, (L + "glu", j))
            ropes = list(ROPES)

            def rope_sin(nm, j):
                key = (L + nm + "_rot", j)
                i = ROPES.index((nm, j))
                wait_result(dve, key)
                if i >= 4:
                    nm2, j2 = ROPES[i - 4]
                    dve.wait_ge(S(L + nm2 + "_roped"), j2 + 1)
                read_out(dve.tensor_tensor(rope_tmp[:, i % 4, :], bank(key)[:, 0:SEQ], grid[:, 1, :], ALU.mult), key)

            last = [0] * NCH
            for tap in range(CONV_W):
                for j in range(NCH):
                    wt = cols[:, l, 1, tap * NCH + j:tap * NCH + j + 1]
                    src = UP[:, j, 0:ns, tap:tap + SEQ]
                    if tap == 0:
                        ins = dve.tensor_scalar(CV[:, j, 0:ns, :], src, wt, cols[:, l, 0, ROW_CB + j:ROW_CB + j + 1], ALU.mult, ALU.add)
                    else:
                        dve.wait_ge(dve_step, last[j])
                        ins = dve.scalar_tensor_tensor(CV[:, j, 0:ns, :], src, wt, CV[:, j, 0:ns, :], ALU.mult, ALU.add)
                    if tap < CONV_W - 1:
                        count["dve"] += 1
                        last[j] = count["dve"]
                        ins.then_inc(dve_step, 1)
                    else:
                        ins.then_inc(S(L + "conv"), 1)
                if tap < 5:
                    split_until(dve, chunk_of[(L + "glu", NCH - 1)] + AHEAD + (tap + 1) // 2)
                elif tap % 2 == 1:
                    rope_sin(*ropes.pop(0))
            for nm, j in ropes:
                rope_sin(nm, j)
            key = (L + "mean",)
            wait_result(dve, key)
            dve.wait_ge(S(L + "pooled"), 4)
            dve_link(dve, dve.tensor_scalar(XN[:, 0, 0:n], bank(key)[:, 0:n], -1.0 / CONV_CH, None, ALU.mult))
            for j in range(NCH):
                ins = dve.tensor_tensor(CV[:, j, 0:ns, :], CV[:, j, 0:ns, :], XN[:, 0, 0:n].rearrange("p (s t) -> p s t", s=ns), ALU.add)
                if j == NCH - 1:
                    read_out(ins, key)
                    wait_read(dve, key)
                else:
                    dve_link(dve, ins)
            for j in range(NCH):
                dve.tensor_tensor(UP[:, j, 0:ns, HALF_W:HALF_W + SEQ], CV[:, j, 0:ns, :], CV[:, j, 0:ns, :], ALU.mult).then_inc(S(L + "conv_sq"), 1)
            us = units_of[l]

            def maxes(i):
                t, h = us[i]
                w = 2 * SEQ if t < 2 else SEQ
                for m in range(2):
                    wait_result(dve, (L + "s", i, m))
                    ins = dve.tensor_reduce(mx[:, i % 2, m:m + 1], bank((L + "s", i, m))[:, 0:w], AX_X, ALU.min)
                ins.then_inc(S(L + "maxes"), 1)

            def probs(i):
                w = 2 * SEQ if us[i][0] < 2 else SEQ
                for m in range(2):
                    wait_read(dve, (L + "s", i, m))
                dve_link(dve, dve.reciprocal(mx[:, i % 2, 6:8], mx[:, i % 2, 4:6]))
                if i >= 2:
                    wait_result(dve, (L + "pt", i - 2))
                dve_link(dve, dve.tensor_scalar(AA[:, i % 2, 0:w], E2[:, i % 2, 1, 0:w], mx[:, i % 2, 7:8], lams[:, l, 5:6], ALU.mult, ALU.mult))
                dve.scalar_tensor_tensor(AA[:, i % 2, 0:w], E2[:, i % 2, 0, 0:w], mx[:, i % 2, 6:7], AA[:, i % 2, 0:w],
                                         ALU.mult, ALU.add).then_inc(S(L + "probs"), 1)

            flat = lambda v: v.rearrange("p (s t) -> p s t", s=ns)
            for i in range(len(us) + 1):
                if i < len(us):
                    maxes(i)
                if i == 2:
                    key = (L + "var",)
                    wait_result(dve, key)
                    read_out(dve.tensor_scalar(XN[:, 0, 0:n], bank(key)[:, 0:n], 1.0 / CONV_CH, EPS, ALU.mult, ALU.add), key)
                if i >= 1:
                    probs(i - 1)
                if i == 4:
                    dve.wait_ge(S(L + "std"), 1)
                    dve_link(dve, dve.reciprocal(XN[:, 1, 0:n], XN[:, 0, 0:n]))
                    for j in range(NCH):
                        dve.tensor_tensor(CV[:, j, 0:ns, :], CV[:, j, 0:ns, :], XN[:, 1, 0:n].rearrange("p (s t) -> p s t", s=ns),
                                          ALU.mult).then_inc(S(L + "conv_normed"), 1)
            for g in range(4):
                wait_read(dve, (L + "mixed", g))
                split_value(dve, flat(MIX[0][:, g, 0:n]), flat(MIX[1][:, g, 0:n]),
                            PP[:, g, 0:ns, POOL_PAD:POOL_PAD + SEQ]).then_inc(S(L + "mixed_parts"), 1)

            def conv_parts(j):
                dve.wait_ge(S(L + "conv_act"), j + 1)
                split_value(dve, flat(CS[0][:, j, 0:n]), flat(CS[1][:, j, 0:n]), CV[:, j, 0:ns, :]).then_inc(S(L + "conv_parts"), 1)

            sq = TMP[:, 2048:3072]

            def head_norms(t):
                for h in range(HEADS):
                    i = t * HEADS + h
                    wait_read(dve, (L + "o", i))
                dve_link(dve, dve.tensor_tensor(sq, O[:, t, :], O[:, t, :], ALU.mult))
                dve_link(dve, dve.tensor_reduce(subs[:, 0, t, :], sq.rearrange("p (h d) -> p h d", h=HEADS), AX_X, ALU.add))
                dve.tensor_scalar(subs[:, 1, t, :], subs[:, 0, t, :], 1.0 / V_DIM, EPS, ALU.mult, ALU.add).then_inc(S(L + "o_squares"), 1)
                dve.wait_ge(S(L + "o_rstd"), t + 1)
                yv = O[:, t, :].rearrange("p (h d) -> p h d", h=HEADS)
                dve.tensor_tensor(yv, yv, subs[:, 2, t, :].rearrange("p (h o) -> p h o", o=1).broadcast_to([P, HEADS, V_DIM]),
                                  ALU.mult).then_inc(S(L + "o_normed"), 1)
            wait_result(dve, (L + "o", len(us) - 1))
            others = [lambda j=j: conv_parts(j) for j in range(NCH)] + [lambda t=t: head_norms(t) for t in tiles]
            done = 0
            for nm in ("yc", "ya", "yb"):
                if nm == "yb":
                    for t in tiles:
                        for g in range(2):
                            wait_read(dve, (L + "ot", t, g))
                            to = (slice(None), slice(4 * g, 4 * g + 4), slice(t * P, (t + 1) * P))
                            split_value(dve, OTH[to], OTL[to], OF[:, g, :].rearrange("p (k c) -> p k c", k=4)).then_inc(S(L + "ot_parts"), 1)
                for j in range(KT):
                    key = (L + nm, j)
                    wait_result(dve, key)
                    wait_read(dve, (L + nm + "_gate", j))
                    if nm == "yc":
                        read_out(dve.tensor_tensor(MT[:, j, 0:n], bank(key)[:, 0:n], SG[:, done % 2, 0:n], ALU.mult), key)
                    else:
                        read_out(dve.tensor_tensor(GY[:, done % 2, 0:n], bank(key)[:, 0:n], SG[:, done % 2, 0:n], ALU.mult), key)
                        wait_read(dve, key)
                        wait_read(dve, (L + "yc", j))
                        dve_link(dve, dve.tensor_tensor(MT[:, j, 0:n], MT[:, j, 0:n], GY[:, done % 2, 0:n], ALU.add))
                    if nm == "yb":
                        split_value(dve, MTH[:, j, 0:n], MTL[:, j, 0:n], MT[:, j, 0:n]).then_inc(S(L + "merged"), 1)
                    done += 1
                    mod_dve(dve, L + "branches", done - 1)
                    if others:
                        others.pop(0)()
                if nm == "ya":
                    gates_dve(dve, l, 0)
            mod_columns(dve, phases[L + "branches"][-1])
            post_dve(dve, L, "y", tiles, 0)
            norm_dve(dve, L + "n2", lambda t: X[:, t, :], tiles, HF, lambda k, t: gain[:, l, 1, k, t // 2:t // 2 + 1],
                     lambda k, t: mod[:, l, SHIFT_2, k, t // 2:t // 2 + 1], x_ready(l, 1))
            ffn_dve(dve, L, n, UT, (UH, UL), lambda p: mod_dve(dve, L + "ffn", p))
            if L + "ffn" in phases:
                mod_columns(dve, phases[L + "ffn"][-1])
            gates_dve(dve, l, 1)
            post_dve(dve, L, "ffn", tiles, 1)

    def load_chunks(sp, first, others={}):
        for i in range(first, len(chunks)):
            c = chunks[i]
            if i in others:
                others[i]()
            if i - RAW[now["block"]] >= first:
                before = chunks[i - RAW[now["block"]]]
                if before["split"] is None:
                    sp.wait_ge(pe_done, before["free"])
                else:
                    sp.wait_ge(low_done, before["split"] + 1)
            w = c["shape"][1] // len(c["pieces"])
            for m, piece in enumerate(c["pieces"]):
                sp.dma_start(c["raw"][:, :, m * w:(m + 1) * w], piece).then_inc(slot_full[c["slot"]], 16)

    @block1.sync
    def _(sp):
        sp.dma_start(ident[:, :], A["ident"]).then_inc(S("consts"), 16)
        sp.dma_start(pick[:], A["pick"]).then_inc(S("consts"), 16)

        def load_x():
            sp.dma_start(X[:, 0:2, :], A["x"][0].rearrange("(t p) d -> p t d", p=P)).then_inc(S("x_loaded"), 16)
            sp.dma_start(X[:, 2:4, :], A["ctx"][0].rearrange("(t p) d -> p t d", p=P)).then_inc(S("x_loaded"), 16)

        def load_params(some):
            def start():
                sp.wait_ge(S("zeroed"), 1)
                for dst, src in some:
                    sp.dma_start(dst, src).then_inc(S("params_loaded"), 16)
            return start

        params = param_loads()
        others = {RAW[0] + i: load_params(params[3 * i:3 * i + 3]) for i in range(len(params) // 3)}
        others[4 * GROUP] = load_x
        load_chunks(sp, 0, others)

    st.close()
    now.update(block=1, chunk0=len(chunks), split0=len(splits))
    place[0] = common_end
    rings.append(weight_rings(1))
    NM, MD = 4, 4 * HEAD_DIM
    FN = sb("FN", [P, D])
    causal = sb("causal", [P, 2, SEQ])
    dilated = sb("dilated", [P, 2, 3, SEQ])
    freqs = sb("freqs", [P, 2])
    table = sb("table", [P, 4, SEQ])
    RL = sb("RL", [P, 2, SEQ])
    WI = sb("WI", [P, 2, IDX_HEADS])
    SC = sb("SC", [P, 2, SEQ])
    TOP = sb("TOP", [P, 2, 8])
    MASK = sb("MASK", [P, 2, SEQ])
    UT2 = over(place[0], "UT2", [P, 2, 2, SEQ])
    RT = over(place[0], "RT", [P, 2, SEQ])
    SM = sb("SM", [P, 3, 3 * SEQ])
    ET = sb("ET", [P, 2, 3 * SEQ])
    mz = sb("mz", [P, 6, 4])
    HF2 = sb("HF2", [P, 2, 512])
    UH2 = over(place[0], "UH2", [P, FT, SEQ], F32R)
    UL2 = over(place[0] + FT * SEQ * 4, "UL2", [P, FT, SEQ], F32R)
    Q2 = sb("Q2", [P, 12, SEQ])
    K2 = sb("K2", [P, 8, SEQ])
    V2 = sb("V2", [P, 8, SEQ])
    angle = over(place[0] + 4 * P, "angle", [P, 4, SEQ])
    turns = over(place[0] + 4 * P + 16 * SEQ, "turns", [P, 4, SEQ])
    pos_i = over(place[0] + 4 * P + 32 * SEQ, "pos_i", [P, SEQ], I32)
    pos = over(place[0] + 4 * P + 36 * SEQ, "pos", [P, SEQ])
    Y = sb("Y", [P, 2, D])
    O2H = sb("O2H", [P, 8, SEQ], F32R)
    O2L = sb("O2L", [P, 8, SEQ], F32R)
    KI = K2[:, 2, :]

    def q_slot(h):
        g = h // 3
        return 64 * (g % 2), (h % 3) + 3 * (g // 2), g

    def attention_units(e):
        us = []
        mem_q, mem_k = (10, 4) if e == 0 else (6, 6)
        for t in range(2):
            for h in range(NM):
                b = 64 * (h % 2)
                part = (Q2[b:b + 64, mem_q + h // 2, t * P:(t + 1) * P], K2[b:b + 64, mem_k + h // 2, :], SEQ)
                c = (768 if e == 0 else 256) + h * 64
                us.append((c, t, [part], [None], [V2[:, 6 + kb, h * 64:(h + 1) * 64] for kb in range(2)]))
        for t in range(2):
            w = (t + 1) * P
            if e == 0:
                for h in range(12):
                    b, j, g = q_slot(h)
                    part = (Q2[b:b + 64, j, t * P:(t + 1) * P], K2[b:b + 64, g // 2, 0:w], w)
                    us.append((h * 64, t, [part], [MASK[:, t, 0:w]], [V2[:, kb, g * 64:(g + 1) * 64] for kb in range(t + 1)]))
            else:
                for h in range(4):
                    b = 64 * (h % 2)
                    parts = [(Q2[b:b + 64, 2 * g + h // 2, t * P:(t + 1) * P], K2[b:b + 64, 2 * g + h // 2, 0:w], w) for g in range(3)]
                    us.append((h * 64, t, parts, [dilated[:, t, g, 0:w] for g in range(3)],
                               [V2[:, 2 * g + kb, h * 64:(h + 1) * 64] for g in range(3) for kb in range(t + 1)]))
        return us

    PROJ = [
        [("qi", 1280, 4, Q2, 6, 2), ("ki", 1792, 1, K2, 2, 2), ("qm", 1864, 2, Q2, 10, None), ("q", 0, 6, Q2, 0, 0), ("k", 768, 2, K2, 0, 0)],
        [("q0", 0, 2, Q2, 0, 0), ("k0", 256, 2, K2, 0, 0), ("q1", 768, 2, Q2, 2, 0), ("k1", 1024, 2, K2, 2, 0),
         ("q2", 1536, 2, Q2, 4, 0), ("k2", 1792, 2, K2, 4, 0), ("qm", 2304, 2, Q2, 6, None)],
    ]
    VALUES = [[("v", 1024, 0)], [("v0", 512, 0), ("v1", 1280, 2), ("v2", 2048, 4)]]
    MEM_K = (4, 6)
    OUT_TILES = (8, 4)

    def pname(e, n):
        return A["l%d_%s_2" % (e, n)]

    def rotations(e):
        r = []
        for nm, _, n, dst, at, tab in PROJ[e]:
            if tab is not None:
                r += [(nm, j, dst[:, at + j, :], tab) for j in range(n)]
        return r

    st = ExitStack()
    block2 = st.enter_context(nc.Block())

    @block2.tensor
    def _(pe):
        T = Tensor(pe)
        own = both((HH, HL), SEQ)
        mem = lambda k: (HH[:, k, SEQ:2 * SEQ], HL[:, k, SEQ:2 * SEQ])
        for e in range(DEPTH):
            L = "E%d_" % e
            w_in = pname(e, "w_in")
            norm_pe(T, pe, L + "n1", [0, 1, 2, 3])
            norm_wait(pe, L + "n1", [0, 1, 2, 3])

            def pieces(nm):
                def of(j):
                    if nm == "ki":
                        return [rows(w_in, 0, KT, 1792, 64)] * 2
                    a = (j % 3) + 6 * (j // 3)
                    return [rows(w_in, 0, KT, h * 64, 64) for h in (a, a + 3)]
                return of if nm in ("ki", "q") else None

            def turn(group):
                for nm, n, dst, at, tab in group:
                    for j in range(n):
                        rope_pe(T, pe, L + nm, j, dst[:, at + j, :], swaps[:, 1 + (tab == 2), :])

            def values():
                for nm, c0, _ in VALUES[e]:
                    product(T, pe, L + nm, w_in[:, c0:c0 + MD], KT, MD, [0, 1], lefts((HH, HL)))

            def memory():
                product_t(T, pe, L + "km", pname(e, "w_mem_kv"), 0, 2, KT, mem, SEQ)
                product(T, pe, L + "vm", pname(e, "w_mem_kv")[:, MD:2 * MD], KT, MD, [2, 3], lefts((HH, HL)))

            pending = []
            for nm, c0, n, dst, at, tab in PROJ[e]:
                product_t(T, pe, L + nm, w_in, c0, n, KT, own, SEQ, source=pieces(nm))
                if nm == "ki":
                    i, ws = T.load(rows(w_in, 0, KT, 1856, IDX_HEADS), (KT, IDX_HEADS))
                    for t in range(2):
                        ps = T.open((L + "wi", t))
                        for k in range(KT):
                            ins = multiply(pe, ps[:, 0:IDX_HEADS], lefts((HH, HL))(k, t), cut2(ws, slice(None), k), k == 0, k == KT - 1)
                        T.close(ins, (L + "wi", t))
                    T.used(i)
                turn(pending)
                pending = [] if tab is None else [(nm, n, dst, at, tab)]
                if nm == "qm" and e == 0:
                    values()
                    memory()
                    pe.wait_ge(S(L + "qi_roped"), 4)
                    pe.wait_ge(S(L + "ki_roped"), 1)
                    for t in range(2):
                        for h in range(IDX_HEADS):
                            b = 64 * (h % 2)
                            ps = T.open((L + "is", t, h))
                            T.close(pe.matmul(ps[:, 0:(t + 1) * P], Q2[b:b + 64, 6 + h // 2, t * P:(t + 1) * P], KI[b:b + 64, 0:(t + 1) * P],
                                              start=True, stop=True), (L + "is", t, h))
            turn(pending)
            if e:
                values()
                memory()
            us = attention_units(e)
            for nm, _, n, _, _, tab in PROJ[e]:
                if tab is None:
                    for j in range(n):
                        wait_read(pe, (L + nm, j))
                else:
                    pe.wait_ge(S(L + nm + "_roped"), n)
            for j in range(2):
                wait_read(pe, (L + "km", j))
                wait_read(pe, (L + "vm", 0, 2 + j))
                for nm, _, _ in VALUES[e]:
                    wait_read(pe, (L + nm, 0, j))
            for i in range(len(us) + 3):
                if i < len(us):
                    _, _, parts, _, _ = us[i]
                    for m, (q, k, w) in enumerate(parts):
                        if m * w % 512 == 0:
                            ps = T.open((L + "s", i, m * w // 512))
                        c = m * w % 512
                        ins = pe.matmul(ps[:, c:c + w], q, k, start=True, stop=True)
                        if m == len(parts) - 1 or (m + 1) * w % 512 == 0:
                            T.close(ins, (L + "s", i, m * w // 512))
                if 2 <= i < len(us) + 2:
                    nb = len(us[i - 2][4])
                    pe.wait_ge(S(L + "exps"), i - 1)
                    for b in range(nb):
                        if b % 4 == 0:
                            ps = T.open((L + "pt", i - 2, b // 4))
                        ins = pe.transpose(ps[:, b % 4 * P:(b % 4 + 1) * P], SM[:, (i - 2) % 3, b * P:(b + 1) * P], ident[:, :])
                        if b == nb - 1 or b % 4 == 3:
                            T.close(ins, (L + "pt", i - 2, b // 4))
                if i >= 3:
                    vs = us[i - 3][4]
                    for b in range(0, len(vs), 4):
                        wait_read(pe, (L + "pt", i - 3, b // 4))
                    ps = T.open((L + "o", i - 3))
                    for b, v in enumerate(vs):
                        ins = pe.matmul(ps[:, 0:64], ET[:, (i - 3) % 2, b * P:(b + 1) * P], v, start=(b == 0), stop=(b == len(vs) - 1))
                    T.close(ins, (L + "o", i - 3))
            for t in range(2):
                for i, u in enumerate(us):
                    if u[1] == t:
                        wait_read(pe, (L + "o", i))
                for g in range(OUT_TILES[e] // 4):
                    ps = T.open((L + "ot", t, g))
                    for k in range(4):
                        ins = pe.transpose(ps[:, k * P:(k + 1) * P], Y[:, t, (4 * g + k) * P:(4 * g + k + 1) * P], ident[:, :])
                    T.close(ins, (L + "ot", t, g))
            pe.wait_ge(S(L + "ot_parts"), 2 * (OUT_TILES[e] // 4))
            product(T, pe, L + "y", pname(e, "w_out"), OUT_TILES[e], D, [0, 1], lefts((O2H, O2L)))
            ffn_pe(T, pe, L, pname(e, "w_gate_up"), pname(e, "w_down"), [0, 1], SEQ, (UH2, UL2))

    def x2_ready(e, which):
        def wait(eng, t):
            if which == 0 and e == 0:
                eng.wait_ge(S("mem_loaded"), 16)
            elif which == 0 and t >= 2:
                pass
            else:
                name = "E%d_y" % e if which else "E%d_ffn" % (e - 1)
                for nn in range(2):
                    wait_read(eng, (name, nn, t))
        return wait

    def gain2(e, which, mem_which=None):
        def col(k, t):
            c = 24 * e + 8 * (mem_which if mem_which is not None and t >= 2 else which) + k
            return cols2[:, c:c + 1]
        return col

    @block2.scalar
    def _(act):
        for e in range(DEPTH):
            L = "E%d_" % e
            norm_act(act, L + "n1", lambda t: X[:, t, :], [0, 1, 2, 3], HF2, gain2(e, 0, 1), None, x2_ready(e, 0))

            def copy(key, dst, width, scale=1.0):
                wait_result(act, key)
                read_out(act.activation(dst, bank(key)[:, 0:width], ACT.Copy, scale=scale), key)

            def copy_values():
                for nm, _, at in VALUES[e]:
                    for t in range(2):
                        copy((L + nm, 0, t), V2[:, at + t, :], MD)
                for j in range(2):
                    copy((L + "km", j), K2[:, MEM_K[e] + j, :], SEQ)
                for t in range(2):
                    copy((L + "vm", 0, 2 + t), V2[:, 6 + t, :], MD)

            for nm, _, n, dst, at, _ in PROJ[e]:
                for j in range(n):
                    copy((L + nm, j), dst[:, at + j, :], SEQ)
                if nm == "ki":
                    for t in range(2):
                        copy((L + "wi", t), WI[:, t, :], IDX_HEADS, IDX_HEADS ** -0.5 * HEAD_DIM ** -0.5)
                    act.wait_ge(S("angles"), 1)
                    act.activation(table[:], angle[:], ACT.Sin).then_inc(S("tables"), 1)
                if nm == "qm" and e == 0:
                    copy_values()
                    for t in range(2):
                        for h in range(IDX_HEADS):
                            key = (L + "is", t, h)
                            i = IDX_HEADS * t + h
                            wait_result(act, key)
                            if i >= 2:
                                act.wait_ge(S("scored"), i - 1)
                            read_out(act.activation(RL[:, i % 2, 0:(t + 1) * P], bank(key)[:, 0:(t + 1) * P], ACT.Relu), key)
            if e:
                copy_values()
            us = attention_units(e)
            for i in range(len(us) + 2):
                if i < len(us):
                    w = P * len(us[i][4])
                    act.wait_ge(S(L + "maxes"), i + 1)
                    if i >= 6:
                        wait_read(act, (L + "o", i - 6))
                    act.activation(SM[:, i % 3, 0:w], SM[:, i % 3, 0:w], ACT.Exp, bias=mz[:, i % 6, 0:1],
                                   scale=-1.0, accum_out=mz[:, i % 6, 2:3]).then_inc(S(L + "exps"), 1)
                if i >= 2:
                    nb = len(us[i - 2][4])
                    if i >= 4:
                        wait_result(act, (L + "o", i - 4))
                    for b in range(0, nb, 4):
                        key = (L + "pt", i - 2, b // 4)
                        w = P * min(4, nb - b)
                        wait_result(act, key)
                        read_out(act.activation(ET[:, i % 2, b * P:b * P + w], bank(key)[:, 0:w], ACT.Copy), key)
            for t in range(2):
                for g in range(OUT_TILES[e] // 4):
                    key = (L + "ot", t, g)
                    wait_result(act, key)
                    n = t * (OUT_TILES[e] // 4) + g
                    if n >= 2:
                        act.wait_ge(S(L + "ot_parts"), n - 1)
                    read_out(act.activation(HF2[:, n % 2, :], bank(key), ACT.Copy), key)
            norm_act(act, L + "n2", lambda t: X[:, t, :], [0, 1], HF2, gain2(e, 2), None, x2_ready(e, 1))
            ffn_act(act, L, SEQ, UT2)
        c = norm_cols("final")
        for t in range(2):
            x2_ready(2, 0)(act, t)
            act.activation(XN[:, t, :], X[:, t, :], ACT.Square, accum_out=ss[:, c + t:c + t + 1]).then_inc(S("final_squares"), 1)

    @block2.gpsimd
    def _(pool):
        for e in range(DEPTH):
            L = "E%d_" % e
            rstd_pool(pool, L + "n1", [0, 1, 2, 3], D, "_rstd")
            if e == 0:
                pool.dma_start(pos_i[:], A["positions_2"][0:1, :].broadcast_to([P, SEQ])).then_inc(S("tables_loaded"), 16)
                pool.dma_start(freqs[:], A["freqs"]).then_inc(S("tables_loaded"), 16)
                pool.dma_start(causal[:], A["causal"].rearrange("t p k -> p t k")).then_inc(S("tables_loaded"), 16)
                for t in range(2):
                    pool.dma_start(dilated[:, t, :, :], A["dilated"][t]).then_inc(S("tables_loaded"), 16)
                pool.dma_start(FN[:, :], A["final_norm_2"].rearrange("(o d) -> o d", o=1).broadcast_to([P, D])).then_inc(S("final_gain"), 16)
            rstd_pool(pool, L + "n2", [0, 1], D, "_rstd")
        rstd_pool(pool, "final", [0, 1], D, "_rstd")

    def add_rows(dve, name):
        for nn in range(2):
            for t in range(2):
                key = (name, nn, t)
                wait_result(dve, key)
                x = X[:, t, nn * 512:(nn + 1) * 512]
                read_out(dve.tensor_tensor(x, x, bank(key), ALU.add), key)

    @block2.vector
    def _(dve):
        TWO_PI_A, TWO_PI_B = 6.28125, 0.0019350051879882812
        TWO_PI_C = 2 * math.pi - TWO_PI_A - TWO_PI_B
        WHOLE = 12582912.0
        def angles():
            dve.wait_ge(S("tables_loaded"), 16 * 5)
            dve_link(dve, dve.tensor_copy(pos[:, :], pos_i[:, :]))
            for r in range(4):
                dve_link(dve, dve.tensor_scalar(angle[:, r, :], pos[:, :], freqs[:, r // 2:r // 2 + 1], None, ALU.mult))
            for r in range(2):
                ahead = 0.25 if r == 0 else 0.0
                dve_link(dve, dve.tensor_scalar(turns[:, r::2, :], angle[:, r::2, :], 0.5 / math.pi, ahead, ALU.mult, ALU.add))
            dve_link(dve, dve.tensor_scalar(turns[:], turns[:], WHOLE, None, ALU.add))
            dve_link(dve, dve.tensor_scalar(turns[:], turns[:], -WHOLE, None, ALU.add))
            for part in (TWO_PI_A, TWO_PI_B, TWO_PI_C):
                dve_link(dve, dve.scalar_tensor_tensor(angle[:], turns[:], -part, angle[:], ALU.mult, ALU.add))
            dve_link(dve, dve.tensor_scalar(angle[:, 0::2, :], angle[:, 0::2, :], 0.5 * math.pi, None, ALU.add))
            dve.tensor_scalar(angle[:], angle[:], 3.1415925, -3.1415925, ALU.min, ALU.max).then_inc(S("angles"), 1)

        for e in range(DEPTH):
            L = "E%d_" % e
            norm_dve(dve, L + "n1", lambda t: X[:, t, :], [0, 1, 2, 3], HF2, gain2(e, 0, 1), None, x2_ready(e, 0))
            def rotate(n, nm, j, x, tab):
                rope_dve(dve, L + nm, j, x, table[:, tab, :], table[:, tab + 1, :], RT[:, n % 2, :])

            turned = list(enumerate(rotations(e)))
            if e == 0:
                angles()
                split_until(dve, chunk_of[(L + "wi", 1)] + AHEAD)
                dve.wait_ge(S("tables"), 1)
                for n, r in turned[:5]:
                    rotate(n, *r)
                for t in range(2):
                    w = (t + 1) * P
                    wait_read(dve, (L + "wi", t))
                    for h in range(IDX_HEADS):
                        i = IDX_HEADS * t + h
                        wait_read(dve, (L + "is", t, h))
                        if h == 0:
                            ins = dve.scalar_tensor_tensor(SC[:, t, 0:w], RL[:, i % 2, 0:w], WI[:, t, h:h + 1], causal[:, t, 0:w], ALU.mult, ALU.add)
                        else:
                            dve.wait_ge(S("scored"), i)
                            ins = dve.scalar_tensor_tensor(SC[:, t, 0:w], RL[:, i % 2, 0:w], WI[:, t, h:h + 1], SC[:, t, 0:w], ALU.mult, ALU.add)
                        ins.then_inc(S("scored"), 1)
                    dve.wait_ge(S("scored"), IDX_HEADS * (t + 1))
                for r in range(N_SEL // 8):
                    for t in range(2):
                        w = (t + 1) * P
                        ins = dve.max(TOP[:, t, :], SC[:, t, 0:w])
                    dve_link(dve, ins)
                    for t in range(2):
                        w = (t + 1) * P
                        ins = dve.match_replace(SC[:, t, 0:w], TOP[:, t, :], SC[:, t, 0:w], TAKEN)
                    dve_link(dve, ins)
                    split_until(dve, chunk_of[(L + "q", r)] + AHEAD if r < 6 else chunk_of[(L + "k", r - 6)] + AHEAD)
                for n, rot in turned[5:]:
                    rotate(n, *rot)
                for t in range(2):
                    w = (t + 1) * P
                    ins = dve.tensor_scalar(MASK[:, t, 0:w], SC[:, t, 0:w], 0.5 * TAKEN, NEG, ALU.is_gt, ALU.mult)
                dve_link(dve, ins)
                for t in range(2):
                    w = (t + 1) * P
                    dve_link(dve, dve.tensor_tensor(MASK[:, t, 0:w], MASK[:, t, 0:w], causal[:, t, 0:w], ALU.add))
            else:
                for n, r in turned:
                    rotate(n, *r)
            us = attention_units(e)

            def maxes(i):
                _, _, parts, masks, _ = us[i]
                if i >= 3:
                    for b in range(0, len(us[i - 3][4]), 4):
                        wait_result(dve, (L + "pt", i - 3, b // 4))
                for m, (_, _, w) in enumerate(parts):
                    key = (L + "s", i, m * w // 512)
                    c = m * w % 512
                    if c == 0:
                        wait_result(dve, key)
                    src, dst = bank(key)[:, c:c + w], SM[:, i % 3, m * w:(m + 1) * w]
                    if masks[m] is None:
                        ins = dve.tensor_scalar(dst, src, -SCALE, None, ALU.mult)
                    else:
                        ins = dve.scalar_tensor_tensor(dst, src, -SCALE, masks[m], ALU.mult, ALU.subtract)
                    if m == len(parts) - 1 or (m + 1) * w % 512 == 0:
                        read_out(ins, key)
                        wait_read(dve, key)
                    else:
                        dve_link(dve, ins)
                dve.tensor_reduce(mz[:, i % 6, 0:1], SM[:, i % 3, 0:sum(p[2] for p in parts)], AX_X, ALU.min).then_inc(S(L + "maxes"), 1)

            def take_o(i):
                c, t, _, _, _ = us[i]
                key = (L + "o", i)
                wait_result(dve, key)
                dve.wait_ge(S(L + "exps"), i + 1)
                dve_link(dve, dve.reciprocal(mz[:, i % 6, 3:4], mz[:, i % 6, 2:3]))
                read_out(dve.tensor_scalar(Y[:, t, c:c + 64], bank(key)[:, 0:64], mz[:, i % 6, 3:4], None, ALU.mult), key)

            for i in range(len(us) + 4):
                if i < len(us):
                    maxes(i)
                if i >= 4:
                    take_o(i - 4)
            for t in range(2):
                for g in range(OUT_TILES[e] // 4):
                    n = t * (OUT_TILES[e] // 4) + g
                    wait_read(dve, (L + "ot", t, g))
                    to = (slice(None), slice(4 * g, 4 * g + 4), slice(t * P, (t + 1) * P))
                    split_value(dve, O2H[to], O2L[to], HF2[:, n % 2, :].rearrange("p (k c) -> p k c", k=4)).then_inc(S(L + "ot_parts"), 1)
            add_rows(dve, L + "y")
            norm_dve(dve, L + "n2", lambda t: X[:, t, :], [0, 1], HF2, gain2(e, 2), None, x2_ready(e, 1))
            ffn_dve(dve, L, SEQ, UT2, (UH2, UL2))
            add_rows(dve, L + "ffn")
        c = norm_cols("final")
        dve.wait_ge(S("final_gain"), 16)
        for t in range(2):
            dve.wait_ge(S("final_rstd"), t + 1)
            dve.scalar_tensor_tensor(Y[:, t, :], X[:, t, :], rstd[:, c + t:c + t + 1], FN[:, :], ALU.mult, ALU.mult).then_inc(S("final"), 1)

    @block2.sync
    def _(sp):
        load_chunks(sp, now["chunk0"])
        for t in range(2):
            sp.wait_ge(S("final"), t + 1)
            sp.dma_start(out[0, t * P:(t + 1) * P, :], Y[:, t, :]).then_inc(S("stored"), 16)
        sp.wait_ge(S("stored"), 32)

    st.close()
    ctx.close()


def kernel(**inputs):
    import numpy as _np
    import concourse.bacc as _bacc
    from concourse import mybir as _mybir
    from concourse.bass_utils import run_bass_kernel_spmd as _run

    nc = _bacc.Bacc("TRN2", target_bir_lowering=False, num_devices=1)
    arrays, args = {}, {}
    for name, a in list(inputs.items()) + list(shape_constants().items()):
        a = _np.ascontiguousarray(a)
        arrays[f"in_{name}_dram"] = a
        args[name] = nc.dram_tensor(f"in_{name}_dram", a.shape, _mybir.dt.from_np(a.dtype), kind="ExternalInput").ap()
    out = nc.dram_tensor("out_0_dram", (1, SEQ, D), F32, kind="ExternalOutput").ap()
    build(nc, args, out)
    r = _run(nc, [arrays], core_ids=[0])
    return r.results[0]["out_0_dram"]
```
